# Optimizing a Trainium2 kernel written in Bass

```python
import math
import jax, jax.numpy as jnp
from jax import lax
import numpy as np

D_MODEL = 1024
BATCH = 1
SEQ = 512
DEPTH = 2

MIX_WIDTH = D_MODEL
GM_GROUPS = 4
GM_DIM = MIX_WIDTH // 2 // GM_GROUPS
GM_W = GM_GROUPS * GM_DIM
GM_CHUNK = 128
ML_HEADS = 4
ML_DIM = MIX_WIDTH // 2 // ML_HEADS
ML_W = ML_HEADS * ML_DIM
ML_CHUNK = 128
CONV_WIDTH = 4
EV_IN = 2 * GM_W + 4 * ML_W + 2 * ML_HEADS

MLA_HEADS = 8
QK_NOPE = 128
QK_ROPE = 64
V_DIM = 128
Q_LORA = 512
KV_LORA = 256
ROPE_THETA = 10000.0
Q_BLOCK = 128
OD_IN = Q_LORA + KV_LORA + QK_ROPE

PEER_HEADS = 8
N_KEYS = 128
N_EXPERTS = N_KEYS * N_KEYS
PEER_TOPK = 16
PEER_QDIM = 256
PEER_HALF = PEER_QDIM // 2
PEER_BLOCK = 512

EPS = 1e-6

kernel_name = "hybrid_sgu_mlstm_mla_peer_trunk"

def rmsnorm(x, gain):
    xf = x.astype(jnp.float32)
    y = xf * lax.rsqrt(jnp.mean(xf * xf, axis=-1, keepdims=True) + EPS)
    return (y * gain.astype(jnp.float32)).astype(x.dtype)

def apply_rope(x, cos, sin):
    xf = x.astype(jnp.float32)
    half = QK_ROPE // 2
    x1, x2 = xf[..., :half], xf[..., half:]
    out = jnp.concatenate([x1 * cos - x2 * sin, x2 * cos + x1 * sin], axis=-1)
    return out.astype(x.dtype)

def causal_conv(z, w, b):
    S = z.shape[1]
    zp = jnp.pad(z, ((0, 0), (CONV_WIDTH - 1, 0), (0, 0)))
    out = b
    for j in range(CONV_WIDTH):
        out = out + w[j] * zp[:, j:j + S]
    return out

def chunked_spatial_gating(u, v, v_gain, ws, sb):
    B, S, _ = u.shape
    nc = S // GM_CHUNK
    vn = rmsnorm(v.reshape(B, nc, GM_CHUNK, GM_GROUPS, GM_DIM), v_gain.reshape(GM_GROUPS, GM_DIM))
    causal = jnp.tril(jnp.ones((GM_CHUNK, GM_CHUNK), dtype=bool))
    wm = jnp.where(causal[None], ws, jnp.zeros_like(ws))
    s = jnp.einsum('gts,bcsgd->bctgd', wm, vn) + sb.T[:, :, None]
    return u * s.reshape(B, S, GM_W)

def mlstm_chunkwise(q, k, v, log_i, log_f):
    B, H, S, D = q.shape
    nc = S // ML_CHUNK
    to_chunks = lambda a: jnp.moveaxis(a.reshape(B, H, nc, ML_CHUNK, *a.shape[3:]), 2, 0)
    qc, kc, vc = to_chunks(q), to_chunks(k), to_chunks(v)
    lic = to_chunks(log_i)
    bc = jnp.cumsum(to_chunks(log_f), axis=-1)
    causal = jnp.tril(jnp.ones((ML_CHUNK, ML_CHUNK), dtype=bool))
    neg_inf = jnp.float32(-jnp.inf)

    def step(carry, inp):
        C, n, m = carry
        qb, kb, vb, lib, bb = inp
        dmat = jnp.where(causal, bb[..., :, None] - bb[..., None, :] + lib[..., None, :], neg_inf)
        inter = bb + m[..., None]
        m_t = jnp.maximum(inter, jnp.max(dmat, axis=-1))
        w_intra = jnp.exp(dmat - m_t[..., None])
        w_inter = jnp.exp(inter - m_t)
        sm = jnp.einsum('bhtd,bhsd->bhts', qb, kb) * w_intra
        num = jnp.einsum('bhts,bhsd->bhtd', sm, vb) + w_inter[..., None] * jnp.einsum('bhtk,bhkv->bhtv', qb, C)
        den = jnp.sum(sm, axis=-1) + w_inter * jnp.einsum('bhtk,bhk->bht', qb, n)
        h = num / jnp.maximum(jnp.abs(den), jnp.exp(-m_t))[..., None]
        b_last = bb[..., -1]
        g = b_last[..., None] - bb + lib
        m_new = jnp.maximum(b_last + m, jnp.max(g, axis=-1))
        a = jnp.exp(b_last + m - m_new)
        w = jnp.exp(g - m_new[..., None])
        C_new = a[..., None, None] * C + jnp.einsum('bhs,bhsk,bhsv->bhkv', w, kb, vb)
        n_new = a[..., None] * n + jnp.einsum('bhs,bhsk->bhk', w, kb)
        return (C_new, n_new, m_new), h

    init = (jnp.zeros((B, H, D, D), jnp.float32), jnp.zeros((B, H, D), jnp.float32),
            jnp.zeros((B, H), jnp.float32))
    _, hs = lax.scan(step, init, (qc, kc, vc, lic, bc))
    return jnp.moveaxis(hs, 0, 2).reshape(B, H, S, D)

def sgu_mlstm_mixer(xn, w_in, gm_v_gain, gm_ws, gm_b, conv_w, conv_b, i_bias, f_bias, h_gain, w_out):
    B, S, _ = xn.shape
    proj = xn @ w_in
    o0 = 2 * GM_W
    u, vg = proj[..., :GM_W], proj[..., GM_W:o0]
    qk_pre = proj[..., o0:o0 + 2 * ML_W]
    v_m = proj[..., o0 + 2 * ML_W:o0 + 3 * ML_W]
    o_pre = proj[..., o0 + 3 * ML_W:o0 + 4 * ML_W]
    i_pre = proj[..., o0 + 4 * ML_W:o0 + 4 * ML_W + ML_HEADS]
    f_pre = proj[..., o0 + 4 * ML_W + ML_HEADS:]
    a_out = chunked_spatial_gating(jax.nn.gelu(u), jax.nn.gelu(vg), gm_v_gain, gm_ws, gm_b)
    qk = jax.nn.silu(causal_conv(qk_pre, conv_w, conv_b))
    heads = lambda t: jnp.transpose(t.reshape(B, S, ML_HEADS, ML_DIM).astype(jnp.float32), (0, 2, 1, 3))
    q = heads(qk[..., :ML_W]) * jnp.float32(ML_DIM ** -0.5)
    k = heads(qk[..., ML_W:])
    v = heads(v_m)
    log_i = jnp.transpose((i_pre + i_bias).astype(jnp.float32), (0, 2, 1))
    log_f = jnp.transpose(jax.nn.log_sigmoid((f_pre + f_bias).astype(jnp.float32)), (0, 2, 1))
    h = mlstm_chunkwise(q, k, v, log_i, log_f)
    h = rmsnorm(jnp.transpose(h, (0, 2, 1, 3)), h_gain.reshape(ML_HEADS, ML_DIM))
    b_out = jax.nn.sigmoid(o_pre) * h.reshape(B, S, ML_W).astype(xn.dtype)
    return jnp.concatenate([a_out, b_out], axis=-1) @ w_out

def mla_mixer(xn, w_in, q_gain, kv_gain, w_uq, w_ukv, w_out, cos, sin):
    B, S, _ = xn.shape
    proj = xn @ w_in
    c_q = rmsnorm(proj[..., :Q_LORA], q_gain)
    c_kv = rmsnorm(proj[..., Q_LORA:Q_LORA + KV_LORA], kv_gain)
    k_rope = apply_rope(proj[..., Q_LORA + KV_LORA:], cos, sin)
    q = (c_q @ w_uq).reshape(B, S, MLA_HEADS, QK_NOPE + QK_ROPE)
    q_nope = q[..., :QK_NOPE]
    q_rope = apply_rope(q[..., QK_NOPE:], cos[:, None, :], sin[:, None, :])
    kv = (c_kv @ w_ukv).reshape(B, S, MLA_HEADS, QK_NOPE + V_DIM)
    k_nope, v = kv[..., :QK_NOPE], kv[..., QK_NOPE:]
    nb = S // Q_BLOCK
    blocks = lambda t: jnp.moveaxis(t.reshape(B, nb, Q_BLOCK, *t.shape[2:]), 1, 0)
    scale = jnp.float32((QK_NOPE + QK_ROPE) ** -0.5)
    key_pos = jnp.arange(S)

    def attend(args):
        qn, qr, i = args
        s = jnp.einsum('bqhd,bkhd->bhqk', qn, k_nope) + jnp.einsum('bqhr,bkr->bhqk', qr, k_rope)
        q_pos = i * Q_BLOCK + jnp.arange(Q_BLOCK)
        s = jnp.where(key_pos[None, :] <= q_pos[:, None], s.astype(jnp.float32) * scale, -jnp.inf)
        p = jax.nn.softmax(s, axis=-1).astype(v.dtype)
        return jnp.einsum('bhqk,bkhd->bqhd', p, v)

    o = lax.map(attend, (blocks(q_nope), blocks(q_rope), jnp.arange(nb)))
    o = jnp.moveaxis(o, 0, 1).reshape(B, S, MLA_HEADS * V_DIM)
    return o @ w_out

def peer_ffn(xn, w_q, sub_keys, u_tab, v_tab):
    B, S, D = xn.shape
    n_tok = B * S
    blk = math.gcd(n_tok, PEER_BLOCK)
    xs = xn.reshape(n_tok // blk, blk, D)

    def retrieve(xb):
        q = (xb @ w_q).reshape(blk, PEER_HEADS, 2, PEER_HALF)
        s = jnp.einsum('thpd,hpnd->thpn', q, sub_keys).astype(jnp.float32)
        sv, si = lax.top_k(s, PEER_TOPK)
        cand_s = (sv[:, :, 0, :, None] + sv[:, :, 1, None, :]).reshape(blk, PEER_HEADS, PEER_TOPK * PEER_TOPK)
        cand_i = (si[:, :, 0, :, None] * N_KEYS + si[:, :, 1, None, :]).reshape(blk, PEER_HEADS, PEER_TOPK * PEER_TOPK)
        top_s, top_p = lax.top_k(cand_s, PEER_TOPK)
        e_idx = jnp.take_along_axis(cand_i, top_p, axis=-1)
        gate = jax.nn.softmax(top_s, axis=-1)
        ug = u_tab[e_idx]
        vg = v_tab[e_idx]
        act = jax.nn.gelu(jnp.einsum('thkd,td->thk', ug, xb).astype(jnp.float32))
        return jnp.einsum('thk,thkd->td', (gate * act).astype(xb.dtype), vg)

    return lax.map(retrieve, xs).reshape(B, S, D)

def setup_inputs(seed: int = 0) -> dict:
    key = jax.random.key(seed)
    ks = jax.random.split(key, 28)
    ne = (DEPTH + 1) // 2
    no = DEPTH // 2
    nrm = lambda k, shape, scale: jax.random.normal(k, shape, jnp.float32) * scale
    gain = lambda k, shape: 1.0 + 0.01 * jax.random.normal(k, shape, jnp.float32)
    return {
        "x": jax.random.normal(ks[0], (BATCH, SEQ, D_MODEL), jnp.float32),
        "norm_mix": gain(ks[1], (DEPTH, D_MODEL)),
        "norm_ffn": gain(ks[2], (DEPTH, D_MODEL)),
        "norm_final": gain(ks[3], (D_MODEL,)),
        "ev_w_in": nrm(ks[4], (ne, D_MODEL, EV_IN), D_MODEL ** -0.5),
        "ev_gm_v_gain": gain(ks[5], (ne, GM_W)),
        "ev_gm_ws": nrm(ks[6], (ne, GM_GROUPS, GM_CHUNK, GM_CHUNK), GM_CHUNK ** -0.5),
        "ev_gm_b": gain(ks[7], (ne, GM_GROUPS, GM_CHUNK)),
        "ev_conv_w": nrm(ks[8], (ne, CONV_WIDTH, 2 * ML_W), CONV_WIDTH ** -0.5),
        "ev_conv_b": nrm(ks[9], (ne, 2 * ML_W), 0.01),
        "ev_i_bias": nrm(ks[10], (ne, ML_HEADS), 0.01),
        "ev_f_bias": 3.0 + 0.5 * jax.random.normal(ks[11], (ne, ML_HEADS), jnp.float32),
        "ev_h_gain": gain(ks[12], (ne, ML_W)),
        "ev_w_out": nrm(ks[13], (ne, MIX_WIDTH, D_MODEL), MIX_WIDTH ** -0.5),
        "od_w_in": nrm(ks[14], (no, D_MODEL, OD_IN), D_MODEL ** -0.5),
        "od_q_gain": gain(ks[15], (no, Q_LORA)),
        "od_kv_gain": gain(ks[16], (no, KV_LORA)),
        "od_w_uq": nrm(ks[17], (no, Q_LORA, MLA_HEADS * (QK_NOPE + QK_ROPE)), Q_LORA ** -0.5),
        "od_w_ukv": nrm(ks[18], (no, KV_LORA, MLA_HEADS * (QK_NOPE + V_DIM)), KV_LORA ** -0.5),
        "od_w_out": nrm(ks[19], (no, MLA_HEADS * V_DIM, D_MODEL), (MLA_HEADS * V_DIM) ** -0.5),
        "peer_w_q": nrm(ks[20], (DEPTH, D_MODEL, PEER_HEADS * PEER_QDIM), D_MODEL ** -0.5),
        "peer_keys": nrm(ks[21], (DEPTH, PEER_HEADS, 2, N_KEYS, PEER_HALF), PEER_HALF ** -0.5),
        "peer_u": nrm(ks[22], (DEPTH, N_EXPERTS, D_MODEL), D_MODEL ** -0.5),
        "peer_v": nrm(ks[23], (DEPTH, N_EXPERTS, D_MODEL), (PEER_HEADS * PEER_TOPK) ** -0.5),
    }

def reference(x, norm_mix, norm_ffn, norm_final, ev_w_in, ev_gm_v_gain, ev_gm_ws, ev_gm_b,
              ev_conv_w, ev_conv_b, ev_i_bias, ev_f_bias, ev_h_gain, ev_w_out,
              od_w_in, od_q_gain, od_kv_gain, od_w_uq, od_w_ukv, od_w_out,
              peer_w_q, peer_keys, peer_u, peer_v):
    S = x.shape[1]
    pos = jnp.arange(S, dtype=jnp.float32)
    inv_freq = ROPE_THETA ** (-jnp.arange(QK_ROPE // 2, dtype=jnp.float32) / (QK_ROPE // 2))
    ang = pos[:, None] * inv_freq[None, :]
    cos, sin = jnp.cos(ang), jnp.sin(ang)
    for layer in range(DEPTH):
        j = layer // 2
        xn = rmsnorm(x, norm_mix[layer])
        if layer % 2 == 0:
            x = x + sgu_mlstm_mixer(xn, ev_w_in[j], ev_gm_v_gain[j], ev_gm_ws[j], ev_gm_b[j],
                                    ev_conv_w[j], ev_conv_b[j], ev_i_bias[j], ev_f_bias[j],
                                    ev_h_gain[j], ev_w_out[j])
        else:
            x = x + mla_mixer(xn, od_w_in[j], od_q_gain[j], od_kv_gain[j], od_w_uq[j],
                              od_w_ukv[j], od_w_out[j], cos, sin)
        x = x + peer_ffn(rmsnorm(x, norm_ffn[layer]), peer_w_q[layer], peer_keys[layer],
                         peer_u[layer], peer_v[layer])
    return rmsnorm(x, norm_final)


_drawn_inputs = setup_inputs


def setup_inputs(seed=0):
    import zlib

    import numpy as np

    out = dict(_drawn_inputs(seed))
    spreads = {}
    factors = {'norm_mix': 5.636,
     'norm_ffn': 64.0,
     'norm_final': 35.824,
     'ev_gm_v_gain': 27.556,
     'ev_gm_b': 21.531,
     'ev_conv_b': 64.0,
     'ev_i_bias': 64.0,
     'ev_h_gain': 64.0,
     'od_q_gain': 27.772,
     'od_kv_gain': 30.058}
    for name, (base, spread) in spreads.items():
        noise = np.random.default_rng([zlib.crc32(name.encode()), seed]).standard_normal(out[name].shape)
        drawn = base * np.exp(spread * noise) if base else spread * noise
        out[name] = __import__('jax').numpy.asarray(drawn.astype(out[name].dtype))
    for name, factor in factors.items():
        out[name] = (out[name] * factor).astype(out[name].dtype)
    return out
```

```python
from contextlib import ExitStack

import concourse.bass as bass
from concourse import mybir
import numpy as np

F32 = mybir.dt.float32
F32R = mybir.dt.float32r
BF16 = mybir.dt.bfloat16
U32 = mybir.dt.uint32
I32 = mybir.dt.int32
ALU = mybir.AluOpType
ACT = mybir.ActivationFunctionType
AX = mybir.AxisListType

P = 128
D = 1024
KT = D // P
T = 512
TT = T // P
EPS = 1e-6

G_N, G_D = 4, 128
H_E, D_E = 4, 128
MIX = G_N * G_D
CONV = 4

H_A, NOPE, ROPE, V_D = 8, 128, 64, 128
Q_LORA, KV_LORA = 512, 256
A_SCALE = float(np.float32((NOPE + ROPE) ** -0.5))

H_P, KEYS, TOPK, QD = 8, 128, 16, 256
PAIRS = H_P * TOPK
NEG = -3.0e38
STAIRS = [(0, 1, 16), (1, 1, 8), (2, 1, 5), (3, 1, 4), (4, 1, 3), (5, 3, 2), (8, 8, 1)]
CAND = sum(n * w for _, n, w in STAIRS)

GROUP = 4
N_GROUPS = KEYS // GROUP
BLOCKS = TT * 2


class Chain:

    def __init__(self, eng, sem, base=0):
        self.eng, self.sem, self.base, self.n = eng, sem, base, 0

    def mark(self, ins):
        self.n += 1
        ins.then_inc(self.sem, 1)

    def then(self, ins):
        self.mark(ins)
        self.eng.wait_ge(self.sem, self.base + self.n)

    def then_pass(self, ins, passed):
        self.then(ins)
        self.eng.sem_inc(passed, 1)


def split_product(pe, out, a, b, first, last):
    pe.matmul(out, a[0], b[0], start=first, stop=False)
    pe.matmul(out, a[0], b[1], start=False, stop=False)
    return pe.matmul(out, a[1], b[0], start=False, stop=last)


def as_f32(ap):
    return ap.bitcast(F32)


class Stage:

    def __init__(self, nc, name):
        self.nc, self.name, self.ctx = nc, name, ExitStack()

    def __enter__(self):
        self.ctx.__enter__()
        return self

    def __exit__(self, *a):
        return self.ctx.__exit__(*a)

    def sb(self, name, shape, dt=F32):
        return self.ctx.enter_context(self.nc.sbuf_tensor(f"{self.name}_{name}", shape, dt))

    def sb_split(self, name, shape):
        at = (self.nc.sbuf_base + 31) // 32 * 32
        return self.sb(name, shape), self.nc.alloc_sbuf_tensor_at(f"{self.name}_{name}_rest", shape, F32R, offset=at)

    def banks(self, n):
        return [self.ctx.enter_context(self.nc.psum_tensor(f"{self.name}_bank{i}", [P, 512], F32)) for i in range(n)]

    def sem(self, name):
        s = self.nc.alloc_semaphore(f"{self.name}_{name}")
        SEMAPHORES.append(s)
        return s


SEMAPHORES = []


def clear_semaphores(nc):
    with nc.Block() as block:
        @block.sync
        def _(sp):
            for s in SEMAPHORES:
                sp.sem_clear(s)
    for s in SEMAPHORES:
        nc.release_semaphore(s)
    SEMAPHORES.clear()


def constants(nc, K, ins):
    with Stage(nc, "const") as st:
        loaded, made = st.sem("loaded"), st.sem("made")
        with nc.Block() as block:
            @block.sync
            def _(sp):
                sp.dma_start(K["X"][:], ins["x"].rearrange("a (c p) d -> p (a c) d", p=P)).then_inc(loaded, 16)
                sp.wait_ge(loaded, 16)

            @block.gpsimd
            def _(pool):
                pool.memset(K["ident"][:], 0.0)
                pool.memset(K["sel"][:], 0.0)
                pool.memset(K["eps"][:], EPS)
                pool.memset(K["one"][:], 1.0)
                pool.iota(K["iota_i"][:], [[1, KEYS]], base=0, channel_multiplier=0).then_inc(made, 1)
                pool.wait_ge(made, 1)
                pool.tensor_copy(K["iota"][:], K["iota_i"][:])
                pool.affine_select(out=K["ident"][:], in_=K["ident"][:], compare_op=ALU.not_equal, fill=1.0,
                                   base=0, pattern=[[-1, P]], channel_multiplier=1)
                pool.affine_select(out=K["sel"][:], in_=K["sel"][:], compare_op=ALU.not_equal, fill=1.0,
                                   base=0, pattern=[[-1, H_E], [0, P]], channel_multiplier=1).then_inc(made, 1)
                pool.wait_ge(made, 2)


def norm_transpose(nc, K, name, gain, xT=None, split=None, ahead=None):
    X, ident = K["X"], K["ident"]
    HALF = TT // 2
    with Stage(nc, name) as st:
        sq = st.sb("sq", [P, 2, D])
        sq_dve = st.sb("sq_dve", [P, 2, D])
        xs = st.sb("xs", [P, TT, D])
        gcol = st.sb("gcol", [P, KT])
        ss, root, y, t1 = (st.sb(n, [P, TT]) for n in ("ss", "root", "y", "t1"))
        bank = st.banks(8)
        gain_in, squared, summed, rooted, step, scaled, scaled_act = (
            st.sem(n) for n in ("gain_in", "squared", "summed", "rooted", "step", "scaled", "scaled_act"))
        turned, high = st.sem("turned"), st.sem("high")
        with nc.Block() as block:
            @block.sync
            def _(sp):
                sp.dma_start(gcol[:], gain).then_inc(gain_in, 16)
                if ahead:
                    ahead(sp)

            @block.scalar
            def _(act):
                for c in range(HALF):
                    act.activation(sq[:, c], X[:, c], ACT.Square, accum_out=ss[:, c:c + 1]).then_inc(squared, 1)
                act.wait_ge(squared, HALF)
                act.wait_ge(summed, HALF)
                act.activation(root[:], ss[:], ACT.Sqrt, scale=1.0 / D, bias=K["eps"][:, 0:1]).then_inc(rooted, 1)
                act.wait_ge(step, 6)
                for c in range(HALF, TT):
                    act.activation(xs[:, c], X[:, c], ACT.Copy, scale=y[:, c:c + 1]).then_inc(scaled_act, 1)
                act.wait_ge(gain_in, 16)
                for k in range(KT):
                    if not split and k % 2:
                        continue
                    act.wait_ge(turned, k + 1)
                    act.activation(split[0][:, k] if split else xT[:, k], bank[k][:], ACT.Copy, scale=gcol[:, k:k + 1]).then_inc(high, 1)

            @block.vector
            def _(dve):
                for c in range(HALF, TT):
                    dve.tensor_tensor_reduce(sq_dve[:, c - HALF], X[:, c], X[:, c], 1.0, 0.0, ALU.mult, ALU.add,
                                             ss[:, c:c + 1]).then_inc(summed, 1)
                own = Chain(dve, step)
                dve.wait_ge(squared, HALF)
                rsqrt_newton(dve, own, rooted, 1, ss, root, y, t1, D)
                for c in range(HALF):
                    dve.tensor_scalar(xs[:, c], X[:, c], y[:, c:c + 1], None, ALU.mult).then_inc(scaled, 1)
                dve.wait_ge(gain_in, 16)
                for k in range(KT):
                    if split:
                        dve.wait_ge(high, k + 1)
                        dve.scalar_tensor_tensor(out=split[1][:, k], in0=bank[k][:], scalar=gcol[:, k:k + 1],
                                                 in1=split[0][:, k].bitcast(F32), op0=ALU.mult, op1=ALU.subtract)
                    elif k % 2:
                        dve.wait_ge(turned, k + 1)
                        dve.tensor_scalar(xT[:, k], bank[k][:], gcol[:, k:k + 1], None, ALU.mult)

            @block.tensor
            def _(pe):
                pe.wait_ge(scaled, HALF)
                pe.wait_ge(scaled_act, TT - HALF)
                for k in range(KT):
                    for c in range(TT):
                        last = pe.transpose(bank[k][:, c * P:(c + 1) * P], xs[:, c, k * P:(k + 1) * P], ident[:])
                    last.then_inc(turned, 1)


def final_norm(nc, K, gain, out):
    X = K["X"]
    with Stage(nc, "fin") as st:
        sq = st.sb("sq", [P, 2, D])
        xs = st.sb("xs", [P, TT, D])
        grow = st.sb("grow", [P, D])
        ss, root, y, t1 = (st.sb(n, [P, TT]) for n in ("ss", "root", "y", "t1"))
        gain_in, squared, rooted, step, stored = (st.sem(n) for n in ("gain_in", "squared", "rooted", "step", "stored"))
        with nc.Block() as block:
            @block.scalar
            def _(act):
                for c in range(TT):
                    if c >= 2:
                        act.wait_ge(squared, c - 1)
                    act.activation(sq[:, c % 2], X[:, c], ACT.Square, accum_out=ss[:, c:c + 1]).then_inc(squared, 1)
                act.wait_ge(squared, TT)
                act.activation(root[:], ss[:], ACT.Sqrt, scale=1.0 / D, bias=K["eps"][:, 0:1]).then_inc(rooted, 1)

            @block.vector
            def _(dve):
                own = Chain(dve, step)
                dve.wait_ge(rooted, 1)
                own.then(dve.reciprocal(y[:], root[:]))
                own.then(dve.tensor_scalar(ss[:], ss[:], 1.0 / D, EPS, ALU.mult, ALU.add))
                own.then(dve.tensor_tensor(t1[:], y[:], y[:], ALU.mult))
                own.then(dve.tensor_tensor(t1[:], t1[:], ss[:], ALU.mult))
                own.then(dve.tensor_scalar(t1[:], t1[:], -0.5, 1.5, ALU.mult, ALU.add))
                own.then(dve.tensor_tensor(y[:], y[:], t1[:], ALU.mult))
                dve.wait_ge(gain_in, 16)
                for c in range(TT):
                    own.mark(dve.scalar_tensor_tensor(out=xs[:, c], in0=X[:, c], scalar=y[:, c:c + 1], in1=grow[:],
                                                      op0=ALU.mult, op1=ALU.mult))

            @block.sync
            def _(sp):
                sp.dma_start(grow[:], gain.to_broadcast([P, D])).then_inc(gain_in, 16)
                for c in range(TT):
                    sp.wait_ge(step, 7 + c)
                    sp.dma_start(out[0, c * P:(c + 1) * P, :], xs[:, c]).then_inc(stored, 16)
                sp.wait_ge(stored, 16 * TT)


class OutputWeights:

    def __init__(self, nc, st, name, src, top):
        self.src = src
        self.bottom = top - 2 * KT * D * 4
        size = KT * D * 4
        self.raw, rest, high = (nc.alloc_sbuf_tensor_at(f"{name}_w_out_{n}", [P, KT, D], dt, offset=top - off)
                                for n, dt, off in (("raw", F32, size), ("rest", F32R, size), ("high", F32R, 2 * size)))
        self.split = (high, rest)
        self.loaded = [st.sem(f"w_out_in{n}") for n in range(2)]
        self.copied = st.sem("w_out_high")

    def load(self, sp):
        half = KT // 2
        for n in range(2):
            ks = slice(n * half, (n + 1) * half)
            sp.dma_start(self.raw[:, ks], self.src[:, ks]).then_inc(self.loaded[n], 16)

    def copy_high(self, act, k):
        act.wait_ge(self.loaded[k // (KT // 2)], 16)
        act.activation(self.split[0][:, k], self.raw[:, k], ACT.Copy).then_inc(self.copied, 1)

    def take_rest(self, pool, k):
        pool.wait_ge(self.copied, k + 1)
        high, rest = self.split
        pool.tensor_tensor(rest[:, k], self.raw[:, k], as_f32(high[:, k]), ALU.subtract)


def project_out(nc, K, name, w, cat=None, split=None):
    X, ident = K["X"], K["ident"]
    wh, wl = w
    turn = cat is not None
    with Stage(nc, name) as st:
        ch, cl = split or (st.sb("ch", [P, KT, T], F32R), st.sb("cl", [P, KT, T], F32R))
        bank = st.banks(8)
        turned, c_high, c_rest, made = (st.sem(n) for n in ("turned", "c_high", "c_rest", "made"))

        with nc.Block() as block:
            @block.tensor
            def _(pe):
                if turn:
                    for k in range(KT):
                        for c in range(TT):
                            last = pe.transpose(bank[k][:, c * P:(c + 1) * P], cat[:, c, k * P:(k + 1) * P], ident[:])
                        last.then_inc(turned, 1)
                for b in range(BLOCKS):
                    tok, col = slice(b // 2 * P, (b // 2 + 1) * P), slice(b % 2 * 512, (b % 2 + 1) * 512)
                    for k in range(KT):
                        if turn and b == 0:
                            pe.wait_ge(c_rest, k + 1)
                        last = split_product(pe, bank[b][:], (ch[:, k, tok], cl[:, k, tok]), (wh[:, k, col], wl[:, k, col]),
                                             k == 0, k == KT - 1)
                    last.then_inc(made, 1)

            @block.scalar
            def _(act):
                if turn:
                    for k in range(KT):
                        act.wait_ge(turned, k + 1)
                        act.activation(ch[:, k], bank[k][:], ACT.Copy).then_inc(c_high, 1)

            @block.vector
            def _(dve):
                if turn:
                    for k in range(KT):
                        dve.wait_ge(c_high, k + 1)
                        dve.tensor_tensor(cl[:, k], bank[k][:], as_f32(ch[:, k]), ALU.subtract).then_inc(c_rest, 1)
                for b in range(BLOCKS):
                    xb = X[:, b // 2, b % 2 * 512:(b % 2 + 1) * 512]
                    dve.wait_ge(made, b + 1)
                    dve.tensor_tensor(xb, xb, bank[b][:], ALU.add)



def load_head(sp, buf, ins, h):
    sp.dma_start(buf["wq"][:, h % 2], ins["wq"][h]).then_inc(buf["w_in"][h % 2], 16)
    sp.dma_start(buf["keys"][:, h % 2], ins["keys"][h]).then_inc(buf["k_in"][h % 2], 16)


def peer_retrieve(nc, K, name, buf, ins, xT, split, pair_i, pair_j, pair_g, limit):
    ident = K["ident"]
    M = 2 * TT
    wq, keys, w_in, k_in = buf["wq"], buf["keys"], buf["w_in"], buf["k_in"]
    BIG = [P, TT, TOPK, CAND]
    with Stage(nc, name) as st:
        qT = st.sb("qT", [P, 2, 2, T])
        S = st.sb("S", [P, 2, M, KEYS])
        S2 = st.sb("S2", [P, M, KEYS])
        top = st.sb("top", [P, M, TOPK])
        top_u = st.sb("top_u", [P, M, TOPK], U32)
        top_n = st.sb("top_n", [P, 2, M, TOPK])
        cand = st.sb("cand", [P, TT, CAND])
        cand2 = st.sb("cand2", [P, TT, CAND])
        code = st.sb("code", [P, 2, TT, CAND])
        best = st.sb("best", [P, TT, TOPK])
        at_u = st.sb("at_u", [P, TT, TOPK], U32)
        at = st.sb("at", [P, 2, TT, TOPK])
        apart = st.sb("apart", [P, 2, TT, TOPK, CAND], BF16)
        picked = st.sb("picked", [P, 2, TT, TOPK, CAND])
        place = st.sb("place", [P, CAND])
        place_i = st.sb("place_i", [P, CAND], I32)
        val = st.sb("val", [P, TT, H_P, TOPK])
        cod = st.sb("cod", [P, TT, H_P, TOPK])
        big = st.sb("big", [P, TT, H_P, TOPK])
        num = st.sb("num", [P, TT, H_P])
        ci = st.sb("ci", [P, TT, PAIRS], I32)
        cj = st.sb("cj", [P, TT, PAIRS], I32)
        assert nc.sbuf_base <= limit, "the pair tables would be overwritten"
        bank = st.banks(8)
        q_made, q_out, s_made, s_out = (st.sem(n) for n in ("q_made", "q_out", "s_made", "s_out"))
        q_free, s_free, ranked = (st.sem(n) for n in ("q_free", "s_free", "ranked"))
        step, passed, placed, expd, ready, turned, spread = (st.sem(n) for n in ("step", "passed", "placed", "expd", "ready", "turned", "spread"))
        high, numbered, located, coded, parted, absed, marked, chosen = (
            st.sem(n) for n in ("high", "numbered", "located", "coded", "parted", "absed", "marked", "chosen"))

        def wide_place():
            return place[:].unsqueeze(1).unsqueeze(1).to_broadcast(BIG)

        def wide_at(u):
            return at[:, u].unsqueeze(3).to_broadcast(BIG)

        def wide_code(u):
            return code[:, u].unsqueeze(2).to_broadcast(BIG)

        def stairs(eng, dst, src):
            o = 0
            for a, rows, w in STAIRS:
                last = eng.tensor_tensor(
                    dst[:, :, o:o + rows * w].rearrange("p c (a b) -> p c a b", a=rows),
                    src[:, 0:TT, a:a + rows].unsqueeze(3).to_broadcast([P, TT, rows, w]),
                    src[:, TT:M, 0:w].unsqueeze(2).to_broadcast([P, TT, rows, w]), ALU.add)
                o += rows * w
            return last

        with nc.Block() as block:
            @block.sync
            def _(sp):
                with sp.Fori(1, H_P // 2) as i:
                    for u in range(2):
                        h = sp.snap(i * 2 + u)
                        sp.wait_ge(q_made, i * 2 + (u - 1))
                        sp.dma_start(wq[:, u], ins["wq"][bass.ds(h, 1)].rearrange("a p k q -> p (a k) q")).then_inc(w_in[u], 16)
                        sp.wait_ge(s_made, i * 2 + (u - 1))
                        sp.dma_start(keys[:, u], ins["keys"][bass.ds(h, 1)].rearrange("a p s n -> p (a s) n")).then_inc(k_in[u], 16)

            @block.gpsimd
            def _(pool):
                pool.iota(place_i[:], [[1, CAND]], base=0, channel_multiplier=0).then_inc(placed, 1)
                pool.wait_ge(placed, 1)
                pool.tensor_copy(place[:], place_i[:]).then_inc(placed, 1)
                pool.wait_ge(placed, 2)

                def number(u, h):
                    pool.wait_ge(numbered, h + 1)
                    if not isinstance(h, int) or h >= 2:
                        pool.wait_ge(chosen, h - 1)
                    stairs(pool, code[:, u], top_n[:, u]).then_inc(coded, 1)

                def part(u, h):
                    pool.wait_ge(located, h + 1)
                    pool.tensor_tensor(apart[:, u], wide_place(), wide_at(u), ALU.subtract).then_inc(parted, 1)

                def choose(u, h):
                    pool.wait_ge(marked, h + 1)
                    pool.wait_ge(coded, h + 1)
                    pool.tensor_tensor(picked[:, u], apart[:, u], wide_code(u), ALU.mult).then_inc(chosen, 1)

                number(0, 0)
                part(0, 0)
                number(1, 1)
                part(1, 1)
                choose(0, 0)
                with pool.Fori(1, H_P // 2 - 1) as i:
                    for u in range(2):
                        number(u, i * 2 + u)
                        part(u, i * 2 + u)
                        choose(1 - u, i * 2 + (u - 1))
                number(0, H_P - 2)
                part(0, H_P - 2)
                choose(1, H_P - 3)
                number(1, H_P - 1)
                choose(0, H_P - 2)

            @block.tensor
            def _(pe):
                def query(u, h):
                    pe.wait_ge(w_in[u], h * 8 + (16 - 8 * u))
                    pe.wait_ge(q_free, h + 1)
                    for s in range(2):
                        for k in range(KT):
                            last = pe.matmul(bank[2 * u + s][:], wq[:, u, k, s * P:(s + 1) * P], xT[:, k],
                                             start=(k == 0), stop=(k == KT - 1))
                    last.then_inc(q_made, 1)

                def scores(u, h):
                    pe.wait_ge(k_in[u], h * 8 + (16 - 8 * u))
                    pe.wait_ge(q_out, h + 1)
                    pe.wait_ge(s_free, h + 1)
                    for s in range(2):
                        for c in range(TT):
                            last = pe.matmul(bank[4 + 2 * u + s][:, c * P:(c + 1) * P],
                                             qT[:, u, s, c * P:(c + 1) * P], keys[:, u, s], start=True, stop=True)
                    last.then_inc(s_made, 1)

                with pe.Fori(0, H_P // 2) as i:
                    for u in range(2):
                        query(u, i * 2 + u)
                        scores(u, i * 2 + u)
                for n, src in enumerate((K["tab_i"], K["tab_j"], K["tab_g"])):
                    pe.wait_ge(ready, n + 1)
                    for c in range(TT):
                        last = pe.transpose(bank[n][:, c * P:(c + 1) * P], src[:, c], ident[:])
                    last.then_inc(turned, 1)

            @block.scalar
            def _(act):
                act.sem_inc(q_free, 2)
                act.sem_inc(s_free, 2)

                def query(u, h):
                    act.wait_ge(q_made, h + 1)
                    act.activation(qT[:, u, 0], bank[2 * u][:], ACT.Copy)
                    act.activation(qT[:, u, 1], bank[2 * u + 1][:], ACT.Copy).then_inc(q_out, 1)
                    act.wait_ge(q_out, h + 1)
                    act.sem_inc(q_free, 1)

                def scores(u, h):
                    act.wait_ge(s_made, h + 1)
                    act.wait_ge(ranked, h + 1)
                    act.activation(S[:, u, 0:TT], bank[4 + 2 * u][:].rearrange("p (c n) -> p c n", c=TT), ACT.Copy)
                    act.activation(S[:, u, TT:M], bank[5 + 2 * u][:].rearrange("p (c n) -> p c n", c=TT),
                                   ACT.Copy).then_inc(s_out, 1)
                    act.wait_ge(s_out, h + 1)
                    act.sem_inc(s_free, 1)

                def mark(u, h):
                    act.wait_ge(parted, h + 1)
                    act.activation(apart[:, u], apart[:, u], ACT.Abs).then_inc(absed, 1)
                    act.wait_ge(absed, h + 1)
                    act.activation(apart[:, u], apart[:, u], ACT.Relu, scale=-1.0, bias=K["one"][:, 0:1]).then_inc(marked, 1)

                for k in range(KT):
                    act.activation(split[0][:, k], xT[:, k], ACT.Copy).then_inc(high, 1)
                query(0, 0)
                scores(0, 0)
                query(1, 1)
                scores(1, 1)
                with act.Fori(0, H_P // 2 - 1) as i:
                    for u in range(2):
                        query(u, i * 2 + (u + 2))
                        scores(u, i * 2 + (u + 2))
                        mark(u, i * 2 + u)
                mark(0, H_P - 2)
                act.wait_ge(expd, 1)
                act.activation(big[:], big[:], ACT.Exp).then_inc(expd, 1)
                for n, dst in enumerate((pair_i, pair_j, pair_g)):
                    act.wait_ge(turned, n + 1)
                    act.activation(dst[:], bank[n][:], ACT.Copy).then_inc(spread, 1)

            @block.vector
            def _(dve):
                STEPS = 10
                dve.sem_inc(ranked, 2)
                for k in range(KT):
                    dve.wait_ge(high, k + 1)
                    dve.tensor_tensor(split[1][:, k], xT[:, k], split[0][:, k].bitcast(F32), ALU.subtract)
                dve.wait_ge(placed, 2)

                def rank(u, h):
                    own = Chain(dve, step, h * STEPS)
                    dve.wait_ge(s_out, h + 1)
                    dve.sem_inc(passed, 1)
                    for m in range(M):
                        last = dve.max(top[:, m, 0:8], S[:, u, m])
                    own.then_pass(last, passed)
                    for m in range(M):
                        dve.match_replace(S2[:, m], top[:, m, 0:8], S[:, u, m], NEG)
                        last = dve.max_index(top_u[:, m, 0:8], top[:, m, 0:8], S[:, u, m])
                    own.then_pass(last, passed)
                    for m in range(M):
                        last = dve.max(top[:, m, 8:16], S2[:, m])
                    own.then_pass(last, passed)
                    for m in range(M):
                        last = dve.max_index(top_u[:, m, 8:16], top[:, m, 8:16], S2[:, m])
                    own.then(last)
                    dve.sem_inc(ranked, 1)
                    if not isinstance(h, int) or h >= 2:
                        dve.wait_ge(coded, h - 1)
                    dve.tensor_scalar(top_n[:, u, 0:TT], top_u[:, 0:TT], float(KEYS), None, ALU.mult)
                    dve.tensor_copy(top_n[:, u, TT:M], top_u[:, TT:M]).then_inc(numbered, 1)
                    own.then_pass(stairs(dve, cand, top), passed)
                    for c in range(TT):
                        last = dve.max(best[:, c, 0:8], cand[:, c])
                    own.then_pass(last, passed)
                    for c in range(TT):
                        dve.match_replace(cand2[:, c], best[:, c, 0:8], cand[:, c], NEG)
                        last = dve.max_index(at_u[:, c, 0:8], best[:, c, 0:8], cand[:, c])
                    own.then_pass(last, passed)
                    for c in range(TT):
                        last = dve.max(best[:, c, 8:16], cand2[:, c])
                    own.then_pass(last, passed)
                    for c in range(TT):
                        last = dve.max_index(at_u[:, c, 8:16], best[:, c, 8:16], cand2[:, c])
                    own.then(last)
                    if not isinstance(h, int) or h >= 2:
                        dve.wait_ge(parted, h - 1)
                    dve.tensor_copy(at[:, u], at_u[:]).then_inc(located, 1)
                    own.then(dve.tensor_copy(val[:, :, bass.ds(h, 1)].rearrange("p c a k -> p c (a k)"), best[:]))
                    assert own.n == STEPS, own.n

                def gather(u, h):
                    dve.wait_ge(chosen, h + 1)
                    dve.tensor_reduce(cod[:, :, bass.ds(h, 1)].rearrange("p c a k -> p c (a k)"), picked[:, u], AX.X, ALU.add)

                rank(0, 0)
                rank(1, 1)
                with dve.Fori(0, H_P // 2 - 1) as i:
                    for u in range(2):
                        rank(u, i * 2 + (u + 2))
                        gather(u, i * 2 + u)
                own = Chain(dve, step, H_P * STEPS)
                own.then(dve.tensor_tensor(big[:], val[:], val[:, :, :, 0:1].to_broadcast([P, TT, H_P, TOPK]), ALU.subtract))
                dve.sem_inc(expd, 1)
                own.then(dve.tensor_tensor(picked[:, 1], wide_place(), wide_at(1), ALU.is_equal))
                dve.wait_ge(coded, H_P)
                own.then(dve.tensor_tensor(picked[:, 1], picked[:, 1], wide_code(1), ALU.mult))
                dve.tensor_reduce(cod[:, :, H_P - 1], picked[:, 1], AX.X, ALU.add)
                dve.wait_ge(chosen, H_P - 1)
                own.then(dve.tensor_reduce(cod[:, :, H_P - 2], picked[:, 0], AX.X, ALU.add))
                codf = cod[:].rearrange("p c h k -> p c (h k)")
                own.then(dve.tensor_copy(ci[:], codf))
                own.then(dve.tensor_scalar(cj[:], ci[:], 7, None, ALU.arith_shift_right))
                own.then(dve.tensor_copy(K["tab_i"][:], cj[:]))
                dve.sem_inc(ready, 1)
                own.then(dve.scalar_tensor_tensor(out=K["tab_j"][:], in0=K["tab_i"][:], scalar=-float(KEYS), in1=codf,
                                                  op0=ALU.mult, op1=ALU.add))
                dve.sem_inc(ready, 1)
                dve.wait_ge(expd, 2)
                own.then(dve.tensor_reduce(num[:], big[:], AX.X, ALU.add))
                own.then(dve.reciprocal(num[:], num[:]))
                own.then(dve.tensor_tensor(K["tab_g"][:].rearrange("p c (h k) -> p c h k", h=H_P), big[:],
                                           num[:].unsqueeze(3).to_broadcast([P, TT, H_P, TOPK]), ALU.mult))
                dve.sem_inc(ready, 1)


def peer_mix(nc, K, name, u_dram, v_dram, g_dram, xh, xl, arena, pair_i, pair_j, pair_g):
    X = K["X"]
    BT = 8
    NB = P // BT
    HALVES = NB // 2
    iota = K["iota"]
    KB = 1024
    with Stage(nc, name) as st:
        st.sb("arena", [P, 152 * KB // 4])

        def at(n, shape, kb, dt=F32):
            return nc.alloc_sbuf_tensor_at(f"{name}_{n}", shape, dt, offset=arena + kb * KB)

        G = [at(f"G{b}", [P, KEYS, P], 64 * b) for b in range(2)]
        hot_i, hot_j = at("hot_i", [P, 2, BT, KEYS], 128), at("hot_j", [P, 2, BT, KEYS], 136)
        u_raw, v_raw = at("u_raw", [P, GROUP, D], 0), at("v_raw", [P, GROUP, D], 16)
        uh, ul = at("uh", [P, GROUP, D], 32, F32R), at("ul", [P, GROUP, D], 48, F32R)
        vh, vl = at("vh", [P, GROUP, D], 64, F32R), at("vl", [P, GROUP, D], 80, F32R)
        gate, al = at("gate", [P, 2, GROUP, T], 96), at("al", [P, 2, GROUP, T], 112, F32R)
        act_raw, ah = at("act_raw", [P, GROUP, T], 128), at("ah", [P, 2, GROUP, T], 136, F32R)
        bank = st.banks(8)
        hot, gated, spread, out = (st.sem(n) for n in ("hot", "gated", "spread", "out"))
        stored = [st.sem(f"stored{b}") for b in range(2)]
        u_in = [st.sem(f"u_in{c}") for c in range(2)]
        v_in = [st.sem(f"v_in{c}") for c in range(2)]
        g_in = [st.sem(f"g_in{c}") for c in range(2)]
        u_high, u_rest, v_high, v_rest = (st.sem(n) for n in ("u_high", "u_rest", "v_high", "v_rest"))
        hidden, gelued, weighed, a_high, a_rest = (st.sem(n) for n in ("hidden", "gelued", "weighed", "a_high", "a_rest"))
        made, added = st.sem("made"), st.sem("added")
        FIRST, LAST = 2, N_GROUPS - 4
        assert (LAST - FIRST) % 2 == 0

        def steps(eng, step):
            for g in range(-1, FIRST):
                step(g, g % 2)
            with eng.Fori(0, (LAST - FIRST) // 2) as i:
                for par in range(2):
                    step(i * 2 + (FIRST + par), par)
            for g in range(LAST, N_GROUPS):
                step(g, g % 2)

        def has(g, ahead):
            return not isinstance(g, int) or 0 <= g + ahead < N_GROUPS

        with nc.Block() as block:
            @block.sync
            def _(sp):
                def rows(t, g, c):
                    return t[bass.ds(g * GROUP + 2 * c, 2)].rearrange("j p n -> p j n")

                for c in range(TT):
                    if c == TT - 1:
                        sp.wait_ge(stored[0], 32)
                        for n in range(2):
                            sp.dma_start(u_raw[:, 2 * n:2 * n + 2], rows(u_dram, 0, n)).then_inc(u_in[n], 16)
                        for n in range(2):
                            sp.dma_start(v_raw[:, 2 * n:2 * n + 2], rows(v_dram, 0, n)).then_inc(v_in[n], 16)
                    sp.wait_ge(out, 2 + NB * (c + 1))
                    sp.dma_start(g_dram.rearrange("j i t -> i j t")[:, :, c * P:(c + 1) * P], G[c % 2][:]).then_inc(stored[c % 2], 16)

                sp.wait_ge(stored[1], 32)
                for b in range(2):
                    sp.dma_start(gate[:, b], g_dram[b * GROUP:(b + 1) * GROUP].rearrange("j p n -> p j n")).then_inc(g_in[b], 16)
                for c in range(2):
                    sp.wait_ge(u_rest, 2 * c + 2)
                    sp.dma_start(u_raw[:, 2 * c:2 * c + 2], rows(u_dram, 1, c)).then_inc(u_in[c], 16)

                def step(g, par):
                    vg, ug, gg = (sp.snap(g * GROUP + k * GROUP) if not isinstance(g, int) else g * GROUP + k * GROUP for k in (1, 3, 2))
                    for c in range(2):
                        if has(g, 1) and has(g, 0):
                            src = v_dram[bass.ds(vg + 2 * c, 2)].rearrange("j p n -> p j n")
                            sp.wait_ge(v_rest, g * GROUP + (2 * c + 2))
                            sp.dma_start(v_raw[:, 2 * c:2 * c + 2], src).then_inc(v_in[c], 16)
                        if has(g, 3):
                            src = u_dram[bass.ds(ug + 2 * c, 2)].rearrange("j p n -> p j n")
                            sp.wait_ge(u_rest, g * GROUP + (2 * GROUP + 2 * c + 2))
                            sp.dma_start(u_raw[:, 2 * c:2 * c + 2], src).then_inc(u_in[c], 16)
                    if has(g, 2) and has(g, 0):
                        src = g_dram[bass.ds(gg, GROUP)].rearrange("j p n -> p j n")
                        sp.wait_ge(weighed, g * GROUP + GROUP)
                        sp.dma_start(gate[:, par], src).then_inc(g_in[par], 16)

                steps(sp, step)

            @block.gpsimd
            def _(pool):
                for c in range(TT):
                    with pool.Fori(0, HALVES) as i:
                        for u in range(2):
                            t0 = i * (2 * BT) + (c * P + u * BT)
                            pool.wait_ge(hot, i * 4 + (2 * (c * NB + u) + 1))
                            pool.tensor_tensor(hot_j[:, u], hot_j[:, u],
                                               pair_g[:, bass.ds(t0, BT)].unsqueeze(2).to_broadcast([P, BT, KEYS]), ALU.mult).then_inc(gated, 1)

            @block.scalar
            def _(act):
                act.sem_inc(out, 2)
                for c in range(TT):
                    if c >= 2:
                        act.wait_ge(stored[c % 2], 16)
                    with act.Fori(0, HALVES) as i:
                        for u in range(2):
                            t0 = i * (2 * BT) + u * BT
                            act.wait_ge(spread, i * 2 + (c * NB + u + 3))
                            for q in range(2):
                                last = act.activation(G[c % 2][:, :, bass.ds(t0 + 4 * q, 4)].rearrange("p j t -> p t j"),
                                                      bank[2 * u + q][:].rearrange("p (t j) -> p t j", t=4), ACT.Copy)
                            last.then_inc(out, 1)

                def copy_u(e, s, g):
                    act.wait_ge(u_in[s // 2], g * 16 + 16)
                    if not isinstance(g, int) or g > 0:
                        act.wait_ge(hidden, e - (GROUP - 1))
                    act.activation(uh[:, s], u_raw[:, s], ACT.Copy).then_inc(u_high, 1)

                for s in range(GROUP):
                    copy_u(s, s, 0)

                def step(g, par):
                    for s in range(GROUP):
                        e = g * GROUP + s
                        if has(g, 0):
                            act.wait_ge(v_in[s // 2], g * 16 + 16)
                            if not isinstance(g, int) or g > 0:
                                act.wait_ge(made, g * BLOCKS)
                            act.activation(vh[:, s], v_raw[:, s], ACT.Copy).then_inc(v_high, 1)
                        if has(g, 1):
                            act.wait_ge(hidden, e + (GROUP + 1))
                            if not isinstance(g, int) or g >= 0:
                                act.wait_ge(a_rest, e + 1)
                            act.activation(act_raw[:, s], bank[4 + s][:], ACT.Gelu_apprx_tanh).then_inc(gelued, 1)
                        if has(g, 2):
                            copy_u(e + 2 * GROUP, s, g + 2)
                        if has(g, 1):
                            act.wait_ge(weighed, e + (GROUP + 1))
                            if not isinstance(g, int) or g > 0:
                                act.wait_ge(made, g * BLOCKS)
                            act.activation(ah[:, 1 - par, s], act_raw[:, s], ACT.Copy).then_inc(a_high, 1)

                steps(act, step)

            @block.vector
            def _(dve):
                for c in range(TT):
                    with dve.Fori(0, HALVES) as i:
                        for u in range(2):
                            t0 = i * (2 * BT) + (c * P + u * BT)
                            dve.wait_ge(spread, i * 2 + (c * NB + u + 1))
                            dve.tensor_tensor(hot_j[:, u], iota[:].unsqueeze(1).to_broadcast([P, BT, KEYS]),
                                              pair_j[:, bass.ds(t0, BT)].unsqueeze(2).to_broadcast([P, BT, KEYS]), ALU.is_equal).then_inc(hot, 1)
                            dve.tensor_tensor(hot_i[:, u], iota[:].unsqueeze(1).to_broadcast([P, BT, KEYS]),
                                              pair_i[:, bass.ds(t0, BT)].unsqueeze(2).to_broadcast([P, BT, KEYS]), ALU.is_equal).then_inc(hot, 1)

                for s in range(GROUP):
                    dve.wait_ge(u_high, s + 1)
                    dve.tensor_tensor(ul[:, s], u_raw[:, s], uh[:, s].bitcast(F32), ALU.subtract).then_inc(u_rest, 1)

                def step(g, par):
                    for s in range(GROUP):
                        e = g * GROUP + s
                        if has(g, 0):
                            dve.wait_ge(v_high, e + 1)
                            dve.tensor_tensor(vl[:, s], v_raw[:, s], vh[:, s].bitcast(F32), ALU.subtract).then_inc(v_rest, 1)
                        if has(g, 1):
                            dve.wait_ge(gelued, e + (GROUP + 1))
                            if s == 0:
                                if isinstance(g, int):
                                    dve.wait_ge(g_in[1 - par], 16 * ((g + 1) // 2 + 1))
                                else:
                                    dve.wait_ge(g_in[1 - par], (g + (2 + 1 - (1 - par))) * 8)
                            dve.tensor_tensor(act_raw[:, s], act_raw[:, s], gate[:, 1 - par, s], ALU.mult).then_inc(weighed, 1)
                        if has(g, 2):
                            dve.wait_ge(u_high, e + (2 * GROUP + 1))
                            dve.tensor_tensor(ul[:, s], u_raw[:, s], uh[:, s].bitcast(F32), ALU.subtract).then_inc(u_rest, 1)
                        if has(g, 1):
                            dve.wait_ge(a_high, e + (GROUP + 1))
                            dve.tensor_tensor(al[:, 1 - par, s], act_raw[:, s], ah[:, 1 - par, s].bitcast(F32),
                                              ALU.subtract).then_inc(a_rest, 1)
                    if has(g, 0):
                        for b in range(BLOCKS):
                            xb = X[:, b // 2, (b % 2) * 512:(b % 2 + 1) * 512]
                            dve.wait_ge(made, g * BLOCKS + (b + 1))
                            dve.tensor_tensor(xb, xb, bank[b % 4][:], ALU.add).then_inc(added, 1)

                steps(dve, step)

            @block.tensor
            def _(pe):
                pe.sem_inc(spread, 2)
                for c in range(TT):
                    with pe.Fori(0, HALVES) as i:
                        for u in range(2):
                            n = i * 2 + (c * NB + u)
                            pe.wait_ge(hot, i * 4 + (2 * (c * NB + u) + 2))
                            pe.wait_ge(gated, n + 1)
                            pe.wait_ge(out, n + 1)
                            for t in range(BT):
                                last = pe.matmul(bank[2 * u + t // 4][:, (t % 4) * P:(t % 4 + 1) * P],
                                                 hot_i[:, u, t], hot_j[:, u, t], start=True, stop=True)
                            last.then_inc(spread, 1)

                def step(g, par):
                    if has(g, 1):
                        for s in range(GROUP):
                            e = g * GROUP + (GROUP + s)
                            pe.wait_ge(u_rest, e + 1)
                            if not isinstance(g, int) or g >= 0:
                                pe.wait_ge(gelued, e - (GROUP - 1))
                            for k in range(KT):
                                hi, lo = uh[:, s, k * P:(k + 1) * P], ul[:, s, k * P:(k + 1) * P]
                                pe.matmul(bank[4 + s][:], hi, xh[:, k], start=(k == 0), stop=False)
                                pe.matmul(bank[4 + s][:], hi, xl[:, k], start=False, stop=False)
                                last = pe.matmul(bank[4 + s][:], lo, xh[:, k], start=False, stop=(k == KT - 1))
                            last.then_inc(hidden, 1)
                    if has(g, 0):
                        pe.wait_ge(a_rest, g * GROUP + GROUP)
                        pe.wait_ge(v_rest, g * GROUP + GROUP)
                        for b in range(BLOCKS):
                            if not isinstance(g, int) or g * BLOCKS + b >= 4:
                                pe.wait_ge(added, g * BLOCKS + (b - 3))
                            tok, col = slice(b // 2 * P, (b // 2 + 1) * P), slice(b % 2 * 512, (b % 2 + 1) * 512)
                            for s in range(GROUP):
                                hi, lo = ah[:, par, s, tok], al[:, par, s, tok]
                                pe.matmul(bank[b % 4][:], hi, vh[:, s, col], start=(s == 0), stop=False)
                                pe.matmul(bank[b % 4][:], hi, vl[:, s, col], start=False, stop=False)
                                last = pe.matmul(bank[b % 4][:], lo, vh[:, s, col], start=False, stop=(s == GROUP - 1))
                            last.then_inc(made, 1)

                steps(pe, step)


def peer(nc, K, layer, ins, g_dram):
    name = f"peer{layer}"
    with Stage(nc, name) as st:
        xh, xl = st.sb("xh", [P, KT, T], F32R), st.sb("xl", [P, KT, T], F32R)
        arena = (nc.sbuf_base + 31) // 32 * 32
        pair_i, pair_j, pair_g = (
            nc.alloc_sbuf_tensor_at(f"{name}_{n}", [P, T], F32, offset=arena + (144 + 2 * i) * 1024)
            for i, n in enumerate(("pair_i", "pair_j", "pair_g")))
        with Stage(nc, name + "x") as sx:
            xT = sx.sb("xT", [P, KT, T])
            for n in ("tab_i", "tab_j", "tab_g"):
                K[n] = sx.sb(n, [P, TT, PAIRS])
            buf = {"wq": sx.sb("wq", [P, 2, KT, QD]), "keys": sx.sb("keys", [P, 2, 2, KEYS]),
                   "w_in": [sx.sem(f"w_in{b}") for b in range(2)], "k_in": [sx.sem(f"k_in{b}") for b in range(2)]}
            own = {"wq": ins["peer_wq_l"][layer], "keys": ins["peer_keys_l"][layer]}

            def first_heads(sp):
                for h in range(2):
                    load_head(sp, buf, own, h)

            norm_transpose(nc, K, name + "n", ins["norm_ffn_c"][layer], xT, ahead=first_heads)
            peer_retrieve(nc, K, name + "r", buf, own, xT, (xh, xl), pair_i, pair_j, pair_g,
                          limit=arena + 144 * 1024)
        peer_mix(nc, K, name + "e", ins["peer_u_l"][layer], ins["peer_v_l"][layer], g_dram, xh, xl,
                 arena, pair_i, pair_j, pair_g)




def even_mixer(nc, K, ins):
    with Stage(nc, "ev") as st:
        top = nc.sbuf_usable_end // 32 * 32 - TT * 2 * MIX * 4
        cat = nc.alloc_sbuf_tensor_at("ev_cat", [P, TT, 2 * MIX], F32, offset=top)
        w_out = OutputWeights(nc, st, "ev", ins["ev_w_out_l"], top)

        with Stage(nc, "evi") as si:
            B = {
                "u": si.sb("u", [P, TT, MIX]), "v": si.sb("v", [P, TT, MIX]),
                "qk": si.sb("qk", [P, 2 * H_E, T]),
                "v1": si.sb("v1", [P, TT, H_E, D_E + 1]),
                "og": si.sb("og", [P, TT, MIX]),
                "li": si.sb("li", [H_E, T]), "lf": si.sb("lf", [H_E, T]),
            }
            with Stage(nc, "evx") as sx:
                W = {"raw": sx.sb("w_raw", [P, KT, MIX]), "in": sx.sem("w_in")}
                xh, xl = sx.sb("xh", [P, KT, T], F32R), sx.sb("xl", [P, KT, T], F32R)
                norm_transpose(nc, K, "evn", ins["norm_mix_c"][0], split=(xh, xl),
                               ahead=lambda sp: sp.dma_start(W["raw"][:], ins["ev_w_in_l"][0]).then_inc(W["in"], 16))
                even_project(nc, K, ins, (xh, xl), W, B)
            even_gating(nc, K, ins, B, cat, w_out.load)
            with Stage(nc, "evw") as sw:
                wT = sw.sb("wT", [P, H_E, TT, P])
                col = sw.sb("col", [P, 4, TT, H_E])
                dec = sw.sb("dec", [P, H_E, TT])
                mlstm_gates(nc, K, B, wT, col, dec, w_out)
                mlstm_cells(nc, K, ins, B, wT, col, dec, cat, w_out)
        project_out(nc, K, "evo", w_out.split, cat=cat)


def even_project(nc, K, ins, x, W, B):
    QK = 2 * H_E
    ITEMS = QK + 1 + 4 * TT
    FQ = 32
    raw, w_in = W["raw"], W["in"]
    with Stage(nc, "evp") as st:
        wh, wl = st.sb("wh", [P, 2, KT, MIX], F32R), st.sb("wl", [P, 2, KT, MIX], F32R)
        gh = st.sb("gh", [P, KT, P], F32R)
        wg, gl = st.sb_split("wg", [P, KT, P])
        cw, cb = st.sb("cw", [P, QK, CONV]), st.sb("cb", [P, QK])
        bias = st.sb("bias", [P, 1])
        lin = st.sb("lin", [H_E, 3, T])
        bank = st.banks(8)
        small_in, made, by_dve, by_act = (st.sem(n) for n in ("small_in", "made", "by_dve", "by_act"))
        w_high, w_rest, g_high, g_rest = (st.sem(n) for n in ("w_high", "w_rest", "g_high", "g_rest"))
        step, silued, fed, expd, logged = (st.sem(n) for n in ("step", "silued", "fed", "expd", "logged"))
        first_item = [0, 4] + [QK + 1 + n * TT for n in range(4)]

        with nc.Block() as block:
            @block.sync
            def _(sp):
                sp.dma_start(cw[:], ins["ev_conv_w_l"]).then_inc(small_in, 16)
                sp.dma_start(cb[:], ins["ev_conv_b_l"]).then_inc(small_in, 16)
                sp.dma_start(wg[:], ins["ev_w_gates_l"]).then_inc(small_in, 16)
                sp.dma_start(bias[0:H_E], ins["ev_bias_l"][0]).then_inc(small_in, 16)
                sp.dma_start(bias[FQ:FQ + H_E], ins["ev_bias_l"][1]).then_inc(small_in, 16)
                for b in range(1, 6):
                    sp.wait_ge(w_rest, KT * b)
                    sp.dma_start(raw[:], ins["ev_w_in_l"][b]).then_inc(w_in, 16)

            @block.tensor
            def _(pe):
                for n in range(ITEMS):
                    if n >= 8:
                        if n - 8 <= QK:
                            pe.wait_ge(by_dve, n - 8 + 1)
                        else:
                            pe.wait_ge(by_act, n - 8 - QK)
                    if n == QK:
                        pe.wait_ge(g_rest, 1)
                    for k in range(KT):
                        flags = (k == 0, k == KT - 1)
                        xk = (x[0][:, k], x[1][:, k])
                        if n in first_item:
                            pe.wait_ge(w_rest, KT * first_item.index(n) + k + 1)
                        if n < QK:
                            s = (slice(None), n // 4, k, slice(n % 4 * P, (n % 4 + 1) * P))
                            last = split_product(pe, bank[n % 8][:], (wh[s], wl[s]), xk, *flags)
                        elif n == QK:
                            last = split_product(pe, bank[n % 8][:], (gh[:, k], gl[:, k]), xk, *flags)
                        else:
                            b, c = 2 + (n - QK - 1) // TT, (n - QK - 1) % TT
                            tok = slice(c * P, (c + 1) * P)
                            last = split_product(pe, bank[n % 8][:], (x[0][:, k, tok], x[1][:, k, tok]),
                                                 (wh[:, b % 2, k], wl[:, b % 2, k]), *flags)
                    last.then_inc(made, 1)

            def block_free(eng, b):
                if b >= 2:
                    eng.wait_ge(made, first_item[b - 1])

            @block.vector
            def _(dve):
                own = Chain(dve, step)
                qk = B["qk"]

                def rest(b):
                    for k in range(KT):
                        dve.wait_ge(w_high, KT * b + k + 1)
                        dve.tensor_tensor(wl[:, b % 2, k], raw[:, k], wh[:, b % 2, k].bitcast(F32), ALU.subtract).then_inc(w_rest, 1)

                def convolve(n):
                    z = bank[n % 8]
                    dve.wait_ge(made, n + 1)
                    own.then(dve.tensor_scalar(qk[:, n], z[:], cw[:, n, 3:4], cb[:, n:n + 1], ALU.mult, ALU.add))
                    for back in range(1, CONV):
                        tap = dve.scalar_tensor_tensor(out=qk[:, n, back:T], in0=z[:, 0:T - back], scalar=cw[:, n, 3 - back:4 - back],
                                                       in1=qk[:, n, back:T], op0=ALU.mult, op1=ALU.add)
                        if back < CONV - 1:
                            own.then(tap)
                        else:
                            tap.then_inc(by_dve, 1)

                rest(0)
                dve.wait_ge(small_in, 80)
                dve.wait_ge(g_high, 1)
                dve.tensor_tensor(gl[:], wg[:], as_f32(gh[:]), ALU.subtract).then_inc(g_rest, 1)
                rest(1)
                for n in range(QK):
                    convolve(n)
                    if n == 4:
                        rest(2)
                dve.wait_ge(made, QK + 1)
                gate = bank[QK % 8]
                dve.tensor_scalar(B["li"][:], gate[0:H_E, :], bias[0:H_E, 0:1], None, ALU.add)
                dve.tensor_scalar(lin[:, 0], gate[FQ:FQ + H_E, :], bias[FQ:FQ + H_E, 0:1], None, ALU.add).then_inc(by_dve, 1)
                dve.wait_ge(by_dve, QK + 1)
                rest(3)
                own.then(dve.tensor_scalar(lin[:, 1], lin[:, 0], -1.0, None, ALU.mult))
                own.then(dve.tensor_tensor(lin[:, 1], lin[:, 0], lin[:, 1], ALU.max))
                dve.sem_inc(fed, 1)
                dve.memset(B["v1"][:, :, :, D_E:D_E + 1], 1.0)
                own.then(dve.tensor_scalar(lin[:, 2], lin[:, 0], 0.0, None, ALU.min))
                for n in range(H_E):
                    dve.wait_ge(silued, n + 1)
                    dve.tensor_scalar(qk[:, n], qk[:, n], float(np.float32(D_E ** -0.5)), None, ALU.mult)
                rest(4)
                rest(5)
                dve.wait_ge(logged, 1)
                dve.tensor_tensor(B["lf"][:], lin[:, 2], lin[:, 1], ALU.subtract)

            @block.scalar
            def _(act):
                def high(b):
                    act.wait_ge(w_in, 16 * (b + 1))
                    block_free(act, b)
                    for k in range(KT):
                        act.activation(wh[:, b % 2, k], raw[:, k], ACT.Copy).then_inc(w_high, 1)

                high(0)
                act.wait_ge(small_in, 80)
                act.activation(gh[:], wg[:], ACT.Copy).then_inc(g_high, 1)
                high(1)
                high(2)
                for n in range(QK):
                    act.wait_ge(by_dve, n + 1)
                    act.activation(B["qk"][:, n], B["qk"][:, n], ACT.Silu).then_inc(silued, 1)
                high(3)
                for n in range(4 * TT):
                    b, c = n // TT, n % TT
                    act.wait_ge(made, QK + 1 + n + 1)
                    src = bank[(QK + 1 + n) % 8]
                    if b < 2:
                        done = act.activation(B["uv"[b]][:, c], src[:], ACT.Gelu_apprx_tanh)
                    elif b == 2:
                        done = act.activation(B["v1"][:, c, :, 0:D_E], src[:].rearrange("p (h d) -> p h d", h=H_E), ACT.Copy)
                    else:
                        done = act.activation(B["og"][:, c], src[:], ACT.Sigmoid)
                    done.then_inc(by_act, 1)
                    if c == TT - 1 and b < 2:
                        high(4 + b)
                act.wait_ge(fed, 1)
                act.activation(lin[:, 1], lin[:, 1], ACT.Exp, scale=-1.0).then_inc(expd, 1)
                act.wait_ge(expd, 1)
                act.activation(lin[:, 1], lin[:, 1], ACT.Ln, bias=K["one"][0:H_E, 0:1]).then_inc(logged, 1)


def even_gating(nc, K, ins, B, cat, ahead):
    N = TT * G_N
    with Stage(nc, "evg") as st:
        ws = st.sb("ws", [P, G_N, P])
        sb = st.sb("sb", [P, G_N])
        gain = st.sb("gain", [P, MIX])
        sqr = st.sb("sqr", [P, N, G_D])
        ss, root, y, t1 = (st.sb(n, [P, N]) for n in ("ss", "root", "y", "t1"))
        bank = st.banks(4)
        ws_in, rest_in, masked, step, summed, rooted, made = (st.sem(n) for n in ("ws_in", "rest_in", "masked", "step", "summed", "rooted", "made"))
        with nc.Block() as block:
            @block.sync
            def _(sp):
                sp.dma_start(ws[:], ins["ev_gm_ws_l"]).then_inc(ws_in, 16)
                sp.dma_start(sb[:], ins["ev_gm_b_l"]).then_inc(rest_in, 16)
                sp.dma_start(gain[:], ins["ev_gm_v_gain"].to_broadcast([P, MIX])).then_inc(rest_in, 16)
                ahead(sp)

            @block.gpsimd
            def _(pool):
                pool.wait_ge(ws_in, 16)
                pool.affine_select(out=ws[:], in_=ws[:], compare_op=ALU.is_ge, fill=0.0, base=0,
                                   pattern=[[0, G_N], [1, P]], channel_multiplier=-1).then_inc(masked, 1)

            @block.scalar
            def _(act):
                act.wait_ge(summed, 1)
                act.activation(root[:], ss[:], ACT.Sqrt, scale=1.0 / G_D, bias=K["eps"][:, 0:1]).then_inc(rooted, 1)

            @block.vector
            def _(dve):
                own = Chain(dve, step)
                v = B["v"][:].rearrange("p c (g d) -> p (c g) d", g=G_N)
                own.then(dve.tensor_tensor(sqr[:], v, v, ALU.mult))
                own.then(dve.tensor_reduce(ss[:], sqr[:], AX.X, ALU.add))
                dve.sem_inc(summed, 1)
                rsqrt_newton(dve, own, rooted, 1, ss, root, y, t1, G_D)
                own.then(dve.tensor_tensor(v, v, y[:].unsqueeze(2).to_broadcast([P, N, G_D]), ALU.mult))
                dve.wait_ge(rest_in, 32)
                own.then(dve.tensor_tensor(B["v"][:], B["v"][:], gain[:].unsqueeze(1).to_broadcast([P, TT, MIX]), ALU.mult))
                normed = own.n
                for c in range(TT):
                    dve.wait_ge(made, c + 1)
                    for g in range(G_N):
                        ch = slice(g * G_D, (g + 1) * G_D)
                        dve.scalar_tensor_tensor(out=cat[:, c, ch], in0=bank[c][:, ch], scalar=sb[:, g:g + 1],
                                                 in1=B["u"][:, c, ch], op0=ALU.add, op1=ALU.mult)
                assert normed == 10, normed

            @block.tensor
            def _(pe):
                pe.wait_ge(masked, 1)
                pe.wait_ge(step, 10)
                for c in range(TT):
                    for g in range(G_N):
                        ch = slice(g * G_D, (g + 1) * G_D)
                        last = pe.matmul(bank[c][:, ch], ws[:, g], B["v"][:, c, ch], start=True, stop=True)
                    last.then_inc(made, 1)


def rsqrt_newton(dve, own, rooted, count, ss, root, y, t1, width):
    widths = width if isinstance(width, list) else [(slice(None), width)]
    dve.wait_ge(rooted, count)
    own.then(dve.reciprocal(y[:], root[:]))
    for cols, w in widths:
        last = dve.tensor_scalar(ss[:, cols], ss[:, cols], 1.0 / w, EPS, ALU.mult, ALU.add)
    own.then(last)
    own.then(dve.tensor_tensor(t1[:], y[:], y[:], ALU.mult))
    own.then(dve.tensor_tensor(t1[:], t1[:], ss[:], ALU.mult))
    own.then(dve.tensor_scalar(t1[:], t1[:], -0.5, 1.5, ALU.mult, ALU.add))
    own.then(dve.tensor_tensor(y[:], y[:], t1[:], ALU.mult))


def mlstm_gates(nc, K, B, wT, col, dec, w_out):
    with Stage(nc, "evm") as st:
        ones = st.sb("ones", [H_E, P])
        b = st.sb("b", [H_E, TT, P])
        M = st.sb("M", [H_E, TT, P])
        row = st.sb("row", [H_E, 4, TT, P])
        m = st.sb("m", [H_E, TT + 1])
        dr = st.sb("dr", [H_E, TT])
        bank = st.banks(6)
        step, maxed, rowed, expd, turned, spread, colled, lagged, weighed = (
            st.sem(n) for n in ("step", "maxed", "rowed", "expd", "turned", "spread", "colled", "lagged", "weighed"))
        with nc.Block() as block:
            @block.vector
            def _(dve):
                own = Chain(dve, step)
                dve.memset(ones[:], 1.0)
                own.then(dve.memset(m[:], 0.0))
                lf = B["lf"][:].rearrange("h (c t) -> h c t", c=TT)
                li = B["li"][:].rearrange("h (c t) -> h c t", c=TT)
                for c in range(TT):
                    last = dve.tensor_tensor_scan(b[:, c], ones[:], lf[:, c], 0.0, ALU.mult, ALU.add)
                own.then(last)
                own.then(dve.tensor_tensor(row[:, 0], li, b[:], ALU.subtract))
                for c in range(TT):
                    own.then(dve.tensor_tensor_scan(M[:, c], row[:, 0, c], row[:, 0, c], m[:, c:c + 1], ALU.max, ALU.max))
                    own.then(dve.tensor_tensor(m[:, c + 1:c + 2], b[:, c, P - 1:P], M[:, c, P - 1:P], ALU.add))
                dve.sem_inc(maxed, 1)
                for c in range(TT):
                    dve.tensor_scalar(row[:, 1, c], M[:, c], m[:, c:c + 1], None, ALU.subtract)
                    dve.tensor_scalar(row[:, 3, c], row[:, 0, c], M[:, c, P - 1:P], None, ALU.subtract)
                dve.tensor_tensor(dr[:], M[:, :, P - 1], m[:, 0:TT], ALU.subtract)
                own.then(dve.tensor_tensor(row[:, 2], b[:], M[:], ALU.add))
                dve.sem_inc(rowed, 1)
                dve.wait_ge(turned, 1)
                dve.tensor_copy(col[:].rearrange("p k c h -> p (k c h)"), bank[4][:, 0:4 * TT * H_E]).then_inc(colled, 1)
                dve.wait_ge(colled, 1)
                dve.wait_ge(spread, 1)
                for h in range(H_E):
                    for c in range(TT):
                        last = dve.tensor_scalar(wT[:, h, c], bank[h][:, c * P:(c + 1) * P], col[:, 0, c, h:h + 1], 0.0,
                                                 ALU.subtract, ALU.max)
                last.then_inc(lagged, 1)
                dve.wait_ge(spread, 2)
                dve.tensor_copy(dec[:].rearrange("p h c -> p (h c)"), bank[5][:, 0:TT * H_E])

            @block.scalar
            def _(act):
                for k in range(KT):
                    w_out.copy_high(act, k)
                act.wait_ge(rowed, 1)
                act.activation(row[:, 1:3], row[:, 1:3], ACT.Exp, scale=-1.0)
                act.activation(dr[:], dr[:], ACT.Exp, scale=-1.0)
                act.activation(row[:, 3], row[:, 3], ACT.Exp).then_inc(expd, 1)
                act.wait_ge(lagged, 1)
                act.activation(wT[:], wT[:], ACT.Exp, scale=-1.0).then_inc(weighed, 1)

            @block.tensor
            def _(pe):
                pe.wait_ge(maxed, 1)
                for h in range(H_E):
                    last = pe.matmul(bank[h][:], K["sel"][:, h], M[:].rearrange("h c t -> h (c t)"), start=True, stop=True)
                last.then_inc(spread, 1)
                pe.wait_ge(expd, 1)
                for k in range(4):
                    for c in range(TT):
                        o = (k * TT + c) * H_E
                        last = pe.transpose(bank[4][:, o:o + H_E], row[:, k, c], K["ident"][0:H_E, 0:H_E])
                last.then_inc(turned, 1)
                for h in range(H_E):
                    last = pe.matmul(bank[5][:, h * TT:(h + 1) * TT], K["sel"][:, h], dr[:], start=True, stop=True)
                last.then_inc(spread, 1)

            @block.gpsimd
            def _(pool):
                for k in range(KT // 2):
                    w_out.take_rest(pool, k)
                pool.wait_ge(weighed, 1)
                w = wT[:].rearrange("p h c t -> p (h c) t")
                pool.affine_select(out=w, in_=w, compare_op=ALU.is_ge, fill=0.0, base=0,
                                   pattern=[[0, H_E * TT], [1, P]], channel_multiplier=-1)


def mlstm_cells(nc, K, ins, B, wT, col, dec, cat, w_out):
    W = D_E + 1
    N = TT * H_E
    with Stage(nc, "evc") as st:
        kw = st.sb("kw", [P, N, D_E])
        state = st.sb("state", [P, TT, H_E, W])
        num = st.sb("num", [P, N, W])
        inter = st.sb("inter", [P, N, W])
        den, den2 = st.sb("den", [P, N]), st.sb("den2", [P, N])
        ss, root, y, t1 = (st.sb(n, [P, N]) for n in ("ss", "root", "y", "t1"))
        gain = st.sb("gain", [P, MIX])
        assert nc.sbuf_base <= w_out.bottom
        bank = st.banks(8)
        gain_in, turned, keyed, scored, weighed, summed, intered = (
            st.sem(n) for n in ("gain_in", "turned", "keyed", "scored", "weighed", "summed", "intered"))
        stated, carried, scaled, numbered, step, rooted, squared = (
            st.sem(n) for n in ("stated", "carried", "scaled", "numbered", "step", "rooted", "squared"))
        qk, v1 = B["qk"], B["v1"]

        with nc.Block() as block:
            @block.sync
            def _(sp):
                sp.dma_start(gain[:], ins["ev_h_gain"].to_broadcast([P, MIX])).then_inc(gain_in, 16)

            @block.gpsimd
            def _(pool):
                for k in range(KT // 2, KT):
                    w_out.take_rest(pool, k)

            @block.tensor
            def _(pe):
                for c in range(TT):
                    tok = slice(c * P, (c + 1) * P)
                    if c >= 2:
                        pe.wait_ge(keyed, H_E * (c - 1))
                    for h in range(H_E):
                        last = pe.transpose(bank[c % 2][:, h * P:(h + 1) * P], qk[:, H_E + h, tok], K["ident"][:])
                    last.then_inc(turned, 1)
                    if c >= 2:
                        pe.wait_ge(weighed, c - 1)
                    for h in range(H_E):
                        last = pe.matmul(bank[2 + c % 2][:, h * P:(h + 1) * P], qk[:, H_E + h, tok], qk[:, h, tok], start=True, stop=True)
                    last.then_inc(scored, 1)
                pe.wait_ge(keyed, N)
                for c in range(TT):
                    tok = slice(c * P, (c + 1) * P)
                    for h in range(H_E):
                        n = c * H_E + h
                        if c < TT - 1:
                            if n >= 2:
                                pe.wait_ge(carried, n - 1)
                            pe.matmul(bank[6 + n % 2][:, 0:W], kw[:, n], v1[:, c, h], start=True, stop=True).then_inc(stated, 1)
                        pe.wait_ge(weighed, c + 1)
                        if n >= 2:
                            pe.wait_ge(numbered, n - 1)
                        pe.matmul(bank[4 if n % 2 else 0][:, 0:W], wT[:, h, c], v1[:, c, h], start=True, stop=True).then_inc(summed, 1)
                        if c:
                            pe.wait_ge(carried, n - H_E + 1)
                            if n >= H_E + 2:
                                pe.wait_ge(intered, n - H_E - 1)
                            pe.matmul(bank[5 if n % 2 else 1][:, 0:W], qk[:, h, tok], state[:, c, h], start=True, stop=True).then_inc(scaled, 1)

            @block.scalar
            def _(act):
                for n in range(N):
                    c, h = n // H_E, n % H_E
                    act.wait_ge(turned, c + 1)
                    act.activation(kw[:, n], bank[c % 2][:, h * P:(h + 1) * P], ACT.Copy, scale=col[:, 3, c, h:h + 1]).then_inc(keyed, 1)
                for n in range(H_E, N):
                    c, h = n // H_E, n % H_E
                    act.wait_ge(scaled, n - H_E + 1)
                    act.activation(inter[:, n], bank[5 if n % 2 else 1][:, 0:W], ACT.Copy, scale=col[:, 1, c, h:h + 1]).then_inc(intered, 1)
                act.wait_ge(squared, 1)
                act.activation(root[:], ss[:], ACT.Sqrt, scale=1.0 / D_E, bias=K["eps"][:, 0:1]).then_inc(rooted, 1)

            @block.vector
            def _(dve):
                own = Chain(dve, step)
                for c in range(TT):
                    dve.wait_ge(scored, c + 1)
                    dve.tensor_tensor(wT[:, :, c], bank[2 + c % 2][:].rearrange("p (h t) -> p h t", h=H_E), wT[:, :, c], ALU.mult).then_inc(weighed, 1)

                def number(n):
                    dve.wait_ge(summed, n + 1)
                    if n >= H_E:
                        dve.wait_ge(intered, n - H_E + 1)
                        dve.tensor_tensor(num[:, n], bank[4 if n % 2 else 0][:, 0:W], inter[:, n], ALU.add).then_inc(numbered, 1)
                    else:
                        dve.tensor_copy(num[:, n], bank[4 if n % 2 else 0][:, 0:W]).then_inc(numbered, 1)

                for n in range(N):
                    c, h = n // H_E, n % H_E
                    if c < TT - 1:
                        dve.wait_ge(stated, n + 1)
                        if c == 0:
                            dve.tensor_copy(state[:, 1, h], bank[6 + n % 2][:, 0:W]).then_inc(carried, 1)
                        else:
                            dve.wait_ge(carried, n - H_E + 1)
                            dve.scalar_tensor_tensor(out=state[:, c + 1, h], in0=state[:, c, h], scalar=dec[:, h, c:c + 1],
                                                     in1=bank[6 + n % 2][:, 0:W], op0=ALU.mult, op1=ALU.add).then_inc(carried, 1)
                    number(n)
                dve.wait_ge(numbered, N)
                own.then(dve.tensor_copy(den[:], num[:, :, D_E]))
                own.then(dve.tensor_scalar(den2[:], den[:], -1.0, None, ALU.mult))
                own.then(dve.tensor_tensor(den[:], den[:], den2[:], ALU.max))
                own.then(dve.tensor_tensor(den[:], den[:], col[:, 2].rearrange("p c h -> p (c h)"), ALU.max))
                own.then(dve.reciprocal(den[:], den[:]))
                hh = inter[:, :, 0:D_E]
                own.then(dve.tensor_tensor(hh, num[:, :, 0:D_E], den[:].unsqueeze(2).to_broadcast([P, N, D_E]), ALU.mult))
                own.then(dve.tensor_tensor(num[:, :, 0:D_E], hh, hh, ALU.mult))
                own.then(dve.tensor_reduce(ss[:], num[:, :, 0:D_E], AX.X, ALU.add))
                dve.sem_inc(squared, 1)
                rsqrt_newton(dve, own, rooted, 1, ss, root, y, t1, D_E)
                own.then(dve.tensor_tensor(hh, hh, y[:].unsqueeze(2).to_broadcast([P, N, D_E]), ALU.mult))
                dve.wait_ge(gain_in, 16)
                own.then(dve.tensor_tensor(B["og"][:], B["og"][:], gain[:].unsqueeze(1).to_broadcast([P, TT, MIX]), ALU.mult))
                for c in range(TT):
                    dve.tensor_tensor(cat[:, c, MIX:2 * MIX].rearrange("p (h d) -> p h d", h=H_E), inter[:, c * H_E:(c + 1) * H_E, 0:D_E],
                                      B["og"][:, c].rearrange("p (h d) -> p h d", h=H_E), ALU.mult)



def mla_mixer(nc, K, ins):
    LAT, KB = Q_LORA + KV_LORA, 1024
    QK_, VK = Q_LORA // P, KV_LORA // P
    with Stage(nc, "od") as st:
        end = nc.sbuf_usable_end // 32 * 32

        def below(n, shape, kb, dt=F32R):
            return nc.alloc_sbuf_tensor_at(f"od_{n}", shape, dt, offset=end - kb * KB)

        c = below("ch", [P, LAT // P, T], 12), below("cl", [P, LAT // P, T], 24)
        cos, sin = below("cos", [P, T], 26, F32), below("sin", [P, T], 28, F32)
        W, rest = ({n: below(f"w{n}{'_rest' if dt == F32R else ''}", [P, tiles, width], kb, dt) for n, tiles, width, kb in
                    (("q", QK_, H_A * NOPE, 44), ("r", QK_, H_A * ROPE, 52), ("k", VK, H_A * NOPE, 60), ("v", VK, H_A * V_D, 68))}
                   for dt in (F32, F32R))
        held = end - 68 * KB
        o = below("oh", [P, H_A, T], 16), below("ol", [P, H_A, T], 32)
        w_out = OutputWeights(nc, st, "od", ins["od_w_out_l"], end - 32 * KB)
        wr_in, heads_in, tab_in = (st.sem(n) for n in ("wr_in", "heads_in", "tab_in"))
        lat_in = [st.sem(f"lat_in{n}") for n in range(2)]

        kr = st.sb("kr", [P, T])
        with Stage(nc, "odx") as sx:
            xh, xl = sx.sb("xh", [P, KT, T], F32R), sx.sb("xl", [P, KT, T], F32R)
            w, wl = sx.sb_split("w", [P, KT, LAT])
            wr, rl = sx.sb_split("wr", [P, KT, P])

            def loads(sp):
                sp.dma_start(wr[:], ins["od_w_kr_l"]).then_inc(wr_in, 16)
                for n in range(2):
                    ks = slice(n * KT // 2, (n + 1) * KT // 2)
                    sp.dma_start(w[:, ks], ins["od_w_lat_l"][:, ks]).then_inc(lat_in[n], 16)
                sp.dma_start(cos[:], ins["cos_t"]).then_inc(tab_in, 16)
                sp.dma_start(sin[:], ins["sin_t"]).then_inc(tab_in, 16)
                for n, src in (("q", "od_w_uq_l"), ("r", "od_w_qr_l"), ("k", "od_w_uk_l"), ("v", "od_w_uv_l")):
                    sp.dma_start(W[n][:], ins[src]).then_inc(heads_in, 16)

            norm_transpose(nc, K, "odn", ins["norm_mix_c"][1], split=(xh, xl), ahead=loads)
            mla_latents(nc, K, ins, (xh, xl), (w, wl), (wr, rl), c, cos, sin, kr, lat_in, wr_in, tab_in, limit=held)
        with Stage(nc, "odq") as sq:
            qT = sq.sb("qT", [P, H_A, T])
            qr = sq.sb("qr", [P, H_A // 2, T])
            kT = sq.sb("kT", [P, H_A, T])
            v = sq.sb("v", [P, TT, H_A * V_D])
            mla_heads(nc, K, W, rest, heads_in, c, cos, sin, qT, qr, kT, v, limit=held)
            mla_attend(nc, K, qT, qr, kT, kr, v, o, w_out)
        project_out(nc, K, "odo", w_out.split, split=o)


def rotate(dve, own, out, rows, cos, sin, tmp):
    H = ROPE // 2
    for a in range(0, P, H):
        b = a + H if a % ROPE == 0 else a - H
        dve.tensor_tensor(tmp[b:b + H], rows[a:a + H], sin[a:a + H], ALU.mult)
    own.then(dve.tensor_tensor(out, rows, cos[:], ALU.mult))
    own.then(dve.tensor_tensor(out, out, tmp, ALU.add))


def mla_latents(nc, K, ins, x, weights, key_weights, c, cos, sin, kr, lat_in, wr_in, tab_in, limit):
    w, wl = weights
    wr, rl = key_weights
    LAT = Q_LORA + KV_LORA
    LK, HALF = LAT // P, TT // 2
    KR = 7
    with Stage(nc, "odl") as st:
        wh, rh = st.sb("wh", [P, KT, LAT], F32R), st.sb("rh", [P, KT, P], F32R)
        lat = st.sb("lat", [P, TT, LAT])
        sqr = st.sb("sqr", [P, 2, Q_LORA])
        gcol = st.sb("gcol", [P, LK])
        tmp = st.sb("tmp", [P, T])
        ss, root, y, t1 = (st.sb(n, [P, 2 * TT]) for n in ("ss", "root", "y", "t1"))
        assert nc.sbuf_base <= limit
        bank = st.banks(8)
        gain_in, made, w_high, w_rest, keyed = (st.sem(n) for n in ("gain_in", "made", "w_high", "w_rest", "keyed"))
        step, squared, rooted, turned, scaled, scaled_act, c_high = (
            st.sem(n) for n in ("step", "squared", "rooted", "turned", "scaled", "scaled_act", "c_high"))
        PARTS = ((0, Q_LORA), (Q_LORA, LAT))
        WIDTHS = [(slice(p * TT, (p + 1) * TT), b - a) for p, (a, b) in enumerate(PARTS)]
        with nc.Block() as block:
            @block.sync
            def _(sp):
                sp.dma_start(gcol[:], ins["od_gain_l"]).then_inc(gain_in, 16)

            @block.tensor
            def _(pe):
                pe.wait_ge(w_rest, 1)
                for k in range(KT):
                    last = split_product(pe, bank[KR][:], (rh[:, k], rl[:, k]), (x[0][:, k], x[1][:, k]), k == 0, k == KT - 1)
                last.then_inc(made, 1)
                for k in range(KT):
                    pe.wait_ge(w_rest, k + 2)
                    for t in range(TT):
                        tok = slice(t * P, (t + 1) * P)
                        for part, (a, b) in enumerate(PARTS):
                            if k == 0 and 2 * t + part == KR:
                                pe.wait_ge(keyed, 1)
                            last = split_product(pe, bank[2 * t + part][:, 0:b - a], (x[0][:, k, tok], x[1][:, k, tok]),
                                                 (wh[:, k, a:b], wl[:, k, a:b]), k == 0, k == KT - 1)
                            if k == KT - 1:
                                last.then_inc(made, 1)
                pe.wait_ge(scaled, 1)
                pe.wait_ge(scaled_act, 1)
                for k in range(LK):
                    for t in range(TT):
                        last = pe.transpose(bank[k][:, t * P:(t + 1) * P], lat[:, t, k * P:(k + 1) * P], K["ident"][:])
                    last.then_inc(turned, 1)

            def scale(eng, tiles, op):
                for t in tiles:
                    for part, (a, b) in enumerate(PARTS):
                        last = op(lat[:, t, a:b], bank[2 * t + part][:, 0:b - a], y[:, part * TT + t:part * TT + t + 1])
                return last

            @block.scalar
            def _(act):
                act.wait_ge(wr_in, 16)
                act.activation(rh[:], wr[:], ACT.Copy).then_inc(w_high, 1)
                for k in range(KT):
                    act.wait_ge(lat_in[k // (KT // 2)], 16)
                    act.activation(wh[:, k], w[:, k], ACT.Copy).then_inc(w_high, 1)
                for t in range(TT):
                    for part, (a, b) in enumerate(PARTS):
                        n = 2 * t + part
                        act.wait_ge(made, n + 2)
                        if n >= 2:
                            act.wait_ge(squared, n - 1)
                        act.activation(sqr[:, part, 0:b - a], bank[n][:, 0:b - a], ACT.Square,
                                       accum_out=ss[:, part * TT + t:part * TT + t + 1]).then_inc(squared, 1)
                act.wait_ge(squared, 2 * TT)
                for cols, width in WIDTHS:
                    last = act.activation(root[:, cols], ss[:, cols], ACT.Sqrt, scale=1.0 / width, bias=K["eps"][:, 0:1])
                last.then_inc(rooted, 1)
                act.wait_ge(step, 2 + 6)
                scale(act, range(HALF, TT), lambda o, i, s: act.activation(o, i, ACT.Copy, scale=s)).then_inc(scaled_act, 1)
                act.wait_ge(gain_in, 16)
                for k in range(LK):
                    act.wait_ge(turned, k + 1)
                    act.activation(c[0][:, k], bank[k][:], ACT.Copy, scale=gcol[:, k:k + 1]).then_inc(c_high, 1)

            @block.vector
            def _(dve):
                own = Chain(dve, step)
                dve.wait_ge(w_high, 1)
                dve.tensor_tensor(rl[:], wr[:], as_f32(rh[:]), ALU.subtract).then_inc(w_rest, 1)
                for k in range(KT):
                    dve.wait_ge(w_high, k + 2)
                    dve.tensor_tensor(wl[:, k], w[:, k], as_f32(wh[:, k]), ALU.subtract).then_inc(w_rest, 1)
                    if k == 3:
                        dve.wait_ge(tab_in, 32)
                        dve.wait_ge(made, 1)
                        rotate(dve, own, kr[:], bank[KR][:], cos, sin, tmp[:])
                        dve.sem_inc(keyed, 1)
                rsqrt_newton(dve, own, rooted, 1, ss, root, y, t1, WIDTHS)
                scale(dve, range(HALF), lambda o, i, s: dve.tensor_scalar(o, i, s, None, ALU.mult)).then_inc(scaled, 1)
                for k in range(LK):
                    dve.wait_ge(c_high, k + 1)
                    dve.scalar_tensor_tensor(out=c[1][:, k], in0=bank[k][:], scalar=gcol[:, k:k + 1], in1=as_f32(c[0][:, k]),
                                             op0=ALU.mult, op1=ALU.subtract)


def mla_heads(nc, K, W, rest, heads_in, c, cos, sin, qT, qr, kT, v, limit):
    QK_, VK = Q_LORA // P, KV_LORA // P
    R = H_A * ROPE // P
    with Stage(nc, "odh") as st:
        H = {n: st.sb(f"high_{n}", [P, QK_ if n in "qr" else VK, H_A * ROPE if n == "r" else H_A * P], F32R) for n in "qrkv"}
        tmp = st.sb("tmp", [P, 2, T])
        assert nc.sbuf_base <= limit
        bank = st.banks(8)
        w_high, w_rest, made, by_act, by_dve, step = (st.sem(n) for n in ("w_high", "w_rest", "made", "by_act", "by_dve", "step"))
        tiles = [(n, k) for n in "qrkv" for k in range(H[n].shape[1])]
        order = [("q", h) for h in range(H_A)] + [("r", r) for r in range(R)] + [("k", h) for h in range(H_A)] + [("v", n) for n in range(BLOCKS)]
        readers = []
        for kind, i in order:
            readers.append((by_dve, i + 1) if kind == "r" else (by_act, i + 1 + H_A * "qkv".index(kind)))
        with nc.Block() as block:
            @block.tensor
            def _(pe):
                def product(n, k):
                    kind, i = order[n]
                    ks = H[kind].shape[1]
                    kc = k if kind in "qr" else QK_ + k
                    if kind == "v":
                        tok, half = slice(i // 2 * P, (i // 2 + 1) * P), slice(i % 2 * 512, (i % 2 + 1) * 512)
                        a, b = (c[0][:, kc, tok], c[1][:, kc, tok]), (H["v"][:, k, half], rest["v"][:, k, half])
                    else:
                        cols = slice(i * P, (i + 1) * P)
                        a, b = (H[kind][:, k, cols], rest[kind][:, k, cols]), (c[0][:, kc], c[1][:, kc])
                    last = split_product(pe, bank[n % 8][:], a, b, k == 0, k == ks - 1)
                    if k == ks - 1:
                        last.then_inc(made, 1)

                for k in range(QK_):
                    pe.wait_ge(w_rest, k + 1)
                    for h in range(H_A):
                        product(h, k)
                for n in range(H_A, len(order)):
                    kind, i = order[n]
                    pe.wait_ge(*readers[n - 8])
                    if i == 0:
                        pe.wait_ge(w_rest, tiles.index((kind, H[kind].shape[1] - 1)) + 1)
                    for k in range(H[kind].shape[1]):
                        product(n, k)

            @block.scalar
            def _(act):
                act.wait_ge(heads_in, 64)
                for n, k in tiles:
                    act.activation(H[n][:, k], W[n][:, k], ACT.Copy).then_inc(w_high, 1)
                for n, (kind, i) in enumerate(order):
                    if kind == "r":
                        continue
                    act.wait_ge(made, n + 1)
                    dst = {"q": qT[:, i], "k": kT[:, i], "v": v[:, i // 2, i % 2 * 512:(i % 2 + 1) * 512]}[kind]
                    act.activation(dst, bank[n % 8][:], ACT.Copy).then_inc(by_act, 1)

            @block.vector
            def _(dve):
                own = Chain(dve, step)
                for m, (n, k) in enumerate(tiles):
                    dve.wait_ge(w_high, m + 1)
                    dve.tensor_tensor(rest[n][:, k], W[n][:, k], as_f32(H[n][:, k]), ALU.subtract).then_inc(w_rest, 1)
                for r in range(R):
                    n = H_A + r
                    dve.wait_ge(made, n + 1)
                    rotate(dve, own, qr[:, r], bank[n % 8][:], cos, sin, tmp[:, r % 2])
                    dve.sem_inc(by_dve, 1)


def mla_attend(nc, K, qT, qr, kT, kr, v, o, w_out):
    N = H_A * TT
    with Stage(nc, "oda") as st:
        prob = st.sb("prob", [P, 2, T])
        pT = st.sb("pT", [P, 2, T])
        mask = st.sb("mask", [P, P])
        top, sums, inv = st.sb("top", [P, N]), st.sb("sums", [P, N]), st.sb("inv", [P, N])
        bank = st.banks(8)
        masked, scored, hidden, reduced, maxed, expd, inverted, normed = (
            st.sem(n) for n in ("masked", "scored", "hidden", "reduced", "maxed", "expd", "inverted", "normed"))
        turned, copied, summed, stored, zeroed = (st.sem(n) for n in ("turned", "copied", "summed", "stored", "zeroed"))
        stored_high = st.sem("stored_high")
        items = [(h, c) for h in range(H_A) for c in range(TT)]
        oh, ol = o
        assert nc.sbuf_base <= w_out.bottom

        with nc.Block() as block:
            @block.sync
            def _(sp):
                w_out.load(sp)

            @block.gpsimd
            def _(pool):
                pool.memset(mask[:], 0.0).then_inc(zeroed, 1)
                pool.wait_ge(zeroed, 1)
                pool.affine_select(out=mask[:], in_=mask[:], compare_op=ALU.is_ge, fill=NEG, base=0,
                                   pattern=[[-1, P]], channel_multiplier=1).then_inc(masked, 1)
                for k in range(KT):
                    w_out.take_rest(pool, k)

            @block.tensor
            def _(pe):
                def score(n):
                    h, c = items[n]
                    if n >= 3:
                        pe.wait_ge(expd, n - 2)
                    keys, half = (c + 1) * P, h % 2 * ROPE
                    pe.matmul(bank[n % 3][:, 0:keys], qT[:, h, c * P:keys], kT[:, h, 0:keys], start=True, stop=False)
                    pe.matmul(bank[n % 3][:, 0:keys], qr[half:half + ROPE, h // 2, c * P:keys], kr[half:half + ROPE, 0:keys],
                              start=False, stop=True).then_inc(scored, 1)

                def turn(n):
                    h, c = items[n]
                    pe.wait_ge(normed, n + 1)
                    if n >= 3:
                        pe.wait_ge(copied, n - 2)
                    for k in range(c + 1):
                        last = pe.transpose(bank[3 + n % 3][:, k * P:(k + 1) * P], prob[:, n % 2, k * P:(k + 1) * P], K["ident"][:])
                    last.then_inc(turned, 1)

                def weigh(n):
                    h, c = items[n]
                    pe.wait_ge(copied, n + 1)
                    if c == 0 and h >= 2:
                        pe.wait_ge(stored, h - 1)
                    for k in range(c + 1):
                        last = pe.matmul(bank[6 + h % 2][:, c * P:(c + 1) * P], v[:, k, h * V_D:(h + 1) * V_D],
                                         pT[:, n % 2, k * P:(k + 1) * P], start=(k == 0), stop=(k == c))
                    last.then_inc(summed, 1)

                for n in range(N + 3):
                    if n < N:
                        score(n)
                    if 0 <= n - 2 < N:
                        turn(n - 2)
                    if 0 <= n - 3 < N:
                        weigh(n - 3)

            @block.vector
            def _(dve):
                dve.wait_ge(masked, 1)

                def top_of(n):
                    h, c = items[n]
                    dve.wait_ge(scored, n + 1)
                    diag = bank[n % 3][:, c * P:(c + 1) * P]
                    dve.tensor_tensor(diag, diag, mask[:], ALU.add).then_inc(hidden, 1)
                    dve.wait_ge(hidden, n + 1)
                    dve.tensor_reduce(top[:, n:n + 1], bank[n % 3][:, 0:(c + 1) * P], AX.X, ALU.max).then_inc(reduced, 1)
                    dve.wait_ge(reduced, n + 1)
                    dve.tensor_scalar(top[:, n:n + 1], top[:, n:n + 1], -A_SCALE, None, ALU.mult).then_inc(maxed, 1)

                def norm(n):
                    h, c = items[n]
                    dve.wait_ge(expd, n + 1)
                    dve.reciprocal(inv[:, n:n + 1], sums[:, n:n + 1]).then_inc(inverted, 1)
                    dve.wait_ge(inverted, n + 1)
                    pr = prob[:, n % 2, 0:(c + 1) * P]
                    dve.tensor_scalar(pr, pr, inv[:, n:n + 1], None, ALU.mult).then_inc(normed, 1)

                def store_rest(h):
                    dve.wait_ge(stored_high, h + 1)
                    dve.tensor_tensor(ol[:, h], bank[6 + h % 2][:], as_f32(oh[:, h]), ALU.subtract).then_inc(stored, 1)

                for n in range(N + 4):
                    if n < N:
                        top_of(n)
                    if 1 <= n <= N:
                        norm(n - 1)
                    if n >= 4 and (n - 4) % TT == TT - 1:
                        store_rest((n - 4) // TT)

            @block.scalar
            def _(act):
                def exp_of(n):
                    h, c = items[n]
                    act.wait_ge(maxed, n + 1)
                    if n >= 2:
                        act.wait_ge(turned, n - 1)
                    act.activation(prob[:, n % 2, 0:(c + 1) * P], bank[n % 3][:, 0:(c + 1) * P], ACT.Exp, scale=A_SCALE,
                                   bias=top[:, n:n + 1], accum_out=sums[:, n:n + 1]).then_inc(expd, 1)

                def copy(n):
                    h, c = items[n]
                    act.wait_ge(turned, n + 1)
                    if n >= 2:
                        act.wait_ge(summed, n - 1)
                    act.activation(pT[:, n % 2, 0:(c + 1) * P], bank[3 + n % 3][:, 0:(c + 1) * P], ACT.Copy).then_inc(copied, 1)

                def store(h):
                    act.wait_ge(summed, TT * (h + 1))
                    act.activation(oh[:, h], bank[6 + h % 2][:], ACT.Copy).then_inc(stored_high, 1)

                for n in range(N + 4):
                    if n < N:
                        exp_of(n)
                    if 0 <= n - 2 < N:
                        copy(n - 2)
                    if n >= 4 and (n - 4) % TT == TT - 1:
                        store((n - 4) // TT)
                    if n > N // 2 and n % 2 and (n - N // 2) // 2 < KT:
                        w_out.copy_high(act, (n - N // 2) // 2)


def lay_out(a):
    a = {k: np.asarray(v) for k, v in a.items()}

    def rows(w):
        *lead, kp, n = w.shape
        return np.ascontiguousarray(np.moveaxis(w.reshape(*lead, kp // P, P, n), -3, -2))

    def cols(g):
        *lead, kp = g.shape
        return np.ascontiguousarray(np.swapaxes(g.reshape(*lead, kp // P, P), -1, -2))

    L = 2
    out = {"x": a["x"]}
    out["norm_mix_c"], out["norm_ffn_c"] = cols(a["norm_mix"]), cols(a["norm_ffn"])
    out["norm_final_r"] = a["norm_final"][None, :]
    w = rows(a["peer_w_q"])
    out["peer_wq_l"] = np.ascontiguousarray(np.moveaxis(w.reshape(L, P, KT, H_P, QD), 3, 1))
    out["peer_keys_l"] = np.ascontiguousarray(np.transpose(a["peer_keys"], (0, 1, 4, 2, 3)))
    u = a["peer_u"].reshape(L, KEYS, KEYS, KT, P)
    out["peer_u_l"] = np.ascontiguousarray(np.transpose(u, (0, 2, 4, 3, 1))).reshape(L, KEYS, P, D)
    out["peer_v_l"] = np.ascontiguousarray(np.swapaxes(a["peer_v"].reshape(L, KEYS, KEYS, D), 1, 2))
    w = rows(a["ev_w_in"][0])
    order = [2 * MIX, 3 * MIX, 0, MIX, 4 * MIX, 5 * MIX]
    out["ev_w_in_l"] = np.ascontiguousarray(np.stack([w[:, :, o:o + MIX] for o in order]))
    gates = np.zeros((P, KT, P), np.float32)
    gates[:, :, 0:H_E] = w[:, :, 6 * MIX:6 * MIX + H_E]
    gates[:, :, 32:32 + H_E] = w[:, :, 6 * MIX + H_E:6 * MIX + 2 * H_E]
    out["ev_w_gates_l"] = gates
    out["ev_bias_l"] = np.ascontiguousarray(np.stack([a["ev_i_bias"][0], a["ev_f_bias"][0]])[:, :, None])
    out["ev_conv_w_l"] = np.ascontiguousarray(np.transpose(a["ev_conv_w"][0].reshape(CONV, 2 * H_E, P), (2, 1, 0)))
    out["ev_conv_b_l"] = cols(a["ev_conv_b"][0])
    out["ev_gm_ws_l"] = np.ascontiguousarray(np.transpose(a["ev_gm_ws"][0], (2, 0, 1)))
    out["ev_gm_b_l"] = np.ascontiguousarray(a["ev_gm_b"][0].T)
    out["ev_gm_v_gain"], out["ev_h_gain"] = a["ev_gm_v_gain"], a["ev_h_gain"]
    out["ev_w_out_l"] = rows(a["ev_w_out"][0])
    w = rows(a["od_w_in"][0])
    LAT = Q_LORA + KV_LORA
    out["od_w_lat_l"] = np.ascontiguousarray(w[:, :, 0:LAT])
    kr = w[:, :, LAT:LAT + ROPE]
    out["od_w_kr_l"] = np.ascontiguousarray(np.concatenate([kr, kr], -1))
    out["od_gain_l"] = np.ascontiguousarray(np.concatenate([cols(a["od_q_gain"][0]), cols(a["od_kv_gain"][0])], -1))
    w = rows(a["od_w_uq"][0]).reshape(P, Q_LORA // P, H_A, NOPE + ROPE)
    out["od_w_uq_l"] = np.ascontiguousarray(w[..., :NOPE]).reshape(P, Q_LORA // P, H_A * NOPE)
    out["od_w_qr_l"] = np.ascontiguousarray(w[..., NOPE:]).reshape(P, Q_LORA // P, H_A * ROPE)
    w = rows(a["od_w_ukv"][0]).reshape(P, KV_LORA // P, H_A, NOPE + V_D)
    out["od_w_uk_l"] = np.ascontiguousarray(w[..., :NOPE]).reshape(P, KV_LORA // P, H_A * NOPE)
    out["od_w_uv_l"] = np.ascontiguousarray(w[..., NOPE:]).reshape(P, KV_LORA // P, H_A * V_D)
    out["od_w_out_l"] = rows(a["od_w_out"][0])
    half = ROPE // 2
    inv_freq = np.float32(10000.0) ** (-np.arange(half, dtype=np.float32) / np.float32(half))
    ang = inv_freq[:, None] * np.arange(T, dtype=np.float32)[None, :]
    cos, sin = np.cos(ang), np.sin(ang)
    out["cos_t"] = np.ascontiguousarray(np.concatenate([cos] * 4, 0))
    out["sin_t"] = np.ascontiguousarray(np.concatenate([sin, -sin] * 2, 0))
    return out


def program(nc, ins, out, stages="all"):
    SEMAPHORES.clear()
    with ExitStack() as ctx:
        def sb(name, shape, dt=F32):
            return ctx.enter_context(nc.sbuf_tensor(name, shape, dt))

        K = {"X": sb("X", [P, TT, D]), "ident": sb("ident", [P, P]), "iota": sb("iota", [P, KEYS]),
             "iota_i": sb("iota_i", [P, KEYS], I32), "sel": sb("sel", [H_E, H_E, P]),
             "eps": sb("eps", [P, 1]), "one": sb("one", [P, 1])}
        g_dram = nc.dram_tensor("gates", (KEYS, P, T), F32).ap()
        constants(nc, K, ins)
        if stages in ("all", "even"):
            even_mixer(nc, K, ins)
            clear_semaphores(nc)
        if stages in ("all", "peer0"):
            peer(nc, K, 0, ins, g_dram)
            clear_semaphores(nc)
        if stages in ("all", "mla"):
            mla_mixer(nc, K, ins)
            clear_semaphores(nc)
        if stages in ("all", "peer1"):
            peer(nc, K, 1, ins, g_dram)
        final_norm(nc, K, ins["norm_final_r"], out)


def kernel(**inputs):
    import concourse.bacc as bacc
    from concourse.bass_utils import run_bass_kernel_spmd

    arrays = {f"in_{n}": v for n, v in lay_out(inputs).items()}
    nc = bacc.Bacc("TRN2", target_bir_lowering=False, num_devices=1)
    ins = {n[3:]: nc.dram_tensor(n, v.shape, F32, kind="ExternalInput").ap() for n, v in arrays.items()}
    out = nc.dram_tensor("out", (1, T, D), F32, kind="ExternalOutput").ap()
    program(nc, ins, out)
    return run_bass_kernel_spmd(nc, [arrays], core_ids=[0]).results[0]["out"]
```

```python
from contextlib import ExitStack

import concourse.bass as bass
from concourse import mybir
import numpy as np

F32 = mybir.dt.float32
F32R = mybir.dt.float32r
BF16 = mybir.dt.bfloat16
U32 = mybir.dt.uint32
I32 = mybir.dt.int32
ALU = mybir.AluOpType
ACT = mybir.ActivationFunctionType
AX = mybir.AxisListType

P = 128
D = 1024
KT = D // P
T = 512
TT = T // P
EPS = 1e-6

G_N, G_D = 4, 128
H_E, D_E = 4, 128
MIX = G_N * G_D
CONV = 4

H_A, NOPE, ROPE, V_D = 8, 128, 64, 128
Q_LORA, KV_LORA = 512, 256
A_SCALE = float(np.float32((NOPE + ROPE) ** -0.5))

H_P, KEYS, TOPK, QD = 8, 128, 16, 256
PAIRS = H_P * TOPK
NEG = -3.0e38


def runs(lo, hi):
    out = []
    for a in range(TOPK):
        if hi(a) > lo(a):
            if out and out[-1][2:] == (lo(a), hi(a) - lo(a)):
                out[-1] = (out[-1][0], out[-1][1] + 1) + out[-1][2:]
            else:
                out.append((a, 1, lo(a), hi(a) - lo(a)))
    return out


STAIRS = runs(lambda a: 0, lambda a: TOPK // (a + 1))
EARLY = TOPK // 2
NEAR = runs(lambda a: 0, lambda a: EARLY // (a + 1))
FAR = runs(lambda a: EARLY // (a + 1), lambda a: TOPK // (a + 1))
CAND, CAND_NEAR = (sum(rows * w for _, rows, _, w in part) for part in (STAIRS, NEAR))
PICKS = ((0, EARLY, CAND_NEAR, 0), (EARLY, TOPK - EARLY, CAND, EARLY * CAND_NEAR))
PICK_WIDTH = sum(n * w for _, n, w, _ in PICKS)

GROUP = 4
N_GROUPS = KEYS // GROUP
BLOCKS = TT * 2


class Chain:

    def __init__(self, eng, sem, base=0):
        self.eng, self.sem, self.base, self.n = eng, sem, base, 0

    def mark(self, ins):
        self.n += 1
        ins.then_inc(self.sem, 1)

    def then(self, ins):
        self.mark(ins)
        self.eng.wait_ge(self.sem, self.base + self.n)

    def then_pass(self, ins, passed):
        self.then(ins)
        self.eng.sem_inc(passed, 1)


def split_product(pe, out, a, b, first, last):
    pe.matmul(out, a[0], b[0], start=first, stop=False)
    pe.matmul(out, a[0], b[1], start=False, stop=False)
    return pe.matmul(out, a[1], b[0], start=False, stop=last)


def as_f32(ap):
    return ap.bitcast(F32)


class Stage:

    def __init__(self, nc, name):
        self.nc, self.name, self.ctx = nc, name, ExitStack()

    def __enter__(self):
        self.ctx.__enter__()
        return self

    def __exit__(self, *a):
        return self.ctx.__exit__(*a)

    def sb(self, name, shape, dt=F32):
        return self.ctx.enter_context(self.nc.sbuf_tensor(f"{self.name}_{name}", shape, dt))

    def sb_split(self, name, shape):
        at = (self.nc.sbuf_base + 31) // 32 * 32
        return self.sb(name, shape), self.nc.alloc_sbuf_tensor_at(f"{self.name}_{name}_rest", shape, F32R, offset=at)

    def banks(self, n):
        return [self.ctx.enter_context(self.nc.psum_tensor(f"{self.name}_bank{i}", [P, 512], F32)) for i in range(n)]

    def sem(self, name):
        s = self.nc.alloc_semaphore(f"{self.name}_{name}")
        SEMAPHORES.append(s)
        return s


SEMAPHORES = []


def clear_semaphores(nc):
    with nc.Block() as block:
        @block.sync
        def _(sp):
            for s in SEMAPHORES:
                sp.sem_clear(s)
    for s in SEMAPHORES:
        nc.release_semaphore(s)
    SEMAPHORES.clear()


def constants(nc, K, ins):
    with Stage(nc, "const") as st:
        made = st.sem("made")
        K["x_in"] = [st.sem(f"x_in{c}") for c in range(TT)]
        with nc.Block() as block:
            @block.sync
            def _(sp):
                for c in range(TT):
                    sp.dma_start(K["X"][:, c], ins["x"][0, c * P:(c + 1) * P, :]).then_inc(K["x_in"][c], 16)

            @block.gpsimd
            def _(pool):
                pool.memset(K["ident"][:], 0.0)
                pool.memset(K["sel"][:], 0.0)
                pool.memset(K["eps"][:], EPS)
                pool.memset(K["one"][:], 1.0)
                pool.iota(K["iota_i"][:], [[1, KEYS]], base=0, channel_multiplier=0).then_inc(made, 1)
                pool.wait_ge(made, 1)
                pool.tensor_copy(K["iota"][:], K["iota_i"][:])
                pool.affine_select(out=K["ident"][:], in_=K["ident"][:], compare_op=ALU.not_equal, fill=1.0,
                                   base=0, pattern=[[-1, P]], channel_multiplier=1)
                pool.affine_select(out=K["sel"][:], in_=K["sel"][:], compare_op=ALU.not_equal, fill=1.0,
                                   base=0, pattern=[[-1, H_E], [0, P]], channel_multiplier=1).then_inc(made, 1)
                pool.wait_ge(made, 2)


def norm_transpose(nc, K, name, gain, split, ahead, high_beside=None, rest_beside=None):
    X, ident = K["X"], K["ident"]
    HALF = TT // 2
    x_in = K.pop("x_in", None)
    with Stage(nc, name) as st:
        sq = st.sb("sq", [P, 2, D])
        sq_dve = st.sb("sq_dve", [P, 2, D])
        xs = st.sb("xs", [P, TT, D])
        gcol = st.sb("gcol", [P, KT])
        ss, root, y, t1 = (st.sb(n, [P, TT]) for n in ("ss", "root", "y", "t1"))
        bank = st.banks(8)
        gain_in, squared, summed, rooted, step, scaled, scaled_act = (
            st.sem(n) for n in ("gain_in", "squared", "summed", "rooted", "step", "scaled", "scaled_act"))
        turned, high = st.sem("turned"), st.sem("high")
        with nc.Block() as block:
            @block.sync
            def _(sp):
                sp.dma_start(gcol[:], gain).then_inc(gain_in, 16)
                ahead(sp)

            @block.scalar
            def _(act):
                for c in range(HALF):
                    if x_in:
                        act.wait_ge(x_in[c], 16)
                    act.activation(sq[:, c], X[:, c], ACT.Square, accum_out=ss[:, c:c + 1]).then_inc(squared, 1)
                act.wait_ge(squared, HALF)
                act.wait_ge(summed, HALF)
                act.activation(root[:], ss[:], ACT.Sqrt, scale=1.0 / D, bias=K["eps"][:, 0:1]).then_inc(rooted, 1)
                act.wait_ge(step, 6)
                for c in range(HALF, TT):
                    act.activation(xs[:, c], X[:, c], ACT.Copy, scale=y[:, c:c + 1]).then_inc(scaled_act, 1)
                if high_beside:
                    high_beside(act)
                act.wait_ge(gain_in, 16)
                for k in range(KT):
                    act.wait_ge(turned, k + 1)
                    act.activation(split[0][:, k], bank[k][:], ACT.Copy, scale=gcol[:, k:k + 1]).then_inc(high, 1)

            @block.vector
            def _(dve):
                for c in range(HALF, TT):
                    if x_in:
                        dve.wait_ge(x_in[c], 16)
                    dve.tensor_tensor_reduce(sq_dve[:, c - HALF], X[:, c], X[:, c], 1.0, 0.0, ALU.mult, ALU.add,
                                             ss[:, c:c + 1]).then_inc(summed, 1)
                own = Chain(dve, step)
                dve.wait_ge(squared, HALF)
                rsqrt_newton(dve, own, rooted, 1, ss, root, y, t1, D)
                for c in range(HALF):
                    dve.tensor_scalar(xs[:, c], X[:, c], y[:, c:c + 1], None, ALU.mult).then_inc(scaled, 1)
                if rest_beside:
                    rest_beside(dve)
                dve.wait_ge(gain_in, 16)
                for k in range(KT):
                    dve.wait_ge(high, k + 1)
                    dve.scalar_tensor_tensor(out=split[1][:, k], in0=bank[k][:], scalar=gcol[:, k:k + 1],
                                             in1=as_f32(split[0][:, k]), op0=ALU.mult, op1=ALU.subtract)

            @block.tensor
            def _(pe):
                pe.wait_ge(scaled, HALF)
                pe.wait_ge(scaled_act, TT - HALF)
                for k in range(KT):
                    for c in range(TT):
                        last = pe.transpose(bank[k][:, c * P:(c + 1) * P], xs[:, c, k * P:(k + 1) * P], ident[:])
                    last.then_inc(turned, 1)


class OutputWeights:

    def __init__(self, nc, st, name, src, top):
        self.src = src
        self.bottom = top - 2 * KT * D * 4
        size = KT * D * 4
        self.raw, rest, high = (nc.alloc_sbuf_tensor_at(f"{name}_w_out_{n}", [P, KT, D], dt, offset=top - off)
                                for n, dt, off in (("raw", F32, size), ("rest", F32R, size), ("high", F32R, 2 * size)))
        self.split = (high, rest)
        self.loaded = [st.sem(f"w_out_in{n}") for n in range(2)]
        self.copied = st.sem("w_out_high")

    def load(self, sp):
        half = KT // 2
        for n in range(2):
            ks = slice(n * half, (n + 1) * half)
            sp.dma_start(self.raw[:, ks], self.src[:, ks]).then_inc(self.loaded[n], 16)

    def copy_high(self, act, k):
        act.wait_ge(self.loaded[k // (KT // 2)], 16)
        act.activation(self.split[0][:, k], self.raw[:, k], ACT.Copy).then_inc(self.copied, 1)

    def take_rest(self, pool, k):
        pool.wait_ge(self.copied, k + 1)
        high, rest = self.split
        pool.tensor_tensor(rest[:, k], self.raw[:, k], as_f32(high[:, k]), ALU.subtract)


def project_out(nc, K, name, w, cat=None, split=None):
    X, ident = K["X"], K["ident"]
    wh, wl = w
    turn = cat is not None
    with Stage(nc, name) as st:
        ch, cl = split or (st.sb("ch", [P, KT, T], F32R), st.sb("cl", [P, KT, T], F32R))
        bank = st.banks(8)
        turned, c_high, c_rest, made = (st.sem(n) for n in ("turned", "c_high", "c_rest", "made"))

        with nc.Block() as block:
            @block.tensor
            def _(pe):
                if turn:
                    for k in range(KT):
                        for c in range(TT):
                            last = pe.transpose(bank[k][:, c * P:(c + 1) * P], cat[:, c, k * P:(k + 1) * P], ident[:])
                        last.then_inc(turned, 1)
                for b in range(BLOCKS):
                    tok, col = slice(b // 2 * P, (b // 2 + 1) * P), slice(b % 2 * 512, (b % 2 + 1) * 512)
                    for k in range(KT):
                        if turn and b == 0:
                            pe.wait_ge(c_rest, k + 1)
                        last = split_product(pe, bank[b][:], (ch[:, k, tok], cl[:, k, tok]), (wh[:, k, col], wl[:, k, col]),
                                             k == 0, k == KT - 1)
                    last.then_inc(made, 1)

            @block.scalar
            def _(act):
                if turn:
                    for k in range(KT):
                        act.wait_ge(turned, k + 1)
                        act.activation(ch[:, k], bank[k][:], ACT.Copy).then_inc(c_high, 1)

            @block.vector
            def _(dve):
                if turn:
                    for k in range(KT):
                        dve.wait_ge(c_high, k + 1)
                        dve.tensor_tensor(cl[:, k], bank[k][:], as_f32(ch[:, k]), ALU.subtract).then_inc(c_rest, 1)
                for b in range(BLOCKS):
                    xb = X[:, b // 2, b % 2 * 512:(b % 2 + 1) * 512]
                    dve.wait_ge(made, b + 1)
                    dve.tensor_tensor(xb, xb, bank[b][:], ALU.add)



def load_head(sp, buf, ins, h):
    sp.dma_start(buf["wq"][:, h % 2], ins["wq"][h]).then_inc(buf["w_in"][h % 2], 16)
    sp.dma_start(buf["keys"][:, h % 2], ins["keys"][h]).then_inc(buf["k_in"][h % 2], 16)


def copy_high(act, buf, u, h):
    act.wait_ge(buf["w_in"][u], h * 8 + (16 - 8 * u))
    for half in range(2):
        ks = slice(half * KT // 2, (half + 1) * KT // 2)
        act.activation(buf["wq_high"][:, u, ks], buf["wq"][:, u, ks], ACT.Copy).then_inc(buf["w_high"], 1)


def peer_retrieve(nc, K, name, buf, ins, x, pair_i, pair_j, pair_g, limit):
    ident = K["ident"]
    M = 2 * TT
    wq, keys, w_in, k_in = buf["wq"], buf["keys"], buf["w_in"], buf["k_in"]
    with Stage(nc, name) as st:
        wq_high, wq_rest, w_high = buf["wq_high"], buf["wq_rest"], buf["w_high"]
        qT = st.sb("qT", [P, 2, 2, T])
        S = st.sb("S", [P, 2, M, KEYS])
        S2 = st.sb("S2", [P, M, KEYS])
        top = st.sb("top", [P, M, TOPK])
        top_u = st.sb("top_u", [P, M, TOPK], U32)
        top_n = st.sb("top_n", [P, 2, M, TOPK])
        cand = st.sb("cand", [P, TT, CAND])
        cand2 = st.sb("cand2", [P, TT, CAND])
        code = st.sb("code", [P, 2, TT, CAND])
        best = st.sb("best", [P, TT, TOPK])
        at_u = st.sb("at_u", [P, TT, TOPK], U32)
        at = st.sb("at", [P, 2, TT, TOPK])
        apart = st.sb("apart", [P, 2, TT, PICK_WIDTH], BF16)
        picked = st.sb("picked", [P, 2, TT, PICK_WIDTH])
        place = st.sb("place", [P, CAND])
        val = st.sb("val", [P, TT, H_P, TOPK])
        cod = st.sb("cod", [P, TT, H_P, TOPK])
        big = st.sb("big", [P, TT, H_P, TOPK])
        num = st.sb("num", [P, TT, H_P])
        ci = st.sb("ci", [P, TT, PAIRS], I32)
        cj = st.sb("cj", [P, TT, PAIRS], I32)
        assert nc.sbuf_base <= limit, "the pair tables would be overwritten"
        bank = st.banks(8)
        q_made, q_out, s_made, s_out = (st.sem(n) for n in ("q_made", "q_out", "s_made", "s_out"))
        q_free, s_free, ranked = (st.sem(n) for n in ("q_free", "s_free", "ranked"))
        step, passed, placed, expd, ready, turned, spread = (st.sem(n) for n in ("step", "passed", "placed", "expd", "ready", "turned", "spread"))
        rest_first, rest_second, compared = (st.sem(n) for n in ("rest_first", "rest_second", "compared"))
        numbered, located, coded, parted, absed, marked, chosen = (
            st.sem(n) for n in ("numbered", "located", "coded", "parted", "absed", "marked", "chosen"))

        def part_of(buffer, u, pick):
            _, n, w, o = pick
            return buffer[:, u, :, o:o + n * w].rearrange("p c (k n) -> p c k n", k=n)

        def wide_place(pick):
            _, n, w, _ = pick
            return place[:, 0:w].unsqueeze(1).unsqueeze(1).to_broadcast([P, TT, n, w])

        def wide_at(u, pick):
            k, n, w, _ = pick
            return at[:, u, :, k:k + n].unsqueeze(3).to_broadcast([P, TT, n, w])

        def wide_code(u, pick):
            _, n, w, _ = pick
            return code[:, u, :, 0:w].unsqueeze(2).to_broadcast([P, TT, n, w])

        def sum_picked(dve, u, h, picks=PICKS):
            for pick in picks:
                k, n = pick[:2]
                last = dve.tensor_reduce(cod[:, :, bass.ds(h, 1), k:k + n].rearrange("p c a k -> p c (a k)"),
                                         part_of(picked, u, pick), AX.X, ALU.add)
            return last

        def sums(eng, dst, src, stairs):
            o = 0
            for a, rows, b, w in stairs:
                last = eng.tensor_tensor(
                    dst[:, :, o:o + rows * w].rearrange("p c (a b) -> p c a b", a=rows),
                    src[:, 0:TT, a:a + rows].unsqueeze(3).to_broadcast([P, TT, rows, w]),
                    src[:, TT:M, b:b + w].unsqueeze(2).to_broadcast([P, TT, rows, w]), ALU.add)
                o += rows * w
            return last

        def take_rest(eng, u, h, first, last, done):
            ks = slice(first * KT // 2, (last + 1) * KT // 2)
            eng.wait_ge(w_high, h * 2 + (1 + last))
            eng.tensor_tensor(wq_rest[:, u, ks], wq[:, u, ks], as_f32(wq_high[:, u, ks]), ALU.subtract).then_inc(done, 1)

        with nc.Block() as block:
            @block.sync
            def _(sp):
                sp.dma_start(place[:], ins["place"].to_broadcast([P, CAND])).then_inc(placed, 16)
                with sp.Fori(1, H_P // 2) as i:
                    for u in range(2):
                        h = sp.snap(i * 2 + u)
                        sp.wait_ge(q_made, i * 2 + (u - 1))
                        sp.dma_start(wq[:, u], ins["wq"][bass.ds(h, 1)].rearrange("a p k q -> p (a k) q")).then_inc(w_in[u], 16)
                        sp.wait_ge(s_made, i * 2 + (u - 1))
                        sp.dma_start(keys[:, u], ins["keys"][bass.ds(h, 1)].rearrange("a p s n -> p (a s) n")).then_inc(k_in[u], 16)

            @block.gpsimd
            def _(pool):
                pool.wait_ge(placed, 16)

                def number(u, h):
                    pool.wait_ge(numbered, h + 1)
                    if not isinstance(h, int) or h >= 2:
                        pool.wait_ge(chosen, h - 1)
                    sums(pool, code[:, u], top_n[:, u], NEAR + FAR).then_inc(coded, 1)

                def part(u, h):
                    pool.wait_ge(located, h + 1)
                    for pick in PICKS:
                        last = pool.tensor_tensor(part_of(apart, u, pick), wide_place(pick), wide_at(u, pick), ALU.subtract)
                    last.then_inc(parted, 1)

                def choose(u, h):
                    pool.wait_ge(marked, h + 1)
                    pool.wait_ge(coded, h + 1)
                    for pick in PICKS:
                        last = pool.tensor_tensor(part_of(picked, u, pick), part_of(apart, u, pick), wide_code(u, pick), ALU.mult)
                    last.then_inc(chosen, 1)

                take_rest(pool, 1, 1, 1, 1, rest_second)
                take_rest(pool, 0, 2, 0, 1, rest_second)
                number(0, 0)
                part(0, 0)
                take_rest(pool, 1, 3, 0, 1, rest_second)
                number(1, 1)
                part(1, 1)
                choose(0, 0)
                with pool.Fori(1, H_P // 2 - 1) as i:
                    for u in range(2):
                        take_rest(pool, u, i * 2 + (u + 2), 0, 1, rest_second)
                        number(u, i * 2 + u)
                        part(u, i * 2 + u)
                        choose(1 - u, i * 2 + (u - 1))
                number(0, H_P - 2)
                part(0, H_P - 2)
                choose(1, H_P - 3)
                number(1, H_P - 1)
                choose(0, H_P - 2)
                late = part_of(picked, 1, PICKS[1])
                pool.wait_ge(coded, H_P)
                pool.wait_ge(compared, 1)
                pool.tensor_tensor(late, late, wide_code(1, PICKS[1]), ALU.mult).then_inc(chosen, 1)

            @block.tensor
            def _(pe):
                def query(u, h):
                    if not isinstance(h, int):
                        pe.wait_ge(rest_second, h)
                    elif h:
                        pe.wait_ge(rest_first, 1)
                    pe.wait_ge(q_free, h + 1)
                    for s in range(2):
                        for k in range(KT):
                            if isinstance(h, int) and h and s == 0 and k == KT // 2:
                                pe.wait_ge(rest_second, 1)
                            w = (slice(None), u, k, slice(s * P, (s + 1) * P))
                            last = split_product(pe, bank[2 * u + s][:], (wq_high[w], wq_rest[w]), (x[0][:, k], x[1][:, k]),
                                                 k == 0, k == KT - 1)
                    last.then_inc(q_made, 1)

                def scores(u, h):
                    pe.wait_ge(k_in[u], h * 8 + (16 - 8 * u))
                    pe.wait_ge(q_out, h + 1)
                    pe.wait_ge(s_free, h + 1)
                    for s in range(2):
                        for c in range(TT):
                            last = pe.matmul(bank[4 + 2 * u + s][:, c * P:(c + 1) * P],
                                             qT[:, u, s, c * P:(c + 1) * P], keys[:, u, s], start=True, stop=True)
                    last.then_inc(s_made, 1)

                for h in range(2):
                    query(h, h)
                    scores(h, h)
                with pe.Fori(1, H_P // 2) as i:
                    for u in range(2):
                        query(u, i * 2 + u)
                        scores(u, i * 2 + u)
                for n, src in enumerate((K["tab_g"], K["tab_i"], K["tab_j"])):
                    pe.wait_ge(ready, n + 1)
                    for c in range(TT):
                        last = pe.transpose(bank[n][:, c * P:(c + 1) * P], src[:, c], ident[:])
                    last.then_inc(turned, 1)

            @block.scalar
            def _(act):
                act.sem_inc(q_free, 2)
                act.sem_inc(s_free, 2)

                def query(u, h):
                    act.wait_ge(q_made, h + 1)
                    act.activation(qT[:, u, 0], bank[2 * u][:], ACT.Copy)
                    act.activation(qT[:, u, 1], bank[2 * u + 1][:], ACT.Copy).then_inc(q_out, 1)
                    act.wait_ge(q_out, h + 1)
                    act.sem_inc(q_free, 1)

                def scores(u, h):
                    act.wait_ge(s_made, h + 1)
                    act.wait_ge(ranked, h + 1)
                    act.activation(S[:, u, 0:TT], bank[4 + 2 * u][:].rearrange("p (c n) -> p c n", c=TT), ACT.Copy)
                    act.activation(S[:, u, TT:M], bank[5 + 2 * u][:].rearrange("p (c n) -> p c n", c=TT),
                                   ACT.Copy).then_inc(s_out, 1)
                    act.wait_ge(s_out, h + 1)
                    act.sem_inc(s_free, 1)

                def mark(u, h):
                    act.wait_ge(parted, h + 1)
                    act.activation(apart[:, u], apart[:, u], ACT.Abs).then_inc(absed, 1)
                    act.wait_ge(absed, h + 1)
                    act.activation(apart[:, u], apart[:, u], ACT.Relu, scale=-1.0, bias=K["one"][:, 0:1]).then_inc(marked, 1)

                def head(u, h):
                    if not isinstance(h, int) or h + 1 < H_P:
                        copy_high(act, buf, 1 - u, h + 1)
                    query(u, h)
                    scores(u, h)
                    if not isinstance(h, int) or h >= 2:
                        mark(u, h - 2)

                head(0, 0)
                head(1, 1)
                with act.Fori(1, H_P // 2 - 1) as i:
                    for u in range(2):
                        head(u, i * 2 + u)
                head(0, H_P - 2)
                head(1, H_P - 1)
                mark(0, H_P - 2)
                act.wait_ge(expd, 1)
                act.activation(big[:], big[:], ACT.Exp).then_inc(expd, 1)
                for n, dst in enumerate((pair_g, pair_i, pair_j)):
                    act.wait_ge(turned, n + 1)
                    act.activation(dst[:], bank[n][:], ACT.Copy).then_inc(spread, 1)

            @block.vector
            def _(dve):
                STEPS = 10
                dve.sem_inc(ranked, 2)
                take_rest(dve, 1, 1, 0, 0, rest_first)
                dve.wait_ge(placed, 16)

                def rank(u, h):
                    own = Chain(dve, step, h * STEPS)
                    dve.wait_ge(s_out, h + 1)
                    dve.sem_inc(passed, 1)
                    for m in range(M):
                        last = dve.max(top[:, m, 0:8], S[:, u, m])
                    own.then_pass(last, passed)
                    for m in range(M):
                        dve.match_replace(S2[:, m], top[:, m, 0:8], S[:, u, m], NEG)
                        last = dve.max_index(top_u[:, m, 0:8], top[:, m, 0:8], S[:, u, m])
                    own.then_pass(last, passed)
                    for m in range(M):
                        last = dve.max(top[:, m, 8:16], S2[:, m])
                    own.then_pass(last, passed)
                    for m in range(M):
                        last = dve.max_index(top_u[:, m, 8:16], top[:, m, 8:16], S2[:, m])
                    own.then(last)
                    dve.sem_inc(ranked, 1)
                    if not isinstance(h, int) or h >= 2:
                        dve.wait_ge(coded, h - 1)
                    dve.tensor_scalar(top_n[:, u, 0:TT], top_u[:, 0:TT], float(KEYS), None, ALU.mult)
                    dve.tensor_copy(top_n[:, u, TT:M], top_u[:, TT:M]).then_inc(numbered, 1)
                    own.then_pass(sums(dve, cand, top, STAIRS), passed)
                    for c in range(TT):
                        last = dve.max(best[:, c, 0:8], cand[:, c])
                    own.then_pass(last, passed)
                    for c in range(TT):
                        dve.match_replace(cand2[:, c], best[:, c, 0:8], cand[:, c], NEG)
                        last = dve.max_index(at_u[:, c, 0:8], best[:, c, 0:8], cand[:, c])
                    own.then_pass(last, passed)
                    for c in range(TT):
                        last = dve.max(best[:, c, 8:16], cand2[:, c])
                    own.then_pass(last, passed)
                    for c in range(TT):
                        last = dve.max_index(at_u[:, c, 8:16], best[:, c, 8:16], cand2[:, c])
                    own.then(last)
                    if not isinstance(h, int) or h >= 2:
                        dve.wait_ge(parted, h - 1)
                    dve.tensor_copy(at[:, u], at_u[:]).then_inc(located, 1)
                    own.then(dve.tensor_copy(val[:, :, bass.ds(h, 1)].rearrange("p c a k -> p c (a k)"), best[:]))
                    assert own.n == STEPS, own.n

                def gather(u, h):
                    dve.wait_ge(chosen, h + 1)
                    sum_picked(dve, u, h)

                rank(0, 0)
                rank(1, 1)
                with dve.Fori(0, H_P // 2 - 1) as i:
                    for u in range(2):
                        rank(u, i * 2 + (u + 2))
                        gather(u, i * 2 + u)
                own = Chain(dve, step, H_P * STEPS)
                own.then(dve.tensor_tensor(big[:], val[:], val[:, :, :, 0:1].to_broadcast([P, TT, H_P, TOPK]), ALU.subtract))
                dve.sem_inc(expd, 1)
                first = part_of(picked, 1, PICKS[0])
                dve.tensor_tensor(part_of(picked, 1, PICKS[1]), wide_place(PICKS[1]), wide_at(1, PICKS[1]), ALU.is_equal).then_inc(compared, 1)
                own.then(dve.tensor_tensor(first, wide_place(PICKS[0]), wide_at(1, PICKS[0]), ALU.is_equal))
                dve.wait_ge(coded, H_P)
                own.then(dve.tensor_tensor(first, first, wide_code(1, PICKS[0]), ALU.mult))
                sum_picked(dve, 1, H_P - 1, PICKS[:1])
                dve.wait_ge(expd, 2)
                own.then(dve.tensor_reduce(num[:], big[:], AX.X, ALU.add))
                own.then(dve.reciprocal(num[:], num[:]))
                own.then(dve.tensor_tensor(K["tab_g"][:].rearrange("p c (h k) -> p c h k", h=H_P), big[:],
                                           num[:].unsqueeze(3).to_broadcast([P, TT, H_P, TOPK]), ALU.mult))
                dve.sem_inc(ready, 1)
                dve.wait_ge(chosen, H_P - 1)
                sum_picked(dve, 0, H_P - 2)
                dve.wait_ge(chosen, H_P)
                own.then(sum_picked(dve, 1, H_P - 1, PICKS[1:]))
                codf = cod[:].rearrange("p c h k -> p c (h k)")
                own.then(dve.tensor_copy(ci[:], codf))
                own.then(dve.tensor_scalar(cj[:], ci[:], 7, None, ALU.arith_shift_right))
                own.then(dve.tensor_copy(K["tab_i"][:], cj[:]))
                dve.sem_inc(ready, 1)
                own.then(dve.scalar_tensor_tensor(out=K["tab_j"][:], in0=K["tab_i"][:], scalar=-float(KEYS), in1=codf,
                                                  op0=ALU.mult, op1=ALU.add))
                dve.sem_inc(ready, 1)


def peer_mix(nc, K, name, u_dram, v_dram, g_dram, xh, xl, arena, pair_i, pair_j, pair_g, final):
    X = K["X"]
    BT = 4
    SLOTS = 4
    NB = P // BT
    ROUNDS = NB // SLOTS
    BY_DVE = BT - 1
    MARK_AHEAD = 2
    iota = K["iota"]
    KB = 1024
    with Stage(nc, name) as st:
        st.sb("arena", [P, 152 * KB // 4])

        def at(n, shape, kb, dt=F32):
            return nc.alloc_sbuf_tensor_at(f"{name}_{n}", shape, dt, offset=arena + kb * KB)

        G = [at(f"G{b}", [P, KEYS, P], 64 * b) for b in range(2)]
        hot_i, hot_j = at("hot_i", [P, SLOTS, BT, KEYS], 128), at("hot_j", [P, SLOTS, BT, KEYS], 136)
        u_raw, v_raw = at("u_raw", [P, GROUP, D], 0), at("v_raw", [P, GROUP, D], 16)
        uh, ul = at("uh", [P, GROUP, D], 32, F32R), at("ul", [P, GROUP, D], 48, F32R)
        gate, al = at("gate", [P, 2, GROUP, T], 64), at("al", [P, 2, GROUP, T], 80, F32R)
        vh, vl = at("vh", [P, GROUP, D], 96, F32R), at("vl", [P, GROUP, D], 112, F32R)
        FRONT = 2 * GROUP * T // P
        act_raw, ah = at("act_raw", [P, GROUP, T], 128), at("ah", [P, 2, GROUP, T], 136, F32R)
        bank = st.banks(8)
        hot, gated, spread, out, parted, marked = (st.sem(n) for n in ("hot", "gated", "spread", "out", "parted", "marked"))
        stored = [st.sem(f"stored{b}") for b in range(2)]
        stored_front = st.sem("stored_front")
        u_in = [st.sem(f"u_in{c}") for c in range(2)]
        v_in = [st.sem(f"v_in{c}") for c in range(2)]
        g_in = [st.sem(f"g_in{c}") for c in range(2)]
        u_high, u_rest, v_high, v_rest = (st.sem(n) for n in ("u_high", "u_rest", "v_high", "v_rest"))
        hidden, gelued, weighed, a_high, a_rest = (st.sem(n) for n in ("hidden", "gelued", "weighed", "a_high", "a_rest"))
        made, added = st.sem("made"), st.sem("added")
        xs, grow = at("xs", [P, TT, D], 96), at("grow", [P, D], 112)
        ss, root, y, t1 = (st.sb(n, [P, TT]) for n in ("ss", "root", "y", "t1"))
        gain_in, squared, rooted, step_done, normed, out_done = (
            st.sem(n) for n in ("gain_in", "squared", "rooted", "step_done", "normed", "out_done"))
        FIRST, LAST = 2, N_GROUPS - 4
        assert (LAST - FIRST) % 2 == 0

        def steps(eng, step):
            for g in range(-1, FIRST):
                step(g, g % 2)
            with eng.Fori(0, (LAST - FIRST) // 2) as i:
                for par in range(2):
                    step(i * 2 + (FIRST + par), par)
            for g in range(LAST, N_GROUPS):
                step(g, g % 2)

        LAST_GROUP = N_GROUPS - 1

        def v_place(g):
            return (uh, ul) if isinstance(g, int) and g == LAST_GROUP else (vh, vl)

        def splits_v(g):
            return not isinstance(g, int) or 0 < g < LAST_GROUP

        def has(g, ahead):
            return not isinstance(g, int) or 0 <= g + ahead < N_GROUPS

        with nc.Block() as block:
            @block.sync
            def _(sp):
                def rows(t, g, c):
                    return t[bass.ds(g * GROUP + 2 * c, 2)].rearrange("j p n -> p j n")

                def store(c, first, end, done):
                    sp.dma_start(g_dram[first:end].rearrange("j i t -> i j t")[:, :, c * P:(c + 1) * P],
                                 G[c % 2][:, first:end]).then_inc(done, 16)

                for c in range(TT):
                    if c == TT - 1:
                        sp.wait_ge(stored[0], 32)
                        for n in range(2):
                            sp.dma_start(u_raw[:, 2 * n:2 * n + 2], rows(u_dram, 0, n)).then_inc(u_in[n], 16)
                        for n in range(2):
                            sp.dma_start(v_raw[:, 2 * n:2 * n + 2], rows(v_dram, 0, n)).then_inc(v_in[n], 16)
                    sp.wait_ge(out, SLOTS + NB * (c + 1))
                    if c < TT - 1:
                        store(c, 0, KEYS, stored[c % 2])

                def load_gates(b):
                    sp.dma_start(gate[:, b], g_dram[b * GROUP:(b + 1) * GROUP].rearrange("j p n -> p j n")).then_inc(g_in[b], 16)

                store(TT - 1, 0, FRONT, stored_front)
                for c in range(2):
                    sp.wait_ge(u_rest, 2 * c + 2)
                    sp.dma_start(u_raw[:, 2 * c:2 * c + 2], rows(u_dram, 1, c)).then_inc(u_in[c], 16)
                sp.wait_ge(stored_front, 16)
                sp.wait_ge(stored[1], 16)
                load_gates(0)
                store(TT - 1, FRONT, 2 * FRONT, stored_front)
                load_gates(1)
                store(TT - 1, 2 * FRONT, KEYS, stored[1])

                def step(g, par):
                    vg, ug, gg = (sp.snap(g * GROUP + k * GROUP) if not isinstance(g, int) else g * GROUP + k * GROUP for k in (1, 3, 2))
                    for c in range(2):
                        if has(g, 1) and has(g, 0):
                            src = v_dram[bass.ds(vg + 2 * c, 2)].rearrange("j p n -> p j n")
                            sp.wait_ge(v_rest, g * GROUP + (2 * c + 2))
                            sp.dma_start(v_raw[:, 2 * c:2 * c + 2], src).then_inc(v_in[c], 16)
                        if has(g, 3):
                            src = u_dram[bass.ds(ug + 2 * c, 2)].rearrange("j p n -> p j n")
                            sp.wait_ge(u_rest, g * GROUP + (2 * GROUP + 2 * c + 2))
                            sp.dma_start(u_raw[:, 2 * c:2 * c + 2], src).then_inc(u_in[c], 16)
                    if isinstance(g, int) and g == 0:
                        sp.wait_ge(stored_front, 32)
                        sp.wait_ge(stored[1], 32)
                    if has(g, 2) and has(g, 0):
                        src = g_dram[bass.ds(gg, GROUP)].rearrange("j p n -> p j n")
                        sp.wait_ge(weighed, g * GROUP + GROUP)
                        sp.dma_start(gate[:, par], src).then_inc(g_in[par], 16)

                steps(sp, step)
                if final:
                    gain, dst = final
                    sp.wait_ge(made, LAST_GROUP * BLOCKS)
                    sp.dma_start(grow[:], gain.to_broadcast([P, D])).then_inc(gain_in, 16)
                    for c in range(TT):
                        sp.wait_ge(normed, c + 1)
                        sp.dma_start(dst[0, c * P:(c + 1) * P, :], xs[:, c]).then_inc(out_done, 16)
                    sp.wait_ge(out_done, 16 * TT)

            @block.gpsimd
            def _(pool):
                for c in range(TT):
                    with pool.Fori(0, ROUNDS) as i:
                        for u in range(SLOTS):
                            n0, t0 = c * NB + u, c * P + u * BT
                            pool.wait_ge(hot, i * (2 * SLOTS) + (2 * n0 + 1))
                            pool.tensor_tensor(hot_j[:, u], hot_j[:, u],
                                               pair_g[:, bass.ds(i * (SLOTS * BT) + t0, BT)].unsqueeze(2).to_broadcast([P, BT, KEYS]),
                                               ALU.mult).then_inc(gated, 1)

            @block.scalar
            def _(act):
                act.sem_inc(out, SLOTS)

                def part(u, n):
                    act.wait_ge(spread, n + 1)
                    act.activation(hot_i[:, u, BY_DVE], iota[:], ACT.Abs, scale=-1.0,
                                   bias=pair_i[:, bass.ds(n * BT + BY_DVE, 1)]).then_inc(parted, 1)

                def mark(u, n):
                    row = hot_i[:, u, BY_DVE]
                    act.wait_ge(parted, n + 1)
                    act.activation(row, row, ACT.Relu, scale=-1.0, bias=K["one"][:, 0:1]).then_inc(marked, 1)

                def copy_g(c, u, n, t):
                    act.wait_ge(spread, n + (SLOTS + 1))
                    act.activation(G[c % 2][:, :, bass.ds(t, BT)].rearrange("p j t -> p t j"),
                                   bank[u][:].rearrange("p (t j) -> p t j", t=BT), ACT.Copy).then_inc(out, 1)

                for n in range(MARK_AHEAD):
                    part(n, n)
                    mark(n, n)
                for c in range(TT):
                    if c >= 2:
                        act.wait_ge(stored[c % 2], 16)
                    with act.Fori(0, ROUNDS - (c == TT - 1)) as i:
                        for u in range(SLOTS):
                            ahead = ((u + MARK_AHEAD) % SLOTS, i * SLOTS + (c * NB + u + MARK_AHEAD))
                            part(*ahead)
                            copy_g(c, u, i * SLOTS + (c * NB + u), i * (SLOTS * BT) + u * BT)
                            mark(*ahead)
                for n in range(TT * NB - SLOTS, TT * NB):
                    if n + MARK_AHEAD < TT * NB:
                        part((n + MARK_AHEAD) % SLOTS, n + MARK_AHEAD)
                        mark((n + MARK_AHEAD) % SLOTS, n + MARK_AHEAD)
                    copy_g(TT - 1, n % SLOTS, n, n * BT - (TT - 1) * P)

                def copy_u(e, s, g):
                    act.wait_ge(u_in[s // 2], g * 16 + 16)
                    if not isinstance(g, int) or g > 0:
                        act.wait_ge(hidden, e - (GROUP - 1))
                    act.activation(uh[:, s], u_raw[:, s], ACT.Copy).then_inc(u_high, 1)

                for s in range(GROUP):
                    copy_u(s, s, 0)

                def copy_v(s, g):
                    act.wait_ge(v_in[s // 2], g * 16 + 16)
                    if isinstance(g, int) and g == LAST_GROUP:
                        act.wait_ge(hidden, N_GROUPS * GROUP)
                    elif not isinstance(g, int) or g > 0:
                        act.wait_ge(made, g * BLOCKS)
                    act.activation(v_place(g)[0][:, s], v_raw[:, s], ACT.Copy).then_inc(v_high, 1)

                def step(g, par):
                    if isinstance(g, int) and g == 0:
                        act.wait_ge(stored[1], 32)
                        for s in range(GROUP):
                            copy_v(s, 0)
                    for s in range(GROUP):
                        e = g * GROUP + s
                        if splits_v(g):
                            copy_v(s, g)
                        if has(g, 1):
                            act.wait_ge(hidden, e + (GROUP + 1))
                            if not isinstance(g, int) or g >= 0:
                                act.wait_ge(a_rest, e + 1)
                            act.activation(act_raw[:, s], bank[4 + s][:], ACT.Gelu_apprx_tanh).then_inc(gelued, 1)
                        if has(g, 2):
                            copy_u(e + 2 * GROUP, s, g + 2)
                        if has(g, 1):
                            act.wait_ge(weighed, e + (GROUP + 1))
                            if not isinstance(g, int) or g > 0:
                                act.wait_ge(made, g * BLOCKS)
                            act.activation(ah[:, 1 - par, s], act_raw[:, s], ACT.Copy).then_inc(a_high, 1)
                    if isinstance(g, int) and g == LAST_GROUP - 1:
                        for s in range(GROUP):
                            copy_v(s, LAST_GROUP)

                steps(act, step)
                if final:
                    for c in range(TT):
                        act.wait_ge(added, LAST_GROUP * BLOCKS + 2 * c + 2)
                        act.activation(xs[:, c], X[:, c], ACT.Square, accum_out=ss[:, c:c + 1]).then_inc(squared, 1)
                        act.wait_ge(squared, c + 1)
                        act.activation(root[:, c:c + 1], ss[:, c:c + 1], ACT.Sqrt, scale=1.0 / D, bias=K["eps"][:, 0:1]).then_inc(rooted, 1)

            @block.vector
            def _(dve):
                for c in range(TT):
                    with dve.Fori(0, ROUNDS) as i:
                        for u in range(SLOTS):
                            n0, t0 = c * NB + u, c * P + u * BT
                            dve.wait_ge(spread, i * SLOTS + (n0 + 1))
                            for rows, pair, tokens in ((hot_j, pair_j, BT), (hot_i, pair_i, BY_DVE)):
                                shape = [P, tokens, KEYS]
                                dve.tensor_tensor(rows[:, u, 0:tokens], iota[:].unsqueeze(1).to_broadcast(shape),
                                                  pair[:, bass.ds(i * (SLOTS * BT) + t0, tokens)].unsqueeze(2).to_broadcast(shape),
                                                  ALU.is_equal).then_inc(hot, 1)

                for s in range(GROUP):
                    dve.wait_ge(u_high, s + 1)
                    dve.tensor_tensor(ul[:, s], u_raw[:, s], uh[:, s].bitcast(F32), ALU.subtract).then_inc(u_rest, 1)

                own = Chain(dve, step_done)

                def norm_tile(c):
                    col = slice(c, c + 1)
                    rsqrt_newton(dve, own, rooted, c + 1, ss[:, col], root[:, col], y[:, col], t1[:, col], D)
                    if c == 0:
                        dve.wait_ge(gain_in, 16)
                    dve.scalar_tensor_tensor(out=xs[:, c], in0=X[:, c], scalar=y[:, col], in1=grow[:],
                                             op0=ALU.mult, op1=ALU.mult).then_inc(normed, 1)

                def rest_of_v(s, g):
                    high, rest = v_place(g)
                    dve.wait_ge(v_high, g * GROUP + (s + 1))
                    dve.tensor_tensor(rest[:, s], v_raw[:, s], as_f32(high[:, s]), ALU.subtract).then_inc(v_rest, 1)

                def step(g, par):
                    if isinstance(g, int) and g == 0:
                        for s in range(GROUP):
                            rest_of_v(s, 0)
                    for s in range(GROUP):
                        e = g * GROUP + s
                        if splits_v(g):
                            rest_of_v(s, g)
                        if has(g, 1):
                            dve.wait_ge(gelued, e + (GROUP + 1))
                            if s == 0:
                                if isinstance(g, int):
                                    dve.wait_ge(g_in[1 - par], 16 * ((g + 1) // 2 + 1))
                                else:
                                    dve.wait_ge(g_in[1 - par], (g + (2 + 1 - (1 - par))) * 8)
                            dve.tensor_tensor(act_raw[:, s], act_raw[:, s], gate[:, 1 - par, s], ALU.mult).then_inc(weighed, 1)
                        if has(g, 2):
                            dve.wait_ge(u_high, e + (2 * GROUP + 1))
                            dve.tensor_tensor(ul[:, s], u_raw[:, s], uh[:, s].bitcast(F32), ALU.subtract).then_inc(u_rest, 1)
                        if has(g, 1):
                            dve.wait_ge(a_high, e + (GROUP + 1))
                            if isinstance(g, int) and e == -GROUP:
                                dve.wait_ge(stored_front, 32)
                            dve.tensor_tensor(al[:, 1 - par, s], act_raw[:, s], ah[:, 1 - par, s].bitcast(F32),
                                              ALU.subtract).then_inc(a_rest, 1)
                    if isinstance(g, int) and g == LAST_GROUP - 1:
                        for s in range(GROUP):
                            rest_of_v(s, LAST_GROUP)
                    if has(g, 0):
                        for b in range(BLOCKS):
                            xb = X[:, b // 2, (b % 2) * 512:(b % 2 + 1) * 512]
                            dve.wait_ge(made, g * BLOCKS + (b + 1))
                            dve.tensor_tensor(xb, xb, bank[b % 4][:], ALU.add).then_inc(added, 1)
                            if final and isinstance(g, int) and g == LAST_GROUP and b % 2 and b > 1:
                                norm_tile(b // 2 - 1)

                steps(dve, step)
                if final:
                    norm_tile(TT - 1)

            @block.tensor
            def _(pe):
                pe.sem_inc(spread, SLOTS)
                for c in range(TT):
                    with pe.Fori(0, ROUNDS) as i:
                        for u in range(SLOTS):
                            n0 = c * NB + u
                            n = i * SLOTS + n0
                            pe.wait_ge(hot, i * (2 * SLOTS) + (2 * n0 + 2))
                            pe.wait_ge(gated, n + 1)
                            pe.wait_ge(out, n + 1)
                            for t in range(BT):
                                if t == BY_DVE:
                                    pe.wait_ge(marked, n + 1)
                                last = pe.matmul(bank[u][:, t * P:(t + 1) * P], hot_i[:, u, t], hot_j[:, u, t], start=True, stop=True)
                            last.then_inc(spread, 1)

                def step(g, par):
                    if has(g, 1):
                        for s in range(GROUP):
                            e = g * GROUP + (GROUP + s)
                            pe.wait_ge(u_rest, e + 1)
                            if not isinstance(g, int) or g >= 0:
                                pe.wait_ge(gelued, e - (GROUP - 1))
                            for k in range(KT):
                                hi, lo = uh[:, s, k * P:(k + 1) * P], ul[:, s, k * P:(k + 1) * P]
                                last = split_product(pe, bank[4 + s][:], (hi, lo), (xh[:, k], xl[:, k]), k == 0, k == KT - 1)
                            last.then_inc(hidden, 1)
                    if has(g, 0):
                        v = v_place(g)
                        pe.wait_ge(a_rest, g * GROUP + GROUP)
                        pe.wait_ge(v_rest, g * GROUP + GROUP)
                        for b in range(BLOCKS):
                            if not isinstance(g, int) or g * BLOCKS + b >= 4:
                                pe.wait_ge(added, g * BLOCKS + (b - 3))
                            tok, col = slice(b // 2 * P, (b // 2 + 1) * P), slice(b % 2 * 512, (b % 2 + 1) * 512)
                            for s in range(GROUP):
                                hi, lo = ah[:, par, s, tok], al[:, par, s, tok]
                                last = split_product(pe, bank[b % 4][:], (hi, lo), (v[0][:, s, col], v[1][:, s, col]), s == 0, s == GROUP - 1)
                            last.then_inc(made, 1)

                steps(pe, step)


def peer(nc, K, layer, ins, g_dram, final=None):
    name = f"peer{layer}"
    with Stage(nc, name) as st:
        xh, xl = st.sb("xh", [P, KT, T], F32R), st.sb("xl", [P, KT, T], F32R)
        arena = (nc.sbuf_base + 31) // 32 * 32
        pair_i, pair_j, pair_g = (
            nc.alloc_sbuf_tensor_at(f"{name}_{n}", [P, T], F32, offset=arena + (144 + 2 * i) * 1024)
            for i, n in enumerate(("pair_i", "pair_j", "pair_g")))
        with Stage(nc, name + "x") as sx:
            for n in ("tab_i", "tab_j", "tab_g"):
                K[n] = sx.sb(n, [P, TT, PAIRS])
            wq, wq_rest = sx.sb_split("wq", [P, 2, KT, QD])
            buf = {"wq": wq, "wq_rest": wq_rest, "wq_high": sx.sb("wq_high", [P, 2, KT, QD], F32R),
                   "w_high": sx.sem("w_high"), "keys": sx.sb("keys", [P, 2, 2, KEYS]),
                   "w_in": [sx.sem(f"w_in{b}") for b in range(2)], "k_in": [sx.sem(f"k_in{b}") for b in range(2)]}
            own = {"wq": ins["peer_wq_l"][layer], "keys": ins["peer_keys_l"][layer], "place": ins["place"]}

            def first_heads(sp):
                for h in range(2):
                    load_head(sp, buf, own, h)

            def rest_of_first(dve):
                dve.wait_ge(buf["w_high"], 2)
                dve.tensor_tensor(wq_rest[:, 0], wq[:, 0], as_f32(buf["wq_high"][:, 0]), ALU.subtract)

            norm_transpose(nc, K, name + "n", ins["norm_ffn_c"][layer], (xh, xl), first_heads,
                           lambda act: copy_high(act, buf, 0, 0), rest_of_first)
            peer_retrieve(nc, K, name + "r", buf, own, (xh, xl), pair_i, pair_j, pair_g,
                          limit=arena + 144 * 1024)
        peer_mix(nc, K, name + "e", ins["peer_u_l"][layer], ins["peer_v_l"][layer], g_dram, xh, xl,
                 arena, pair_i, pair_j, pair_g, final)




def even_mixer(nc, K, ins):
    with Stage(nc, "ev") as st:
        top = nc.sbuf_usable_end // 32 * 32 - TT * 2 * MIX * 4
        cat = nc.alloc_sbuf_tensor_at("ev_cat", [P, TT, 2 * MIX], F32, offset=top)
        w_out = OutputWeights(nc, st, "ev", ins["ev_w_out_l"], top)

        with Stage(nc, "evi") as si:
            B = {
                "u": si.sb("u", [P, TT, MIX]), "v": si.sb("v", [P, TT, MIX]),
                "qk": si.sb("qk", [P, 2 * H_E, T]),
                "v1": si.sb("v1", [P, TT, H_E, D_E + 1]),
                "og": si.sb("og", [P, TT, MIX]),
                "li": si.sb("li", [H_E, T]), "lf": si.sb("lf", [H_E, T]),
                "ws": si.sb("ws", [P, G_N, P]),
                "sb": si.sb("sb", [P, G_N]), "v_gain": si.sb("v_gain", [P, MIX]),
            }
            with Stage(nc, "evx") as sx:
                W = {"raw": sx.sb("w_raw", [P, KT, MIX]), "in": sx.sem("w_in")}
                xh, xl = sx.sb("xh", [P, KT, T], F32R), sx.sb("xl", [P, KT, T], F32R)
                norm_transpose(nc, K, "evn", ins["norm_mix_c"][0], (xh, xl),
                               lambda sp: sp.dma_start(W["raw"][:], ins["ev_w_in_l"][0]).then_inc(W["in"], 16))
                even_project(nc, K, ins, (xh, xl), W, B)
            even_gating(nc, K, ins, B, cat, w_out.load)
            with Stage(nc, "evw") as sw:
                wT = sw.sb("wT", [P, H_E, TT, P])
                col = sw.sb("col", [P, 4, TT, H_E])
                dec = sw.sb("dec", [P, H_E, TT])
                mlstm_gates(nc, K, B, wT, col, dec, w_out)
                mlstm_cells(nc, K, ins, B, wT, col, dec, cat, w_out)
        project_out(nc, K, "evo", w_out.split, cat=cat)


def even_project(nc, K, ins, x, W, B):
    QK = 2 * H_E
    ITEMS = QK + 1 + 4 * TT
    FQ = 32
    raw, w_in = W["raw"], W["in"]
    with Stage(nc, "evp") as st:
        wh, wl = st.sb("wh", [P, 2, KT, MIX], F32R), st.sb("wl", [P, 2, KT, MIX], F32R)
        gh = st.sb("gh", [P, KT, P], F32R)
        wg, gl = st.sb_split("wg", [P, KT, P])
        cw, cb = st.sb("cw", [P, QK, CONV]), st.sb("cb", [P, QK])
        bias = st.sb("bias", [P, 1])
        lin = st.sb("lin", [H_E, 3, T])
        bank = st.banks(8)
        NG = TT * G_N
        square = st.sb("square", [P, 2, G_D])
        ss, root, y, t1 = (st.sb(n, [P, NG]) for n in ("ss", "root", "y", "t1"))
        small_in, made, by_dve, by_act = (st.sem(n) for n in ("small_in", "made", "by_dve", "by_act"))
        ws_in, squared, rooted = (st.sem(n) for n in ("ws_in", "squared", "rooted"))
        w_high, w_rest, g_high, g_rest = (st.sem(n) for n in ("w_high", "w_rest", "g_high", "g_rest"))
        step, silued, fed, expd, logged = (st.sem(n) for n in ("step", "silued", "fed", "expd", "logged"))
        first_item = [0, 4] + [QK + 1 + n * TT for n in range(4)]

        with nc.Block() as block:
            @block.sync
            def _(sp):
                sp.dma_start(cw[:], ins["ev_conv_w_l"]).then_inc(small_in, 16)
                sp.dma_start(cb[:], ins["ev_conv_b_l"]).then_inc(small_in, 16)
                sp.dma_start(wg[:], ins["ev_w_gates_l"]).then_inc(small_in, 16)
                sp.dma_start(bias[0:H_E], ins["ev_bias_l"][0]).then_inc(small_in, 16)
                sp.dma_start(bias[FQ:FQ + H_E], ins["ev_bias_l"][1]).then_inc(small_in, 16)
                sp.dma_start(B["ws"][:], ins["ev_gm_ws_l"]).then_inc(ws_in, 16)
                sp.dma_start(B["sb"][:], ins["ev_gm_b_l"]).then_inc(small_in, 16)
                sp.dma_start(B["v_gain"][:], ins["ev_gm_v_gain"].to_broadcast([P, MIX])).then_inc(small_in, 16)
                for b in range(1, 6):
                    sp.wait_ge(w_rest, KT * b)
                    sp.dma_start(raw[:], ins["ev_w_in_l"][b]).then_inc(w_in, 16)

            @block.tensor
            def _(pe):
                for n in range(ITEMS):
                    if n >= 8:
                        if n - 8 <= QK:
                            pe.wait_ge(by_dve, n - 8 + 1)
                        else:
                            pe.wait_ge(by_act, n - 8 - QK)
                    if n == QK:
                        pe.wait_ge(g_rest, 1)
                    for k in range(KT):
                        flags = (k == 0, k == KT - 1)
                        xk = (x[0][:, k], x[1][:, k])
                        if n in first_item:
                            pe.wait_ge(w_rest, KT * first_item.index(n) + k + 1)
                        if n < QK:
                            s = (slice(None), n // 4, k, slice(n % 4 * P, (n % 4 + 1) * P))
                            last = split_product(pe, bank[n % 8][:], (wh[s], wl[s]), xk, *flags)
                        elif n == QK:
                            last = split_product(pe, bank[n % 8][:], (gh[:, k], gl[:, k]), xk, *flags)
                        else:
                            b, c = 2 + (n - QK - 1) // TT, (n - QK - 1) % TT
                            tok = slice(c * P, (c + 1) * P)
                            last = split_product(pe, bank[n % 8][:], (x[0][:, k, tok], x[1][:, k, tok]),
                                                 (wh[:, b % 2, k], wl[:, b % 2, k]), *flags)
                    last.then_inc(made, 1)

            def block_free(eng, b):
                if b >= 2:
                    eng.wait_ge(made, first_item[b - 1])

            @block.vector
            def _(dve):
                own = Chain(dve, step)
                qk = B["qk"]

                def rest(b):
                    for k in range(KT):
                        dve.wait_ge(w_high, KT * b + k + 1)
                        dve.tensor_tensor(wl[:, b % 2, k], raw[:, k], wh[:, b % 2, k].bitcast(F32), ALU.subtract).then_inc(w_rest, 1)

                def convolve(n):
                    z = bank[n % 8]
                    dve.wait_ge(made, n + 1)
                    own.then(dve.tensor_scalar(qk[:, n], z[:], cw[:, n, 3:4], cb[:, n:n + 1], ALU.mult, ALU.add))
                    for back in range(1, CONV):
                        tap = dve.scalar_tensor_tensor(out=qk[:, n, back:T], in0=z[:, 0:T - back], scalar=cw[:, n, 3 - back:4 - back],
                                                       in1=qk[:, n, back:T], op0=ALU.mult, op1=ALU.add)
                        if back < CONV - 1:
                            own.then(tap)
                        else:
                            tap.then_inc(by_dve, 1)

                rest(0)
                dve.wait_ge(small_in, 112)
                dve.wait_ge(g_high, 1)
                dve.tensor_tensor(gl[:], wg[:], as_f32(gh[:]), ALU.subtract).then_inc(g_rest, 1)
                rest(1)
                for n in range(QK):
                    convolve(n)
                    if n == 4:
                        rest(2)
                dve.wait_ge(made, QK + 1)
                gate = bank[QK % 8]
                dve.tensor_scalar(B["li"][:], gate[0:H_E, :], bias[0:H_E, 0:1], None, ALU.add)
                dve.tensor_scalar(lin[:, 0], gate[FQ:FQ + H_E, :], bias[FQ:FQ + H_E, 0:1], None, ALU.add).then_inc(by_dve, 1)
                dve.wait_ge(by_dve, QK + 1)
                rest(3)
                own.then(dve.tensor_scalar(lin[:, 1], lin[:, 0], -1.0, None, ALU.mult))
                own.then(dve.tensor_tensor(lin[:, 1], lin[:, 0], lin[:, 1], ALU.max))
                dve.sem_inc(fed, 1)
                dve.memset(B["v1"][:, :, :, D_E:D_E + 1], 1.0)
                own.then(dve.tensor_scalar(lin[:, 2], lin[:, 0], 0.0, None, ALU.min))
                for n in range(H_E):
                    dve.wait_ge(silued, n + 1)
                    dve.tensor_scalar(qk[:, n], qk[:, n], float(np.float32(D_E ** -0.5)), None, ALU.mult)
                rest(4)
                rest(5)
                rsqrt_newton(dve, own, rooted, 1, ss, root, y, t1, G_D)
                v = B["v"][:].rearrange("p c (g d) -> p (c g) d", g=G_N)
                own.then(dve.tensor_tensor(v, v, y[:].unsqueeze(2).to_broadcast([P, NG, G_D]), ALU.mult))
                own.then(dve.tensor_tensor(B["v"][:], B["v"][:], B["v_gain"][:].unsqueeze(1).to_broadcast([P, TT, MIX]), ALU.mult))
                dve.wait_ge(logged, 1)
                dve.tensor_tensor(B["lf"][:], lin[:, 2], lin[:, 1], ALU.subtract)

            @block.gpsimd
            def _(pool):
                pool.wait_ge(ws_in, 16)
                pool.affine_select(out=B["ws"][:], in_=B["ws"][:], compare_op=ALU.is_ge, fill=0.0, base=0,
                                   pattern=[[0, G_N], [1, P]], channel_multiplier=-1)

            @block.scalar
            def _(act):
                def high(b):
                    act.wait_ge(w_in, 16 * (b + 1))
                    block_free(act, b)
                    for k in range(KT):
                        act.activation(wh[:, b % 2, k], raw[:, k], ACT.Copy).then_inc(w_high, 1)

                high(0)
                act.wait_ge(small_in, 112)
                act.activation(gh[:], wg[:], ACT.Copy).then_inc(g_high, 1)
                high(1)
                high(2)
                for n in range(QK):
                    act.wait_ge(by_dve, n + 1)
                    act.activation(B["qk"][:, n], B["qk"][:, n], ACT.Silu).then_inc(silued, 1)
                high(3)
                for n in range(4 * TT):
                    b, c = n // TT, n % TT
                    act.wait_ge(made, QK + 1 + n + 1)
                    src = bank[(QK + 1 + n) % 8]
                    if b < 2:
                        done = act.activation(B["uv"[b]][:, c], src[:], ACT.Gelu_apprx_tanh)
                    elif b == 2:
                        done = act.activation(B["v1"][:, c, :, 0:D_E], src[:].rearrange("p (h d) -> p h d", h=H_E), ACT.Copy)
                    else:
                        done = act.activation(B["og"][:, c], src[:], ACT.Sigmoid)
                    done.then_inc(by_act, 1)
                    if b == 1:
                        act.wait_ge(by_act, n + 1)
                        for g in range(G_N):
                            m = c * G_N + g
                            if m >= 2:
                                act.wait_ge(squared, m - 1)
                            act.activation(square[:, m % 2], B["v"][:, c, g * G_D:(g + 1) * G_D], ACT.Square,
                                           accum_out=ss[:, m:m + 1]).then_inc(squared, 1)
                    if c == TT - 1 and b < 2:
                        high(4 + b)
                        if b == 1:
                            act.wait_ge(squared, NG)
                            act.activation(root[:], ss[:], ACT.Sqrt, scale=1.0 / G_D, bias=K["eps"][:, 0:1]).then_inc(rooted, 1)
                act.wait_ge(fed, 1)
                act.activation(lin[:, 1], lin[:, 1], ACT.Exp, scale=-1.0).then_inc(expd, 1)
                act.wait_ge(expd, 1)
                act.activation(lin[:, 1], lin[:, 1], ACT.Ln, bias=K["one"][0:H_E, 0:1]).then_inc(logged, 1)


def even_gating(nc, K, ins, B, cat, ahead):
    with Stage(nc, "evg") as st:
        bank = st.banks(4)
        made = st.sem("made")
        with nc.Block() as block:
            @block.sync
            def _(sp):
                ahead(sp)

            @block.vector
            def _(dve):
                for c in range(TT):
                    dve.wait_ge(made, c + 1)
                    for g in range(G_N):
                        ch = slice(g * G_D, (g + 1) * G_D)
                        dve.scalar_tensor_tensor(out=cat[:, c, ch], in0=bank[c][:, ch], scalar=B["sb"][:, g:g + 1],
                                                 in1=B["u"][:, c, ch], op0=ALU.add, op1=ALU.mult)

            @block.tensor
            def _(pe):
                for c in range(TT):
                    for g in range(G_N):
                        ch = slice(g * G_D, (g + 1) * G_D)
                        last = pe.matmul(bank[c][:, ch], B["ws"][:, g], B["v"][:, c, ch], start=True, stop=True)
                    last.then_inc(made, 1)


def rsqrt_newton(dve, own, rooted, count, ss, root, y, t1, width):
    widths = width if isinstance(width, list) else [(slice(None), width)]
    dve.wait_ge(rooted, count)
    own.then(dve.reciprocal(y[:], root[:]))
    for cols, w in widths:
        last = dve.tensor_scalar(ss[:, cols], ss[:, cols], 1.0 / w, EPS, ALU.mult, ALU.add)
    own.then(last)
    own.then(dve.tensor_tensor(t1[:], y[:], y[:], ALU.mult))
    own.then(dve.tensor_tensor(t1[:], t1[:], ss[:], ALU.mult))
    own.then(dve.tensor_scalar(t1[:], t1[:], -0.5, 1.5, ALU.mult, ALU.add))
    own.then(dve.tensor_tensor(y[:], y[:], t1[:], ALU.mult))


def mlstm_gates(nc, K, B, wT, col, dec, w_out):
    with Stage(nc, "evm") as st:
        ones = st.sb("ones", [H_E, P])
        b = st.sb("b", [H_E, TT, P])
        M = st.sb("M", [H_E, TT, P])
        row = st.sb("row", [H_E, 4, TT, P])
        m = st.sb("m", [H_E, TT + 1])
        dr = st.sb("dr", [H_E, TT])
        bank = st.banks(6)
        step, maxed, rowed, expd, turned, spread, colled, lagged, weighed = (
            st.sem(n) for n in ("step", "maxed", "rowed", "expd", "turned", "spread", "colled", "lagged", "weighed"))
        with nc.Block() as block:
            @block.vector
            def _(dve):
                own = Chain(dve, step)
                dve.memset(ones[:], 1.0)
                own.then(dve.memset(m[:], 0.0))
                lf = B["lf"][:].rearrange("h (c t) -> h c t", c=TT)
                li = B["li"][:].rearrange("h (c t) -> h c t", c=TT)
                for c in range(TT):
                    last = dve.tensor_tensor_scan(b[:, c], ones[:], lf[:, c], 0.0, ALU.mult, ALU.add)
                own.then(last)
                own.then(dve.tensor_tensor(row[:, 0], li, b[:], ALU.subtract))
                for c in range(TT):
                    own.then(dve.tensor_tensor_scan(M[:, c], row[:, 0, c], row[:, 0, c], m[:, c:c + 1], ALU.max, ALU.max))
                    own.then(dve.tensor_tensor(m[:, c + 1:c + 2], b[:, c, P - 1:P], M[:, c, P - 1:P], ALU.add))
                dve.sem_inc(maxed, 1)
                for c in range(TT):
                    dve.tensor_scalar(row[:, 1, c], M[:, c], m[:, c:c + 1], None, ALU.subtract)
                    dve.tensor_scalar(row[:, 3, c], row[:, 0, c], M[:, c, P - 1:P], None, ALU.subtract)
                dve.tensor_tensor(dr[:], M[:, :, P - 1], m[:, 0:TT], ALU.subtract)
                own.then(dve.tensor_tensor(row[:, 2], b[:], M[:], ALU.add))
                dve.sem_inc(rowed, 1)
                dve.wait_ge(turned, 1)
                dve.tensor_copy(col[:].rearrange("p k c h -> p (k c h)"), bank[4][:, 0:4 * TT * H_E]).then_inc(colled, 1)
                dve.wait_ge(colled, 1)
                dve.wait_ge(spread, 1)
                for h in range(H_E):
                    for c in range(TT):
                        last = dve.tensor_scalar(wT[:, h, c], bank[h][:, c * P:(c + 1) * P], col[:, 0, c, h:h + 1], 0.0,
                                                 ALU.subtract, ALU.max)
                last.then_inc(lagged, 1)
                dve.wait_ge(spread, 2)
                dve.tensor_copy(dec[:].rearrange("p h c -> p (h c)"), bank[5][:, 0:TT * H_E])

            @block.scalar
            def _(act):
                act.wait_ge(rowed, 1)
                act.activation(row[:, 1:3], row[:, 1:3], ACT.Exp, scale=-1.0)
                act.activation(dr[:], dr[:], ACT.Exp, scale=-1.0)
                act.activation(row[:, 3], row[:, 3], ACT.Exp).then_inc(expd, 1)
                for k in range(KT // 4):
                    w_out.copy_high(act, k)
                act.wait_ge(lagged, 1)
                act.activation(wT[:], wT[:], ACT.Exp, scale=-1.0).then_inc(weighed, 1)
                for k in range(KT // 4, KT // 2):
                    w_out.copy_high(act, k)

            @block.tensor
            def _(pe):
                pe.wait_ge(maxed, 1)
                for h in range(H_E):
                    last = pe.matmul(bank[h][:], K["sel"][:, h], M[:].rearrange("h c t -> h (c t)"), start=True, stop=True)
                last.then_inc(spread, 1)
                pe.wait_ge(expd, 1)
                for k in range(4):
                    for c in range(TT):
                        o = (k * TT + c) * H_E
                        last = pe.transpose(bank[4][:, o:o + H_E], row[:, k, c], K["ident"][0:H_E, 0:H_E])
                last.then_inc(turned, 1)
                for h in range(H_E):
                    last = pe.matmul(bank[5][:, h * TT:(h + 1) * TT], K["sel"][:, h], dr[:], start=True, stop=True)
                last.then_inc(spread, 1)

            @block.gpsimd
            def _(pool):
                for k in range(KT // 4):
                    w_out.take_rest(pool, k)
                pool.wait_ge(weighed, 1)
                w = wT[:].rearrange("p h c t -> p (h c) t")
                pool.affine_select(out=w, in_=w, compare_op=ALU.is_ge, fill=0.0, base=0,
                                   pattern=[[0, H_E * TT], [1, P]], channel_multiplier=-1)


def mlstm_cells(nc, K, ins, B, wT, col, dec, cat, w_out):
    W = D_E + 1
    N = TT * H_E
    with Stage(nc, "evc") as st:
        kw = st.sb("kw", [P, N, D_E])
        state = st.sb("state", [P, TT, H_E, W])
        num = st.sb("num", [P, N, W])
        inter = st.sb("inter", [P, N, W])
        den, den2 = st.sb("den", [P, N]), st.sb("den2", [P, N])
        ss, root, y, t1 = (st.sb(n, [P, N]) for n in ("ss", "root", "y", "t1"))
        gain = st.sb("gain", [P, MIX])
        assert nc.sbuf_base <= w_out.bottom
        bank = st.banks(8)
        gain_in, turned, keyed, scored, weighed, summed, intered = (
            st.sem(n) for n in ("gain_in", "turned", "keyed", "scored", "weighed", "summed", "intered"))
        stated, carried, scaled, numbered, step, rooted, squared, summed_squares, gained = (
            st.sem(n) for n in ("stated", "carried", "scaled", "numbered", "step", "rooted", "squared", "summed_squares", "gained"))
        qk, v1 = B["qk"], B["v1"]

        with nc.Block() as block:
            @block.sync
            def _(sp):
                sp.dma_start(gain[:], ins["ev_h_gain"].to_broadcast([P, MIX])).then_inc(gain_in, 16)

            @block.gpsimd
            def _(pool):
                pool.wait_ge(gain_in, 16)
                pool.tensor_tensor(B["og"][:], B["og"][:], gain[:].unsqueeze(1).to_broadcast([P, TT, MIX]), ALU.mult).then_inc(gained, 1)
                for k in range(KT // 4, KT):
                    w_out.take_rest(pool, k)

            @block.tensor
            def _(pe):
                for c in range(TT):
                    tok = slice(c * P, (c + 1) * P)
                    if c >= 2:
                        pe.wait_ge(keyed, H_E * (c - 1))
                    for h in range(H_E):
                        last = pe.transpose(bank[c % 2][:, h * P:(h + 1) * P], qk[:, H_E + h, tok], K["ident"][:])
                    last.then_inc(turned, 1)
                    if c >= 2:
                        pe.wait_ge(weighed, c - 1)
                    for h in range(H_E):
                        last = pe.matmul(bank[2 + c % 2][:, h * P:(h + 1) * P], qk[:, H_E + h, tok], qk[:, h, tok], start=True, stop=True)
                    last.then_inc(scored, 1)
                pe.wait_ge(keyed, N)
                for c in range(TT):
                    tok = slice(c * P, (c + 1) * P)
                    for h in range(H_E):
                        n = c * H_E + h
                        if c < TT - 1:
                            if n >= 2:
                                pe.wait_ge(carried, n - 1)
                            pe.matmul(bank[6 + n % 2][:, 0:W], kw[:, n], v1[:, c, h], start=True, stop=True).then_inc(stated, 1)
                        pe.wait_ge(weighed, c + 1)
                        if n >= 2:
                            pe.wait_ge(numbered, n - 1)
                        pe.matmul(bank[4 if n % 2 else 0][:, 0:W], wT[:, h, c], v1[:, c, h], start=True, stop=True).then_inc(summed, 1)
                        if c:
                            pe.wait_ge(carried, n - H_E + 1)
                            if n >= H_E + 2:
                                pe.wait_ge(intered, n - H_E - 1)
                            pe.matmul(bank[5 if n % 2 else 1][:, 0:W], qk[:, h, tok], state[:, c, h], start=True, stop=True).then_inc(scaled, 1)

            @block.scalar
            def _(act):
                for n in range(N):
                    c, h = n // H_E, n % H_E
                    act.wait_ge(turned, c + 1)
                    act.activation(kw[:, n], bank[c % 2][:, h * P:(h + 1) * P], ACT.Copy, scale=col[:, 3, c, h:h + 1]).then_inc(keyed, 1)
                for k in range(KT // 2, KT):
                    w_out.copy_high(act, k)

                def square(n):
                    act.wait_ge(numbered, n + 1)
                    act.activation(kw[:, n], num[:, n, 0:D_E], ACT.Square, accum_out=ss[:, n:n + 1]).then_inc(summed_squares, 1)

                for n in range(H_E, N):
                    c, h = n // H_E, n % H_E
                    act.wait_ge(scaled, n - H_E + 1)
                    act.activation(inter[:, n], bank[5 if n % 2 else 1][:, 0:W], ACT.Copy, scale=col[:, 1, c, h:h + 1]).then_inc(intered, 1)
                    if n >= 2 * H_E:
                        square(n - 2 * H_E)
                for n in range(N - 2 * H_E, N):
                    if n == N - H_E:
                        act.wait_ge(summed, N)
                    square(n)
                act.wait_ge(squared, 1)
                act.activation(root[:], ss[:], ACT.Sqrt, scale=1.0 / D_E, bias=K["eps"][:, 0:1]).then_inc(rooted, 1)

            @block.vector
            def _(dve):
                own = Chain(dve, step)
                for c in range(TT):
                    dve.wait_ge(scored, c + 1)
                    dve.tensor_tensor(wT[:, :, c], bank[2 + c % 2][:].rearrange("p (h t) -> p h t", h=H_E), wT[:, :, c], ALU.mult).then_inc(weighed, 1)

                def number(n):
                    dve.wait_ge(summed, n + 1)
                    if n >= H_E:
                        dve.wait_ge(intered, n - H_E + 1)
                        dve.tensor_tensor(num[:, n], bank[4 if n % 2 else 0][:, 0:W], inter[:, n], ALU.add).then_inc(numbered, 1)
                    else:
                        dve.tensor_copy(num[:, n], bank[4 if n % 2 else 0][:, 0:W]).then_inc(numbered, 1)

                for n in range(N):
                    c, h = n // H_E, n % H_E
                    if c < TT - 1:
                        dve.wait_ge(stated, n + 1)
                        if c == 0:
                            dve.tensor_copy(state[:, 1, h], bank[6 + n % 2][:, 0:W]).then_inc(carried, 1)
                        else:
                            dve.wait_ge(carried, n - H_E + 1)
                            dve.scalar_tensor_tensor(out=state[:, c + 1, h], in0=state[:, c, h], scalar=dec[:, h, c:c + 1],
                                                     in1=bank[6 + n % 2][:, 0:W], op0=ALU.mult, op1=ALU.add).then_inc(carried, 1)
                    number(n)
                dve.wait_ge(numbered, N)
                own.then(dve.tensor_copy(den[:], num[:, :, D_E]))
                own.then(dve.tensor_scalar(den2[:], den[:], -1.0, None, ALU.mult))
                own.then(dve.tensor_tensor(den[:], den[:], den2[:], ALU.max))
                own.then(dve.tensor_tensor(den[:], den[:], col[:, 2].rearrange("p c h -> p (c h)"), ALU.max))
                own.then(dve.reciprocal(den[:], den[:]))
                dve.wait_ge(summed_squares, N)
                own.then(dve.tensor_tensor(ss[:], ss[:], den[:], ALU.mult))
                own.then(dve.tensor_tensor(ss[:], ss[:], den[:], ALU.mult))
                dve.sem_inc(squared, 1)
                rsqrt_newton(dve, own, rooted, 1, ss, root, y, t1, D_E)
                own.then(dve.tensor_tensor(y[:], y[:], den[:], ALU.mult))
                dve.wait_ge(gained, 1)
                for c in range(TT):
                    hh = inter[:, c * H_E:(c + 1) * H_E, 0:D_E]
                    own.then(dve.tensor_tensor(hh, num[:, c * H_E:(c + 1) * H_E, 0:D_E],
                                               y[:, c * H_E:(c + 1) * H_E].unsqueeze(2).to_broadcast([P, H_E, D_E]), ALU.mult))
                    dve.tensor_tensor(cat[:, c, MIX:2 * MIX].rearrange("p (h d) -> p h d", h=H_E), hh,
                                      B["og"][:, c].rearrange("p (h d) -> p h d", h=H_E), ALU.mult)



def mla_mixer(nc, K, ins):
    LAT, KB = Q_LORA + KV_LORA, 1024
    QK_, VK = Q_LORA // P, KV_LORA // P
    with Stage(nc, "od") as st:
        end = nc.sbuf_usable_end // 32 * 32

        def below(n, shape, kb, dt=F32R):
            return nc.alloc_sbuf_tensor_at(f"od_{n}", shape, dt, offset=end - kb * KB)

        c = below("ch", [P, LAT // P, T], 12), below("cl", [P, LAT // P, T], 24)
        cos, sin = below("cos", [P, T], 26, F32), below("sin", [P, T], 28, F32)
        W, rest = ({n: below(f"w{n}{'_rest' if dt == F32R else ''}", [P, tiles, width], kb, dt) for n, tiles, width, kb in
                    (("q", QK_, H_A * NOPE, 44), ("r", QK_, H_A * ROPE, 52), ("k", VK, H_A * NOPE, 60), ("v", VK, H_A * V_D, 68))}
                   for dt in (F32, F32R))
        held = end - 68 * KB
        o = below("oh", [P, H_A, T], 16), below("ol", [P, H_A, T], 32)
        w_out = OutputWeights(nc, st, "od", ins["od_w_out_l"], end - 32 * KB)
        wr_in, heads_in, tab_in = (st.sem(n) for n in ("wr_in", "heads_in", "tab_in"))
        lat_in = [st.sem(f"lat_in{n}") for n in range(2)]

        kr = st.sb("kr", [P, T])
        with Stage(nc, "odx") as sx:
            xh, xl = sx.sb("xh", [P, KT, T], F32R), sx.sb("xl", [P, KT, T], F32R)
            w, wl = sx.sb_split("w", [P, KT, LAT])
            wr, rl = sx.sb_split("wr", [P, KT, P])

            def loads(sp):
                sp.dma_start(wr[:], ins["od_w_kr_l"]).then_inc(wr_in, 16)
                for n in range(2):
                    ks = slice(n * KT // 2, (n + 1) * KT // 2)
                    sp.dma_start(w[:, ks], ins["od_w_lat_l"][:, ks]).then_inc(lat_in[n], 16)
                sp.dma_start(cos[:], ins["cos_t"]).then_inc(tab_in, 16)
                sp.dma_start(sin[:], ins["sin_t"]).then_inc(tab_in, 16)
                for n, src in (("q", "od_w_uq_l"), ("r", "od_w_qr_l"), ("k", "od_w_uk_l"), ("v", "od_w_uv_l")):
                    sp.dma_start(W[n][:], ins[src]).then_inc(heads_in, 16)

            rh, key_high = sx.sb("rh", [P, KT, P], F32R), sx.sem("key_high")

            def high_of_key(act):
                act.wait_ge(wr_in, 16)
                act.activation(rh[:], wr[:], ACT.Copy).then_inc(key_high, 1)

            def rest_of_key(dve):
                dve.wait_ge(key_high, 1)
                dve.tensor_tensor(rl[:], wr[:], as_f32(rh[:]), ALU.subtract)

            norm_transpose(nc, K, "odn", ins["norm_mix_c"][1], (xh, xl), loads, high_of_key, rest_of_key)
            mla_latents(nc, K, ins, (xh, xl), (w, wl), (rh, rl), c, cos, sin, kr, lat_in, tab_in, limit=held)
        with Stage(nc, "odq") as sq:
            qT = sq.sb("qT", [P, H_A, T])
            qr = sq.sb("qr", [P, H_A // 2, T])
            kT = sq.sb("kT", [P, H_A, T])
            v = sq.sb("v", [P, TT, H_A * V_D])
            mla_heads(nc, K, W, rest, heads_in, c, cos, sin, qT, qr, kT, v, limit=held)
            mla_attend(nc, K, qT, qr, kT, kr, v, o, w_out)
        project_out(nc, K, "odo", w_out.split, split=o)


def rotate(dve, own, out, rows, cos, sin, tmp):
    H = ROPE // 2
    for a in range(0, P, H):
        b = a + H if a % ROPE == 0 else a - H
        dve.tensor_tensor(tmp[b:b + H], rows[a:a + H], sin[a:a + H], ALU.mult)
    own.then(dve.tensor_tensor(out, rows, cos[:], ALU.mult))
    own.then(dve.tensor_tensor(out, out, tmp, ALU.add))


def mla_latents(nc, K, ins, x, weights, key_weights, c, cos, sin, kr, lat_in, tab_in, limit):
    w, wl = weights
    rh, rl = key_weights
    LAT = Q_LORA + KV_LORA
    LK, HALF = LAT // P, TT // 2
    KR = 7
    with Stage(nc, "odl") as st:
        wh = st.sb("wh", [P, KT, LAT], F32R)
        lat = st.sb("lat", [P, TT, LAT])
        sqr = st.sb("sqr", [P, 2, Q_LORA])
        gcol = st.sb("gcol", [P, LK])
        tmp = st.sb("tmp", [P, T])
        ss, root, y, t1 = (st.sb(n, [P, 2 * TT]) for n in ("ss", "root", "y", "t1"))
        assert nc.sbuf_base <= limit
        bank = st.banks(8)
        gain_in, made, w_high, w_rest, keyed = (st.sem(n) for n in ("gain_in", "made", "w_high", "w_rest", "keyed"))
        step, squared, rooted, turned, scaled, scaled_act, c_high = (
            st.sem(n) for n in ("step", "squared", "rooted", "turned", "scaled", "scaled_act", "c_high"))
        PARTS = ((0, Q_LORA), (Q_LORA, LAT))
        WIDTHS = [(slice(p * TT, (p + 1) * TT), b - a) for p, (a, b) in enumerate(PARTS)]
        with nc.Block() as block:
            @block.sync
            def _(sp):
                sp.dma_start(gcol[:], ins["od_gain_l"]).then_inc(gain_in, 16)

            @block.tensor
            def _(pe):
                for k in range(KT):
                    last = split_product(pe, bank[KR][:], (rh[:, k], rl[:, k]), (x[0][:, k], x[1][:, k]), k == 0, k == KT - 1)
                last.then_inc(made, 1)
                for k in range(KT):
                    pe.wait_ge(w_rest, k + 1)
                    for t in range(TT):
                        tok = slice(t * P, (t + 1) * P)
                        for part, (a, b) in enumerate(PARTS):
                            if k == 0 and 2 * t + part == KR:
                                pe.wait_ge(keyed, 1)
                            last = split_product(pe, bank[2 * t + part][:, 0:b - a], (x[0][:, k, tok], x[1][:, k, tok]),
                                                 (wh[:, k, a:b], wl[:, k, a:b]), k == 0, k == KT - 1)
                            if k == KT - 1:
                                last.then_inc(made, 1)
                pe.wait_ge(scaled, 1)
                pe.wait_ge(scaled_act, 1)
                for k in range(LK):
                    for t in range(TT):
                        last = pe.transpose(bank[k][:, t * P:(t + 1) * P], lat[:, t, k * P:(k + 1) * P], K["ident"][:])
                    last.then_inc(turned, 1)

            def scale(eng, tiles, op):
                for t in tiles:
                    for part, (a, b) in enumerate(PARTS):
                        last = op(lat[:, t, a:b], bank[2 * t + part][:, 0:b - a], y[:, part * TT + t:part * TT + t + 1])
                return last

            @block.scalar
            def _(act):
                for k in range(KT):
                    act.wait_ge(lat_in[k // (KT // 2)], 16)
                    act.activation(wh[:, k], w[:, k], ACT.Copy).then_inc(w_high, 1)
                for t in range(TT):
                    for part, (a, b) in enumerate(PARTS):
                        n = 2 * t + part
                        act.wait_ge(made, n + 2)
                        if n >= 2:
                            act.wait_ge(squared, n - 1)
                        act.activation(sqr[:, part, 0:b - a], bank[n][:, 0:b - a], ACT.Square,
                                       accum_out=ss[:, part * TT + t:part * TT + t + 1]).then_inc(squared, 1)
                act.wait_ge(squared, 2 * TT)
                for cols, width in WIDTHS:
                    last = act.activation(root[:, cols], ss[:, cols], ACT.Sqrt, scale=1.0 / width, bias=K["eps"][:, 0:1])
                last.then_inc(rooted, 1)
                act.wait_ge(step, 2 + 6)
                scale(act, range(HALF, TT), lambda o, i, s: act.activation(o, i, ACT.Copy, scale=s)).then_inc(scaled_act, 1)
                act.wait_ge(gain_in, 16)
                for k in range(LK):
                    act.wait_ge(turned, k + 1)
                    act.activation(c[0][:, k], bank[k][:], ACT.Copy, scale=gcol[:, k:k + 1]).then_inc(c_high, 1)

            @block.vector
            def _(dve):
                own = Chain(dve, step)
                for k in range(KT):
                    dve.wait_ge(w_high, k + 1)
                    dve.tensor_tensor(wl[:, k], w[:, k], as_f32(wh[:, k]), ALU.subtract).then_inc(w_rest, 1)
                    if k == 3:
                        dve.wait_ge(tab_in, 32)
                        dve.wait_ge(made, 1)
                        rotate(dve, own, kr[:], bank[KR][:], cos, sin, tmp[:])
                        dve.sem_inc(keyed, 1)
                rsqrt_newton(dve, own, rooted, 1, ss, root, y, t1, WIDTHS)
                scale(dve, range(HALF), lambda o, i, s: dve.tensor_scalar(o, i, s, None, ALU.mult)).then_inc(scaled, 1)
                for k in range(LK):
                    dve.wait_ge(c_high, k + 1)
                    dve.scalar_tensor_tensor(out=c[1][:, k], in0=bank[k][:], scalar=gcol[:, k:k + 1], in1=as_f32(c[0][:, k]),
                                             op0=ALU.mult, op1=ALU.subtract)


def mla_heads(nc, K, W, rest, heads_in, c, cos, sin, qT, qr, kT, v, limit):
    QK_, VK = Q_LORA // P, KV_LORA // P
    R = H_A * ROPE // P
    with Stage(nc, "odh") as st:
        H = {n: st.sb(f"high_{n}", [P, QK_ if n in "qr" else VK, H_A * ROPE if n == "r" else H_A * P], F32R) for n in "qrkv"}
        tmp = st.sb("tmp", [P, 2, T])
        assert nc.sbuf_base <= limit
        bank = st.banks(8)
        w_high, w_rest, made, by_act, by_dve, step = (st.sem(n) for n in ("w_high", "w_rest", "made", "by_act", "by_dve", "step"))
        tiles = [(n, k) for n in "qrkv" for k in range(H[n].shape[1])]
        order = [("q", h) for h in range(H_A)] + [("r", r) for r in range(R)] + [("k", h) for h in range(H_A)] + [("v", n) for n in range(BLOCKS)]
        readers = []
        for kind, i in order:
            readers.append((by_dve, i + 1) if kind == "r" else (by_act, i + 1 + H_A * "qkv".index(kind)))
        with nc.Block() as block:
            @block.tensor
            def _(pe):
                def product(n, k):
                    kind, i = order[n]
                    ks = H[kind].shape[1]
                    kc = k if kind in "qr" else QK_ + k
                    if kind == "v":
                        tok, half = slice(i // 2 * P, (i // 2 + 1) * P), slice(i % 2 * 512, (i % 2 + 1) * 512)
                        a, b = (c[0][:, kc, tok], c[1][:, kc, tok]), (H["v"][:, k, half], rest["v"][:, k, half])
                    else:
                        cols = slice(i * P, (i + 1) * P)
                        a, b = (H[kind][:, k, cols], rest[kind][:, k, cols]), (c[0][:, kc], c[1][:, kc])
                    last = split_product(pe, bank[n % 8][:], a, b, k == 0, k == ks - 1)
                    if k == ks - 1:
                        last.then_inc(made, 1)

                for k in range(QK_):
                    pe.wait_ge(w_rest, k + 1)
                    for h in range(H_A):
                        product(h, k)
                for n in range(H_A, len(order)):
                    kind, i = order[n]
                    pe.wait_ge(*readers[n - 8])
                    if i == 0:
                        pe.wait_ge(w_rest, tiles.index((kind, H[kind].shape[1] - 1)) + 1)
                    for k in range(H[kind].shape[1]):
                        product(n, k)

            @block.scalar
            def _(act):
                act.wait_ge(heads_in, 64)
                for n, k in tiles:
                    act.activation(H[n][:, k], W[n][:, k], ACT.Copy).then_inc(w_high, 1)
                for n, (kind, i) in enumerate(order):
                    if kind == "r":
                        continue
                    act.wait_ge(made, n + 1)
                    dst = {"q": qT[:, i], "k": kT[:, i], "v": v[:, i // 2, i % 2 * 512:(i % 2 + 1) * 512]}[kind]
                    act.activation(dst, bank[n % 8][:], ACT.Copy).then_inc(by_act, 1)

            @block.vector
            def _(dve):
                own = Chain(dve, step)
                for m, (n, k) in enumerate(tiles):
                    dve.wait_ge(w_high, m + 1)
                    dve.tensor_tensor(rest[n][:, k], W[n][:, k], as_f32(H[n][:, k]), ALU.subtract).then_inc(w_rest, 1)
                for r in range(R):
                    n = H_A + r
                    dve.wait_ge(made, n + 1)
                    rotate(dve, own, qr[:, r], bank[n % 8][:], cos, sin, tmp[:, r % 2])
                    dve.sem_inc(by_dve, 1)


def mla_attend(nc, K, qT, qr, kT, kr, v, o, w_out):
    N = H_A * TT
    SCORES, TURNED = 4, 2
    AHEAD = 5
    TURN = AHEAD - 1
    with Stage(nc, "oda") as st:
        prob = st.sb("prob", [P, AHEAD, T])
        pT = st.sb("pT", [P, 2, T])
        mask = st.sb("mask", [P, P])
        top, sums, inv = st.sb("top", [P, N]), st.sb("sums", [P, N]), st.sb("inv", [P, N])
        bank = st.banks(8)
        masked, scored, hidden, reduced, maxed, expd, inverted, normed = (
            st.sem(n) for n in ("masked", "scored", "hidden", "reduced", "maxed", "expd", "inverted", "normed"))
        turned, copied, summed, stored, zeroed = (st.sem(n) for n in ("turned", "copied", "summed", "stored", "zeroed"))
        stored_high = st.sem("stored_high")
        items = [(h, c) for h in range(H_A) for c in range(TT)]
        oh, ol = o
        assert nc.sbuf_base <= w_out.bottom

        with nc.Block() as block:
            @block.sync
            def _(sp):
                w_out.load(sp)

            @block.gpsimd
            def _(pool):
                pool.memset(mask[:], 0.0).then_inc(zeroed, 1)
                pool.wait_ge(zeroed, 1)
                pool.affine_select(out=mask[:], in_=mask[:], compare_op=ALU.is_ge, fill=NEG, base=0,
                                   pattern=[[-1, P]], channel_multiplier=1).then_inc(masked, 1)
                for k in range(KT):
                    w_out.take_rest(pool, k)

            @block.tensor
            def _(pe):
                def score(n):
                    h, c = items[n]
                    if n >= SCORES:
                        pe.wait_ge(expd, n - SCORES + 1)
                    keys, half = (c + 1) * P, h % 2 * ROPE
                    pe.matmul(bank[n % SCORES][:, 0:keys], qT[:, h, c * P:keys], kT[:, h, 0:keys], start=True, stop=False)
                    pe.matmul(bank[n % SCORES][:, 0:keys], qr[half:half + ROPE, h // 2, c * P:keys], kr[half:half + ROPE, 0:keys],
                              start=False, stop=True).then_inc(scored, 1)

                def turn(n):
                    h, c = items[n]
                    pe.wait_ge(normed, n + 1)
                    if n >= TURNED:
                        pe.wait_ge(copied, n - TURNED + 1)
                    for k in range(c + 1):
                        last = pe.transpose(bank[SCORES + n % TURNED][:, k * P:(k + 1) * P], prob[:, n % AHEAD, k * P:(k + 1) * P], K["ident"][:])
                    last.then_inc(turned, 1)

                def weigh(n):
                    h, c = items[n]
                    pe.wait_ge(copied, n + 1)
                    if c == 0 and h >= 2:
                        pe.wait_ge(stored, h - 1)
                    for k in range(c + 1):
                        last = pe.matmul(bank[6 + h % 2][:, c * P:(c + 1) * P], v[:, k, h * V_D:(h + 1) * V_D],
                                         pT[:, n % 2, k * P:(k + 1) * P], start=(k == 0), stop=(k == c))
                    last.then_inc(summed, 1)

                for n in range(N + AHEAD):
                    if n < N:
                        score(n)
                    if 0 <= n - TURN < N:
                        turn(n - TURN)
                    if 0 <= n - AHEAD < N:
                        weigh(n - AHEAD)

            @block.vector
            def _(dve):
                dve.wait_ge(masked, 1)

                def top_of(n):
                    h, c = items[n]
                    dve.wait_ge(scored, n + 1)
                    diag = bank[n % SCORES][:, c * P:(c + 1) * P]
                    dve.tensor_tensor(diag, diag, mask[:], ALU.add).then_inc(hidden, 1)
                    dve.wait_ge(hidden, n + 1)
                    dve.tensor_reduce(top[:, n:n + 1], bank[n % SCORES][:, 0:(c + 1) * P], AX.X, ALU.max).then_inc(reduced, 1)
                    dve.wait_ge(reduced, n + 1)
                    dve.tensor_scalar(top[:, n:n + 1], top[:, n:n + 1], -A_SCALE, None, ALU.mult).then_inc(maxed, 1)

                def norm(n):
                    h, c = items[n]
                    dve.wait_ge(expd, n + 1)
                    dve.reciprocal(inv[:, n:n + 1], sums[:, n:n + 1]).then_inc(inverted, 1)
                    dve.wait_ge(inverted, n + 1)
                    pr = prob[:, n % AHEAD, 0:(c + 1) * P]
                    dve.tensor_scalar(pr, pr, inv[:, n:n + 1], None, ALU.mult).then_inc(normed, 1)

                def store_rest(h):
                    dve.wait_ge(stored_high, h + 1)
                    dve.tensor_tensor(ol[:, h], bank[6 + h % 2][:], as_f32(oh[:, h]), ALU.subtract).then_inc(stored, 1)

                for n in range(N + AHEAD + 1):
                    if n < N:
                        top_of(n)
                    if 1 <= n <= N:
                        norm(n - 1)
                    if n > AHEAD and (n - AHEAD) % TT == 0:
                        store_rest((n - AHEAD) // TT - 1)

            @block.scalar
            def _(act):
                def exp_of(n):
                    h, c = items[n]
                    act.wait_ge(maxed, n + 1)
                    if n >= AHEAD:
                        act.wait_ge(turned, n - AHEAD + 1)
                    act.activation(prob[:, n % AHEAD, 0:(c + 1) * P], bank[n % SCORES][:, 0:(c + 1) * P], ACT.Exp, scale=A_SCALE,
                                   bias=top[:, n:n + 1], accum_out=sums[:, n:n + 1]).then_inc(expd, 1)

                def copy(n):
                    h, c = items[n]
                    act.wait_ge(turned, n + 1)
                    if n >= 2:
                        act.wait_ge(summed, n - 1)
                    act.activation(pT[:, n % 2, 0:(c + 1) * P], bank[SCORES + n % TURNED][:, 0:(c + 1) * P], ACT.Copy).then_inc(copied, 1)

                def store(h):
                    act.wait_ge(summed, TT * (h + 1))
                    act.activation(oh[:, h], bank[6 + h % 2][:], ACT.Copy).then_inc(stored_high, 1)

                for n in range(N + AHEAD + 1):
                    if n < N:
                        exp_of(n)
                    if 0 <= n - TURN < N:
                        copy(n - TURN)
                    if n > AHEAD and (n - AHEAD) % TT == 0:
                        store((n - AHEAD) // TT - 1)
                    if n > N // 2 and n % 2 and (n - N // 2) // 2 < KT:
                        w_out.copy_high(act, (n - N // 2) // 2)


def lay_out(a):
    a = {k: np.asarray(v) for k, v in a.items()}

    def rows(w):
        *lead, kp, n = w.shape
        return np.ascontiguousarray(np.moveaxis(w.reshape(*lead, kp // P, P, n), -3, -2))

    def cols(g):
        *lead, kp = g.shape
        return np.ascontiguousarray(np.swapaxes(g.reshape(*lead, kp // P, P), -1, -2))

    L = 2
    out = {"x": a["x"]}
    out["norm_mix_c"], out["norm_ffn_c"] = cols(a["norm_mix"]), cols(a["norm_ffn"])
    out["norm_final_r"] = a["norm_final"][None, :]
    w = rows(a["peer_w_q"])
    out["peer_wq_l"] = np.ascontiguousarray(np.moveaxis(w.reshape(L, P, KT, H_P, QD), 3, 1))
    out["peer_keys_l"] = np.ascontiguousarray(np.transpose(a["peer_keys"], (0, 1, 4, 2, 3)))
    u = a["peer_u"].reshape(L, KEYS, KEYS, KT, P)
    out["peer_u_l"] = np.ascontiguousarray(np.transpose(u, (0, 2, 4, 3, 1))).reshape(L, KEYS, P, D)
    out["peer_v_l"] = np.ascontiguousarray(np.swapaxes(a["peer_v"].reshape(L, KEYS, KEYS, D), 1, 2))
    def pairs(stairs):
        return [(r, c) for a, n, b, w in stairs for r in range(a, a + n) for c in range(b, b + w)]

    order = pairs(STAIRS)
    out["place"] = np.array([[order.index(p) for p in pairs(NEAR + FAR)]], np.float32)
    w = rows(a["ev_w_in"][0])
    order = [2 * MIX, 3 * MIX, 0, MIX, 4 * MIX, 5 * MIX]
    out["ev_w_in_l"] = np.ascontiguousarray(np.stack([w[:, :, o:o + MIX] for o in order]))
    gates = np.zeros((P, KT, P), np.float32)
    gates[:, :, 0:H_E] = w[:, :, 6 * MIX:6 * MIX + H_E]
    gates[:, :, 32:32 + H_E] = w[:, :, 6 * MIX + H_E:6 * MIX + 2 * H_E]
    out["ev_w_gates_l"] = gates
    out["ev_bias_l"] = np.ascontiguousarray(np.stack([a["ev_i_bias"][0], a["ev_f_bias"][0]])[:, :, None])
    out["ev_conv_w_l"] = np.ascontiguousarray(np.transpose(a["ev_conv_w"][0].reshape(CONV, 2 * H_E, P), (2, 1, 0)))
    out["ev_conv_b_l"] = cols(a["ev_conv_b"][0])
    out["ev_gm_ws_l"] = np.ascontiguousarray(np.transpose(a["ev_gm_ws"][0], (2, 0, 1)))
    out["ev_gm_b_l"] = np.ascontiguousarray(a["ev_gm_b"][0].T)
    out["ev_gm_v_gain"], out["ev_h_gain"] = a["ev_gm_v_gain"], a["ev_h_gain"]
    out["ev_w_out_l"] = rows(a["ev_w_out"][0])
    w = rows(a["od_w_in"][0])
    LAT = Q_LORA + KV_LORA
    out["od_w_lat_l"] = np.ascontiguousarray(w[:, :, 0:LAT])
    kr = w[:, :, LAT:LAT + ROPE]
    out["od_w_kr_l"] = np.ascontiguousarray(np.concatenate([kr, kr], -1))
    out["od_gain_l"] = np.ascontiguousarray(np.concatenate([cols(a["od_q_gain"][0]), cols(a["od_kv_gain"][0])], -1))
    w = rows(a["od_w_uq"][0]).reshape(P, Q_LORA // P, H_A, NOPE + ROPE)
    out["od_w_uq_l"] = np.ascontiguousarray(w[..., :NOPE]).reshape(P, Q_LORA // P, H_A * NOPE)
    out["od_w_qr_l"] = np.ascontiguousarray(w[..., NOPE:]).reshape(P, Q_LORA // P, H_A * ROPE)
    w = rows(a["od_w_ukv"][0]).reshape(P, KV_LORA // P, H_A, NOPE + V_D)
    out["od_w_uk_l"] = np.ascontiguousarray(w[..., :NOPE]).reshape(P, KV_LORA // P, H_A * NOPE)
    out["od_w_uv_l"] = np.ascontiguousarray(w[..., NOPE:]).reshape(P, KV_LORA // P, H_A * V_D)
    out["od_w_out_l"] = rows(a["od_w_out"][0])
    half = ROPE // 2
    inv_freq = np.float32(10000.0) ** (-np.arange(half, dtype=np.float32) / np.float32(half))
    ang = inv_freq[:, None] * np.arange(T, dtype=np.float32)[None, :]
    cos, sin = np.cos(ang), np.sin(ang)
    out["cos_t"] = np.ascontiguousarray(np.concatenate([cos] * 4, 0))
    out["sin_t"] = np.ascontiguousarray(np.concatenate([sin, -sin] * 2, 0))
    return out


def program(nc, ins, out, stages="all"):
    SEMAPHORES.clear()
    with ExitStack() as ctx:
        def sb(name, shape, dt=F32):
            return ctx.enter_context(nc.sbuf_tensor(name, shape, dt))

        K = {"X": sb("X", [P, TT, D]), "ident": sb("ident", [P, P]), "iota": sb("iota", [P, KEYS]),
             "iota_i": sb("iota_i", [P, KEYS], I32), "sel": sb("sel", [H_E, H_E, P]),
             "eps": sb("eps", [P, 1]), "one": sb("one", [P, 1])}
        g_dram = nc.dram_tensor("gates", (KEYS, P, T), F32).ap()
        constants(nc, K, ins)
        if stages in ("all", "even"):
            even_mixer(nc, K, ins)
            clear_semaphores(nc)
        if stages in ("all", "peer0"):
            peer(nc, K, 0, ins, g_dram)
            clear_semaphores(nc)
        if stages in ("all", "mla"):
            mla_mixer(nc, K, ins)
            clear_semaphores(nc)
        if stages in ("all", "peer1"):
            peer(nc, K, 1, ins, g_dram, (ins["norm_final_r"], out))


def kernel(**inputs):
    import concourse.bacc as bacc
    from concourse.bass_utils import run_bass_kernel_spmd

    arrays = {f"in_{n}": v for n, v in lay_out(inputs).items()}
    nc = bacc.Bacc("TRN2", target_bir_lowering=False, num_devices=1)
    ins = {n[3:]: nc.dram_tensor(n, v.shape, F32, kind="ExternalInput").ap() for n, v in arrays.items()}
    out = nc.dram_tensor("out", (1, T, D), F32, kind="ExternalOutput").ap()
    program(nc, ins, out)
    return run_bass_kernel_spmd(nc, [arrays], core_ids=[0]).results[0]["out"]
```
